# Optimizing a Trainium2 kernel written in Bass

```python
import jax, jax.numpy as jnp
from jax import lax
import numpy as np

D_MODEL = 1024
BATCH = 1
SEQ = 256
DEPTH = 1

N_META = 16
CONV_CH = 512
CONV_KERNEL = 31
RWKV_WIDTH = 512
RWKV_HEAD = 64
RWKV_HEADS = RWKV_WIDTH // RWKV_HEAD
RANK_W = 64
RANK_A = 64
RANK_G = 128
N_BRANCH = 2
SHIFT_TOTAL = 3 * RWKV_WIDTH + RANK_W + RANK_A + RANK_G
IN_SPLITS = [CONV_CH, 2 * CONV_CH, 2 * CONV_CH + SHIFT_TOTAL]
IN_TOTAL = 2 * CONV_CH + SHIFT_TOTAL + N_BRANCH * D_MODEL
RWKV_SPLITS = [RWKV_WIDTH, 2 * RWKV_WIDTH, 3 * RWKV_WIDTH, 3 * RWKV_WIDTH + RANK_W, 3 * RWKV_WIDTH + RANK_W + RANK_A]
PEER_HEADS = 8
PEER_NKEYS = 128
PEER_EXPERTS = PEER_NKEYS * PEER_NKEYS
PEER_DHALF = 128
PEER_TOPK = 16
TOK_BLOCK = 256
RMS_EPS = 1e-6
LN_EPS = 1e-5
GN_EPS = 64e-5


def rmsnorm(x, g):
    xf = x.astype(jnp.float32)
    y = xf * lax.rsqrt(jnp.mean(xf * xf, axis=-1, keepdims=True) + RMS_EPS)
    return (y * g.astype(jnp.float32)).astype(x.dtype)

def token_shift(z):
    return jnp.pad(z[:, :-1], ((0, 0), (1, 0), (0, 0)))

def conformer_conv(val, gate, conv_w, conv_b, ln_g, ln_b, w_out):
    u = val * jax.nn.sigmoid(gate)
    y = lax.conv_general_dilated(
        u, conv_w[:, None, :].astype(u.dtype), window_strides=(1,),
        padding=[(CONV_KERNEL - 1, 0)], dimension_numbers=('NWC', 'WIO', 'NWC'),
        feature_group_count=CONV_CH) + conv_b
    yf = y.astype(jnp.float32)
    mean = jnp.mean(yf, axis=-1, keepdims=True)
    var = jnp.mean(jnp.square(yf - mean), axis=-1, keepdims=True)
    yn = (yf - mean) * lax.rsqrt(var + LN_EPS) * ln_g + ln_b
    return jax.nn.silu(yn).astype(val.dtype) @ w_out

def wkv7_scan(r, decay, k, v, kk, a):
    def step(S, inp):
        r_t, w_t, k_t, v_t, kk_t, a_t = inp
        sa = jnp.einsum('bhvk,bhk->bhv', S, kk_t)
        S = (S * w_t[:, :, None, :]
             - sa[..., None] * (kk_t * a_t)[:, :, None, :]
             + v_t[..., None] * k_t[:, :, None, :])
        return S, jnp.einsum('bhvk,bhk->bhv', S, r_t)
    B, T, H, N = r.shape
    S0 = jnp.zeros((B, H, N, N), jnp.float32)
    xs = tuple(jnp.moveaxis(z, 1, 0) for z in (r, decay, k, v, kk, a))
    _, o = lax.scan(step, S0, xs)
    return jnp.moveaxis(o, 0, 1)

def rwkv7_mix(z, mu, w0, w_up, a0, a_up, g_up, k_k, k_a, r_k, gn_g, gn_b, w_out):
    B, T, _ = z.shape
    zf = z.astype(jnp.float32)
    zf = zf + (token_shift(zf) - zf) * mu
    r, k, v, lw, la, lg = jnp.split(zf, RWKV_SPLITS, axis=-1)
    w = -jax.nn.softplus(-(w0 + jnp.tanh(lw) @ w_up)) - 0.5
    decay = jnp.exp(-jnp.exp(w))
    a = jax.nn.sigmoid(a0 + la @ a_up)
    g = jax.nn.sigmoid(lg) @ g_up
    hd = lambda t: t.reshape(B, T, RWKV_HEADS, RWKV_HEAD)
    kk = hd(k * k_k)
    kk = kk * lax.rsqrt(jnp.maximum(jnp.sum(kk * kk, axis=-1, keepdims=True), 1e-24))
    k = k * (1.0 + (a - 1.0) * k_a)
    r_h, k_h, v_h, a_h = hd(r), hd(k), hd(v), hd(a)
    o = wkv7_scan(r_h, hd(decay), k_h, v_h, kk, a_h)
    mean = jnp.mean(o, axis=-1, keepdims=True)
    var = jnp.mean(jnp.square(o - mean), axis=-1, keepdims=True)
    o = ((o - mean) * lax.rsqrt(var + GN_EPS)).reshape(B, T, RWKV_WIDTH) * gn_g + gn_b
    bonus = jnp.sum(r_h * k_h * r_k, axis=-1, keepdims=True) * v_h
    o = (o + bonus.reshape(B, T, RWKV_WIDTH)) * g
    return o.astype(z.dtype) @ w_out

def peer_ffn(x, w_q, sub_keys, expert_u, expert_v):
    B, T, D = x.shape
    n_tok = B * T
    n_blocks = -(-n_tok // TOK_BLOCK)
    pad = n_blocks * TOK_BLOCK - n_tok
    xt = jnp.pad(x.reshape(n_tok, D), ((0, pad), (0, 0))).reshape(n_blocks, TOK_BLOCK, D)
    K = PEER_TOPK

    def block(xb):
        q = (xb @ w_q).reshape(TOK_BLOCK, PEER_HEADS, 2, PEER_DHALF)
        s = jnp.einsum('thcd,hcnd->thcn', q, sub_keys).astype(jnp.float32)
        top_s, top_i = lax.top_k(s, K)
        cand = top_s[:, :, 0, :, None] + top_s[:, :, 1, None, :]
        best_s, best_c = lax.top_k(cand.reshape(TOK_BLOCK, PEER_HEADS, K * K), K)
        i1 = jnp.take_along_axis(top_i[:, :, 0], best_c // K, axis=-1)
        i2 = jnp.take_along_axis(top_i[:, :, 1], best_c % K, axis=-1)
        e = (i1 * PEER_NKEYS + i2).reshape(TOK_BLOCK, PEER_HEADS * K)
        gate = jax.nn.softmax(best_s, axis=-1).reshape(TOK_BLOCK, PEER_HEADS * K)
        u = expert_u[e]
        act = jax.nn.gelu(jnp.einsum('td,ted->te', xb, u), approximate=False)
        coef = (gate * act.astype(jnp.float32)).astype(xb.dtype)
        return jnp.einsum('te,ted->td', coef, expert_v[e])

    y = lax.map(block, xt)
    return y.reshape(n_blocks * TOK_BLOCK, D)[:n_tok].reshape(B, T, D)

def first_inputs(seed: int = 0) -> dict:
    key = jax.random.key(seed)
    ks = jax.random.split(key, 32)
    f32 = jnp.float32
    L = DEPTH
    D = D_MODEL

    def nrm(k, shape, s):
        return jax.random.normal(k, shape, f32) * s

    return {
        "x": nrm(ks[0], (BATCH, SEQ, D), 1.0),
        "meta_tokens": nrm(ks[1], (N_META, D), 1.0),
        "g_mix": 1.0 + nrm(ks[2], (L, D), 0.01),
        "w_in": nrm(ks[3], (L, D, IN_TOTAL), D ** -0.5),
        "conv_w": nrm(ks[4], (L, CONV_KERNEL, CONV_CH), CONV_KERNEL ** -0.5),
        "conv_b": nrm(ks[5], (L, CONV_CH), 0.01),
        "conv_ln_g": 1.0 + nrm(ks[6], (L, CONV_CH), 0.01),
        "conv_ln_b": nrm(ks[7], (L, CONV_CH), 0.01),
        "w_conv_out": nrm(ks[8], (L, CONV_CH, D), CONV_CH ** -0.5),
        "mu_shift": jax.random.uniform(ks[9], (L, SHIFT_TOTAL), f32),
        "w0": jax.random.uniform(ks[10], (L, RWKV_WIDTH), f32, -6.0, -1.0),
        "w_up": nrm(ks[11], (L, RANK_W, RWKV_WIDTH), 0.1 * RANK_W ** -0.5),
        "a0": nrm(ks[12], (L, RWKV_WIDTH), 0.1),
        "a_up": nrm(ks[13], (L, RANK_A, RWKV_WIDTH), 0.1 * RANK_A ** -0.5),
        "g_up": nrm(ks[14], (L, RANK_G, RWKV_WIDTH), RANK_G ** -0.5),
        "k_k": 0.85 + nrm(ks[15], (L, RWKV_WIDTH), 0.02),
        "k_a": 1.0 + nrm(ks[16], (L, RWKV_WIDTH), 0.02),
        "r_k": nrm(ks[17], (L, RWKV_HEADS, RWKV_HEAD), 0.1),
        "gn_g": 1.0 + nrm(ks[18], (L, RWKV_WIDTH), 0.01),
        "gn_b": nrm(ks[19], (L, RWKV_WIDTH), 0.01),
        "w_rwkv_out": nrm(ks[20], (L, RWKV_WIDTH, D), RWKV_WIDTH ** -0.5),
        "w_o": nrm(ks[21], (L, D, D), D ** -0.5),
        "g_ffn": 1.0 + nrm(ks[22], (L, D), 0.01),
        "w_q": nrm(ks[23], (L, D, PEER_HEADS * 2 * PEER_DHALF), D ** -0.5),
        "sub_keys": nrm(ks[24], (L, PEER_HEADS, 2, PEER_NKEYS, PEER_DHALF), PEER_DHALF ** -0.5),
        "expert_u": nrm(ks[25], (L, PEER_EXPERTS, D), D ** -0.5),
        "expert_v": nrm(ks[26], (L, PEER_EXPERTS, D), PEER_HEADS ** -0.5),
        "g_final": 1.0 + nrm(ks[27], (D,), 0.01),
    }

def first_block(x, meta_tokens, g_mix, w_in, conv_w, conv_b, conv_ln_g, conv_ln_b, w_conv_out,
              mu_shift, w0, w_up, a0, a_up, g_up, k_k, k_a, r_k, gn_g, gn_b, w_rwkv_out,
              w_o, g_ffn, w_q, sub_keys, expert_u, expert_v, g_final):
    B = x.shape[0]
    meta = jnp.broadcast_to(meta_tokens[None].astype(x.dtype), (B, N_META, D_MODEL))
    h = jnp.concatenate([meta, x], axis=1)
    for l in range(DEPTH):
        z = rmsnorm(h, g_mix[l]) @ w_in[l]
        conv_val, conv_gate, rwkv_in, gate_logits = jnp.split(z, IN_SPLITS, axis=-1)
        y_a = conformer_conv(conv_val, conv_gate, conv_w[l], conv_b[l], conv_ln_g[l], conv_ln_b[l], w_conv_out[l])
        y_b = rwkv7_mix(rwkv_in, mu_shift[l], w0[l], w_up[l], a0[l], a_up[l], g_up[l],
                        k_k[l], k_a[l], r_k[l], gn_g[l], gn_b[l], w_rwkv_out[l])
        gate_a, gate_b = jnp.split(jax.nn.sigmoid(gate_logits), N_BRANCH, axis=-1)
        h = h + (gate_a * y_a + gate_b * y_b) @ w_o[l]
        h = h + peer_ffn(rmsnorm(h, g_ffn[l]), w_q[l], sub_keys[l], expert_u[l], expert_v[l])
    return rmsnorm(h, g_final)[:, N_META:]


DEPTH_2 = 2

N_MEM = 256
GLA_HEADS = 6
GLA_DK = 64
GLA_DV = 128
GLA_K = GLA_HEADS * GLA_DK
GLA_V = GLA_HEADS * GLA_DV
GLA_GATE_RANK = 16
GLA_TAU = 16.0
GLA_CHUNK = 64
SB_HEADS = 12
SB_DIM = 64
SB_W = SB_HEADS * SB_DIM
SB_BLOCK = 128
MEM_HEADS = 4
MEM_DIM = 64
MEM_W = MEM_HEADS * MEM_DIM
PEER_KEYS = 128
PEER_EXPERTS_2 = PEER_KEYS * PEER_KEYS
PEER_QHALF = 128
PEER_TOKEN_BLOCK = 128
N_A_LAYERS = DEPTH_2 // 2
N_B_LAYERS = DEPTH_2 - N_A_LAYERS
DEEPNORM_ALPHA = (2.0 * DEPTH_2) ** 0.25
DEEPNORM_BETA = (8.0 * DEPTH_2) ** -0.25
EPS = 1e-5
A_IN_SPLITS = [GLA_K, 2 * GLA_K, 2 * GLA_K + GLA_V, 2 * GLA_K + 2 * GLA_V, 2 * GLA_K + 2 * GLA_V + GLA_GATE_RANK]
A_IN_W = 2 * GLA_K + 2 * GLA_V + GLA_GATE_RANK + MEM_W
B_IN_W = SB_W + MEM_W


def layer_norm(x, g, b):
    xf = x.astype(jnp.float32)
    mu = jnp.mean(xf, axis=-1, keepdims=True)
    var = jnp.mean(jnp.square(xf - mu), axis=-1, keepdims=True)
    return ((xf - mu) * lax.rsqrt(var + EPS) * g + b).astype(x.dtype)

def to_heads(t, n_heads, d):
    B, T, _ = t.shape
    return t.reshape(B, T, n_heads, d).transpose(0, 2, 1, 3)

def from_heads(t):
    B, H, T, d = t.shape
    return t.transpose(0, 2, 1, 3).reshape(B, T, H * d)

def memory_attention(qm, mem, w_mem_kv):
    B, T, _ = qm.shape
    kv = mem @ w_mem_kv
    km, vm = jnp.split(kv, [MEM_W], axis=-1)
    q = qm.reshape(B, T, MEM_HEADS, MEM_DIM)
    k = km.reshape(B, -1, MEM_HEADS, MEM_DIM)
    v = vm.reshape(B, -1, MEM_HEADS, MEM_DIM)
    s = jnp.einsum('bthd,bmhd->bhtm', q, k).astype(jnp.float32) * (MEM_DIM ** -0.5)
    p = jax.nn.softmax(s, axis=-1).astype(v.dtype)
    return jnp.einsum('bhtm,bmhd->bthd', p, v).reshape(B, T, MEM_W)

def gla_chunked(q, k, v, log_g):
    B, H, T, dk = q.shape
    dv = v.shape[-1]
    n = T // GLA_CHUNK
    c = lambda t: t.astype(jnp.float32).reshape(B, H, n, GLA_CHUNK, t.shape[-1])
    q, k, v, log_g = c(q), c(k), c(v), c(log_g)
    b = jnp.cumsum(log_g, axis=-2)
    b_last = b[..., -1, :]
    q_dec = q * jnp.exp(b)
    k_inv = k * jnp.exp(-b)
    causal = jnp.tril(jnp.ones((GLA_CHUNK, GLA_CHUNK), dtype=bool))
    attn = jnp.where(causal, jnp.einsum('bhncd,bhnsd->bhncs', q_dec, k_inv), 0.0)
    o_intra = jnp.einsum('bhncs,bhnsv->bhncv', attn, v)
    k_to_end = k * jnp.exp(b_last[..., None, :] - b)
    du = jnp.einsum('bhncd,bhncv->bhndv', k_to_end, v)

    def step(S, inp):
        decay, inc = inp
        return decay[..., None] * S + inc, S

    S0 = jnp.zeros((B, H, dk, dv), jnp.float32)
    _, S_start = lax.scan(step, S0, (jnp.moveaxis(jnp.exp(b_last), 2, 0), jnp.moveaxis(du, 2, 0)))
    S_start = jnp.moveaxis(S_start, 0, 2)
    o_inter = jnp.einsum('bhncd,bhndv->bhncv', q_dec, S_start)
    return (o_intra + o_inter).reshape(B, H, T, dv)

def gla_layer_mixer(x, mem, w_in, w_gate2, b_gate, head_g, w_mem_kv, w_out):
    proj = x @ w_in
    q, k, v, r, glr, qm = jnp.split(proj, A_IN_SPLITS, axis=-1)
    log_g = jax.nn.log_sigmoid((glr @ w_gate2 + b_gate).astype(jnp.float32)) / GLA_TAU
    o = gla_chunked(to_heads(q, GLA_HEADS, GLA_DK) * (GLA_DK ** -0.5),
                    to_heads(k, GLA_HEADS, GLA_DK),
                    to_heads(v, GLA_HEADS, GLA_DV),
                    to_heads(log_g, GLA_HEADS, GLA_DK))
    o = o * lax.rsqrt(jnp.mean(jnp.square(o), axis=-1, keepdims=True) + EPS) * head_g[None, :, None, :]
    o = from_heads(o).astype(x.dtype) * jax.nn.silu(r)
    m = memory_attention(qm, mem, w_mem_kv)
    return jnp.concatenate([o, m], axis=-1) @ w_out

def stick_breaking(q, k, v):
    B, H, T, d = q.shape
    scale = d ** -0.5
    outs = []
    for i in range(T // SB_BLOCK):
        t0, t1 = i * SB_BLOCK, (i + 1) * SB_BLOCK
        z = jnp.einsum('bhtd,bhsd->bhts', q[:, :, t0:t1], k[:, :, :t1]).astype(jnp.float32) * scale
        t_pos = t0 + jnp.arange(SB_BLOCK)[:, None]
        s_pos = jnp.arange(t1)[None, :]
        mask = s_pos < t_pos
        log_not = jnp.where(mask, jax.nn.log_sigmoid(-z), 0.0)
        log_A = jax.nn.log_sigmoid(z) + lax.cumsum(log_not, axis=3, reverse=True) - log_not
        A = jnp.where(mask, jnp.exp(log_A), 0.0).astype(v.dtype)
        outs.append(jnp.einsum('bhts,bhsd->bhtd', A, v[:, :, :t1]))
    return jnp.concatenate(outs, axis=2)

def sb_layer_mixer(x, mem, k_sb, v_sb, w_in, w_mem_kv, w_out):
    q, qm = jnp.split(x @ w_in, [SB_W], axis=-1)
    o = from_heads(stick_breaking(to_heads(q, SB_HEADS, SB_DIM), k_sb, v_sb))
    m = memory_attention(qm, mem, w_mem_kv)
    return jnp.concatenate([o, m], axis=-1) @ w_out

def peer(x, w_q, subkeys, u_tab, v_tab):
    B, T, D = x.shape
    N = B * T
    xf = x.reshape(N, D)
    q = (xf @ w_q).reshape(N, PEER_HEADS, 2, PEER_QHALF)
    s = jnp.einsum('nhpd,hpkd->nhpk', q, subkeys).astype(jnp.float32)
    top_s, top_i = lax.top_k(s, PEER_TOPK)
    cand_s = (top_s[:, :, 0, :, None] + top_s[:, :, 1, None, :]).reshape(N, PEER_HEADS, PEER_TOPK * PEER_TOPK)
    cand_i = (top_i[:, :, 0, :, None] * PEER_KEYS + top_i[:, :, 1, None, :]).reshape(N, PEER_HEADS, PEER_TOPK * PEER_TOPK)
    best_s, best_pos = lax.top_k(cand_s, PEER_TOPK)
    idx = jnp.take_along_axis(cand_i, best_pos, axis=-1)
    g = jax.nn.softmax(best_s, axis=-1).astype(x.dtype)
    nb = N // PEER_TOKEN_BLOCK
    xb = xf.reshape(nb, PEER_TOKEN_BLOCK, D)
    ib = idx.reshape(nb, PEER_TOKEN_BLOCK, PEER_HEADS, PEER_TOPK)
    gb = g.reshape(nb, PEER_TOKEN_BLOCK, PEER_HEADS, PEER_TOPK)

    def apply_experts(args):
        xt, it, gt = args
        act = jax.nn.gelu(jnp.einsum('nd,nhkd->nhk', xt, u_tab[it]), approximate=False)
        return jnp.einsum('nhk,nhkd->nd', gt * act, v_tab[it])

    return lax.map(apply_experts, (xb, ib, gb)).reshape(B, T, D)

def second_inputs(seed: int = 0) -> dict:
    key = jax.random.key(seed)
    ks = jax.random.split(key, 20)
    nrm = lambda k, shape, scale: jax.random.normal(k, shape, jnp.float32) * scale
    ds = D_MODEL ** -0.5
    beta = DEEPNORM_BETA
    a_col_scale = jnp.concatenate([
        jnp.ones((2 * GLA_K,), jnp.float32),
        jnp.full((GLA_V,), beta, jnp.float32),
        jnp.ones((GLA_V + GLA_GATE_RANK + MEM_W,), jnp.float32)])
    mem_col_scale = jnp.concatenate([jnp.ones((MEM_W,), jnp.float32), jnp.full((MEM_W,), beta, jnp.float32)])
    sb_col_scale = jnp.concatenate([jnp.ones((SB_W,), jnp.float32), jnp.full((SB_W,), beta, jnp.float32)])
    return {
        "x": nrm(ks[0], (BATCH, SEQ, D_MODEL), 1.0),
        "mem": nrm(ks[1], (BATCH, N_MEM, D_MODEL), 1.0),
        "a_w_in": nrm(ks[2], (N_A_LAYERS, D_MODEL, A_IN_W), ds) * a_col_scale,
        "a_w_gate2": nrm(ks[3], (N_A_LAYERS, GLA_GATE_RANK, GLA_K), GLA_GATE_RANK ** -0.5),
        "a_b_gate": nrm(ks[4], (N_A_LAYERS, GLA_K), 0.1),
        "a_head_g": 1.0 + nrm(ks[5], (N_A_LAYERS, GLA_HEADS, GLA_DV), 0.05),
        "a_w_mem_kv": nrm(ks[6], (N_A_LAYERS, D_MODEL, 2 * MEM_W), ds) * mem_col_scale,
        "a_w_out": nrm(ks[7], (N_A_LAYERS, GLA_V + MEM_W, D_MODEL), (GLA_V + MEM_W) ** -0.5 * beta),
        "b_w_in": nrm(ks[8], (N_B_LAYERS, D_MODEL, B_IN_W), ds),
        "b_w_mem_kv": nrm(ks[9], (N_B_LAYERS, D_MODEL, 2 * MEM_W), ds) * mem_col_scale,
        "b_w_out": nrm(ks[10], (N_B_LAYERS, SB_W + MEM_W, D_MODEL), (SB_W + MEM_W) ** -0.5 * beta),
        "sb_w_kv": nrm(ks[11], (D_MODEL, 2 * SB_W), ds) * sb_col_scale,
        "peer_w_q": nrm(ks[12], (DEPTH_2, D_MODEL, PEER_HEADS * 2 * PEER_QHALF), ds),
        "peer_subkeys": nrm(ks[13], (DEPTH_2, PEER_HEADS, 2, PEER_KEYS, PEER_QHALF), PEER_QHALF ** -0.5),
        "peer_u": nrm(ks[14], (DEPTH_2, PEER_EXPERTS_2, D_MODEL), ds),
        "peer_v": nrm(ks[15], (DEPTH_2, PEER_EXPERTS_2, D_MODEL), beta * PEER_HEADS ** -0.5),
        "ln_g": 1.0 + nrm(ks[16], (DEPTH_2, 2, D_MODEL), 0.05),
        "ln_b": nrm(ks[17], (DEPTH_2, 2, D_MODEL), 0.02),
    }

def second_block(x, mem, a_w_in, a_w_gate2, a_b_gate, a_head_g, a_w_mem_kv, a_w_out,
              b_w_in, b_w_mem_kv, b_w_out, sb_w_kv, peer_w_q, peer_subkeys, peer_u, peer_v,
              ln_g, ln_b):
    h = x
    k_sb = None
    v_sb = None
    for layer in range(DEPTH_2):
        if layer < N_A_LAYERS:
            i = layer
            mix = gla_layer_mixer(h, mem, a_w_in[i], a_w_gate2[i], a_b_gate[i], a_head_g[i],
                                  a_w_mem_kv[i], a_w_out[i])
        else:
            if layer == N_A_LAYERS:
                ksb, vsb = jnp.split(h @ sb_w_kv, [SB_W], axis=-1)
                k_sb = to_heads(ksb, SB_HEADS, SB_DIM)
                v_sb = to_heads(vsb, SB_HEADS, SB_DIM)
            j = layer - N_A_LAYERS
            mix = sb_layer_mixer(h, mem, k_sb, v_sb, b_w_in[j], b_w_mem_kv[j], b_w_out[j])
        h = layer_norm(DEEPNORM_ALPHA * h + mix, ln_g[layer, 0], ln_b[layer, 0])
        ffn = peer(h, peer_w_q[layer], peer_subkeys[layer], peer_u[layer], peer_v[layer])
        h = layer_norm(DEEPNORM_ALPHA * h + ffn, ln_g[layer, 1], ln_b[layer, 1])
    return h


def setup_inputs(seed=0):
    out = dict(first_inputs(seed))
    for name, value in second_inputs(seed + 1).items():
        if name != "x":
            out[name + "_2"] = value
    return out


def reference(
    x, meta_tokens, g_mix, w_in, conv_w, conv_b, conv_ln_g, conv_ln_b, w_conv_out, mu_shift, w0,
    w_up, a0, a_up, g_up, k_k, k_a, r_k, gn_g, gn_b, w_rwkv_out, w_o, g_ffn, w_q, sub_keys,
    expert_u, expert_v, g_final, mem_2, a_w_in_2, a_w_gate2_2, a_b_gate_2, a_head_g_2,
    a_w_mem_kv_2, a_w_out_2, b_w_in_2, b_w_mem_kv_2, b_w_out_2, sb_w_kv_2, peer_w_q_2,
    peer_subkeys_2, peer_u_2, peer_v_2, ln_g_2, ln_b_2,
):
    x = first_block(
        x, meta_tokens, g_mix, w_in, conv_w, conv_b, conv_ln_g, conv_ln_b, w_conv_out, mu_shift,
        w0, w_up, a0, a_up, g_up, k_k, k_a, r_k, gn_g, gn_b, w_rwkv_out, w_o, g_ffn, w_q,
        sub_keys, expert_u, expert_v, g_final,
    )
    return second_block(
        x, mem_2, a_w_in_2, a_w_gate2_2, a_b_gate_2, a_head_g_2, a_w_mem_kv_2, a_w_out_2,
        b_w_in_2, b_w_mem_kv_2, b_w_out_2, sb_w_kv_2, peer_w_q_2, peer_subkeys_2, peer_u_2,
        peer_v_2, ln_g_2, ln_b_2,
    )


_drawn_inputs = setup_inputs


def setup_inputs(seed=0):
    import zlib

    import numpy as np

    out = dict(_drawn_inputs(seed))
    spreads = {}
    factors = {'g_mix': 2.885,
     'conv_b': 2.915,
     'conv_ln_g': 3.823,
     'conv_ln_b': 3.883,
     'w_up': 6.371,
     'k_k': 3.321,
     'k_a': 2.985,
     'gn_g': 4.021,
     'gn_b': 4.138,
     'g_final': 4.083,
     'mem_2': 3.422,
     'a_b_gate_2': 4.829,
     'a_head_g_2': 4.441,
     'a_w_mem_kv_2': 3.774,
     'b_w_mem_kv_2': 4.361}
    for name, (base, spread) in spreads.items():
        noise = np.random.default_rng([zlib.crc32(name.encode()), seed]).standard_normal(out[name].shape)
        drawn = base * np.exp(spread * noise) if base else spread * noise
        out[name] = __import__('jax').numpy.asarray(drawn.astype(out[name].dtype))
    for name, factor in factors.items():
        out[name] = (out[name] * factor).astype(out[name].dtype)
    return out
```

```python
from contextlib import ExitStack

import numpy as np

import concourse.bass as bass
from concourse import mybir

ALU = mybir.AluOpType
ACT = mybir.ActivationFunctionType
AX = mybir.AxisListType
F32 = mybir.dt.float32
U32 = mybir.dt.uint32

P = 128
D = 1024
KC = D // P
TOK = 256
NT = TOK // P
META = 16
TALL = TOK + META
CONV_C = 512
TAPS = 31
CT = CONV_C // P
RW = 512
RH = 64
RM = RW // P
CH = 64
LEVELS = 6
PH = 8
PK = 16
NKEYS = 128
Q_GROUPS = ((0, 2), (2, 6), (6, 10), (10, 14), (14, 16))
SLOTS = 6
RING = 8
DECAY = float(np.exp(-0.5))
GLA_H, GLA_DK, GLA_DV = 6, 64, 128
SB_H = 12
MEM_H = 4
ALPHA = float((2.0 * 2) ** 0.25)

CONST = {}
_n = 0
for _name, _w in (("ident", P), ("ones", P), ("headsum", P), ("strict", P), ("incl", P), ("ident2", 64),
                  ("scan_all", TALL), ("scan", TOK), ("below", P), ("sbmask", P), ("iota", PK),
                  ("onehead", RM * 8), ("levels", LEVELS * P)):
    CONST[_name] = (_n, _w)
    _n += _w
NCONST = _n
NCONST_KEEP = CONST["onehead"][0]

COLS = {}
_n = 0
for _name, _w in (("g_mix", 8), ("mu", 14), ("w0", 4), ("a0", 4), ("k_k", 4), ("k_a", 4), ("r_k", 4),
                  ("conv_b", 4), ("conv_ln_g", 4), ("conv_ln_b", 4), ("conv_w", CT * TAPS),
                  ("b_gate", 3), ("head_g", 6)):
    COLS[_name] = (_n, _w)
    _n += _w
NCOLS = _n


def constants():
    c = np.zeros((P, NCONST), np.float32)
    p = np.arange(P)[:, None]
    f = np.arange(P)[None, :]

    def put(name, value):
        at, w = CONST[name]
        c[:, at:at + w] = value

    put("ident", p == f)
    put("ones", 1.0)
    put("headsum", p // RH == f // RH)
    put("strict", (p // CH == f // CH) & (p < f))
    put("incl", (p // CH == f // CH) & (p <= f))
    put("ident2", p % 64 == f[:, :64])
    t = np.arange(TALL)[None, :] + 0 * p
    put("scan_all", (t != 0) & ((t - META) % CH != 0))
    put("scan", t[:, :TOK] % CH != 0)
    put("below", p > f)
    put("sbmask", p < f)
    put("iota", np.arange(PK)[None, :] + 0 * p)
    m = np.arange(RM)[None, :, None]
    h = np.arange(8)[None, None, :]
    put("onehead", (2 * m + p[:, :, None] // RH == h).reshape(P, RM * 8))
    lev = [((p // (2 * s) == f // (2 * s)) & (p // s % 2 == 0) & (f // s % 2 == 1)) for s in (1, 2, 4, 8, 16, 32)]
    put("levels", np.concatenate(lev, 1))
    return c


class Banks:

    def __init__(self, banks, full, emptied):
        self.banks, self.sem_full, self.sem_emptied = banks, full, emptied
        self.fills = [0] * len(banks)
        self.reads = [0] * len(banks)
        self.jobs = {}
        self.n = 0

    def take(self, name, reads=1):
        b = self.n % len(self.banks)
        self.n += 1
        before = self.reads[b] + 1
        self.fills[b] += 1
        self.reads[b] += reads
        self.jobs[name] = (b, self.fills[b], self.reads[b] + 1)
        return self.sem_emptied[b], before

    def bank(self, name):
        return self.banks[self.jobs[name][0]]

    def full_sem(self, name):
        return self.sem_full[self.jobs[name][0]]

    def emptied_sem(self, name):
        return self.sem_emptied[self.jobs[name][0]]

    def full(self, name):
        b, fills, _ = self.jobs[name]
        return self.sem_full[b], fills

    def emptied(self, name):
        b, _, reads = self.jobs[name]
        return self.sem_emptied[b], reads


class Arena:

    def __init__(self, tensor, size):
        self.t, self.size, self.at = tensor, size, 0

    def view(self, at, *dims):
        n = int(np.prod(dims))
        assert at + n <= self.size, (at, n, self.size)
        ap = self.t[:, at:at + n]
        if len(dims) == 2:
            ap = ap.rearrange("p (a b) -> p a b", a=dims[0])
        elif len(dims) == 3:
            ap = ap.rearrange("p (a b c) -> p a b c", a=dims[0], b=dims[1])
        return ap

    def take(self, *dims):
        v = self.view(self.at, *dims)
        self.at += int(np.prod(dims))
        return v


def bc(ap, *dims):
    return bass.AP(tensor=ap.tensor, offset=ap.offset, ap=[list(ap.ap[0])] + [list(d) for d in dims])


def build(nc, io):
    with ExitStack() as ctx:
        def sbuf(name, shape, dt=F32):
            return ctx.enter_context(nc.sbuf_tensor(name, shape, dt))

        sems = {}

        def sem(name):
            if name not in sems:
                sems[name] = ctx.enter_context(nc.semaphore(name))
            return sems[name]

        counts = {}

        def count(name, by=1):
            counts[name] = counts.get(name, 0) + by
            return counts[name]

        const = sbuf("const", [P, NCONST_KEEP])
        cols = sbuf("cols", [P, NCOLS])
        h = sbuf("h", [P, NT, D])
        xT = sbuf("xT", [P, KC, TALL])
        weights = sbuf("weights", [P, SLOTS, D])
        rows = sbuf("rows", [P, 2, D])
        small = sbuf("small", [P, 64])
        idx_best = sbuf("idx_best", [P, 2, PK], U32)
        idx_pos = sbuf("idx_pos", [P, 3, PK], U32)
        idx_next = sbuf("idx_next", [P, PK], U32)
        idx = sbuf("idx", [P, 3, PK], U32)
        ARENA = 38600
        arena_t = sbuf("arena", [P, ARENA])

        def k(name, parts=P):
            at, w = CONST[name]
            return const[0:parts, at:at + w]

        def col(name, j, lo=0, hi=P):
            at, _ = COLS[name]
            return cols[lo:hi, at + j:at + j + 1]

        ident = k("ident")
        ones = k("ones")

        psum = [ctx.enter_context(nc.psum_tensor(f"bank{b}", [P, 512], F32)) for b in range(8)]
        NB = 6
        banks = Banks(psum[:NB], [sem(f"full_{b}") for b in range(NB)], [sem(f"emptied_{b}") for b in range(NB)])
        acc_lo, acc_hi = psum[6], psum[7]

        plan = []

        def block_of(name, src, width=D, parts=P):
            plan.append((name, src, width, parts))

        for c in range(CT):
            block_of(("gate", c), io["w_in"][4 + c])
            block_of(("val", c), io["w_in"][c])
        for j in range(14):
            block_of(("z", j), io["w_in"][8 + j])
        for j in range(4):
            block_of(("ab", j), io["w_in"][22 + j])
        block_of("lora", io["lora"])
        for j in range(4, 16):
            block_of(("ab", j), io["w_in"][22 + j])
        for j in range(4):
            block_of(("conv_out", j), io["w_conv_out"][j])
        for j in range(4):
            block_of(("rwkv_out", j), io["w_rwkv_out"][j])
        for j in range(KC):
            block_of(("w_o", j), io["w_o"][j])

        def plan_peer(n):
            for lo, hi in Q_GROUPS:
                for j in range(lo, hi):
                    block_of(("w_q", n, j), io["w_q"][n][j])
                block_of(("keys", n, lo), io["keys"][n][:, lo * P:hi * P], (hi - lo) * P)

        def plan_mem(n):
            for j in range(2):
                block_of(("mem_k", n, j), io["mem_k"][n][j])
            for j in range(2):
                block_of(("mem_v", n, j), io["mem_v"][n][j])

        plan_peer(0)
        plan_mem(0)
        block_of("glr", io["a_glr"], P // 8 * KC)
        for j in range(3):
            block_of(("a_q", j), io["a_fm"][j])
            block_of(("a_k", j), io["a_fm"][3 + j])
        for j in range(KC):
            block_of(("a_v", j), io["a_v"][j], 768)
        for j in range(6):
            block_of(("a_r", j), io["a_fm"][6 + j])
        for j in range(2):
            block_of(("a_qm", j), io["a_fm"][12 + j])
        for j in range(KC):
            block_of(("a_out", j), io["a_out"][j])
        plan_peer(1)
        plan_mem(1)
        for j in range(6):
            block_of(("b_q", j), io["b_fm"][j])
            block_of(("b_k", j), io["sb_k"][j])
        for j in range(KC):
            block_of(("b_v", j), io["sb_v"][j], 768)
        for j in range(2):
            block_of(("b_qm", j), io["b_fm"][6 + j])
        for j in range(KC):
            block_of(("b_out", j), io["b_out"][j])
        plan_peer(2)

        taken = []

        def landed(name):
            n = len(taken)
            assert plan[n][0] == name, (plan[n][0], name)
            taken.append(name)
            return sem(f"landed_{n % SLOTS}"), 16 * (n // SLOTS + 1)

        def slot(name):
            return weights[:, taken.index(name) % SLOTS, :]

        released = {}

        def last_use(job):
            released[len(taken) - 1] = job

        def last_use_here():
            released[len(taken) - 1] = count("blocks_used")

        def load_blocks(sp, lo, hi):
            for n in range(lo, min(hi, len(plan))):
                _, src, width, parts = plan[n]
                if n >= SLOTS:
                    by = released[n - SLOTS]
                    if type(by) is int:
                        sp.wait_ge(sem("blocks_used"), by)
                    else:
                        sp.wait_ge(*banks.full(by))
                sp.dma_start(weights[0:parts, n % SLOTS, 0:width], src).then_inc(sem(f"landed_{n % SLOTS}"), 16)

        def fm_tile(pe, job, block, x, n):
            pe.wait_ge(*landed(block))
            w = slot(block)
            pe.wait_ge(*banks.take(job))
            out = banks.bank(job)
            for kc in range(KC):
                ins = nc.tensor.matmul(out[:, 0:n], w[:, kc * P:(kc + 1) * P], x[:, kc, :],
                                       start=kc == 0, stop=kc == KC - 1)
            ins.then_inc(banks.full_sem(job), 1)
            last_use(job)

        REGION = 8 * 2048
        A = Arena(arena_t, ARENA)
        region = A.take(REGION)
        zs = A.take(14, TALL)
        ycv = A.take(CT, TOK)
        gates = A.take(16, TOK)
        alpha, beta, kappa, rho = (A.take(RM, TALL) for _ in range(4))
        tm = A.take(NT * 4, RW)
        tmm = A.take(4, RW)
        gtm = A.take(NT, RW)
        L1C = A.at
        onehead = A.take(RM, 8)
        levels = A.take(LEVELS, P)
        meta_mats = A.take(12, 64)
        rksel = A.take(RM, 8)
        pend = A.take(5, RM)
        front_end = A.at
        B = Arena(arena_t, REGION)
        z = B.take(14, TALL + 1)
        sg, av, kk, kp, cum, tt = (B.take(RM, TALL) for _ in range(6))
        sgate = B.take(CT, TALL)
        u = B.take(CT, TALL + TAPS - 1)
        sq = B.take(CT, TOK)
        E1, E2, E3 = (A.view(i * RM * TALL, RM, TALL) for i in range(3))
        B = Arena(arena_t, REGION)
        GROUPS = [(i, par) for i in range(NT) for par in range(2)]
        MT, NTm, QK, QB, Tm, Wm = ({g: B.take(4, P) for g in GROUPS} for _ in range(6))
        MTl4 = [B.take(4, P) for _ in range(4)]
        Ym = {g: B.take(4, P) for g in GROUPS}
        mm = {}
        n = 0
        for g in (("meta", 0), ("meta", 1)):
            for q in ("MT", "NT", "T", "W", "MTl", "Y"):
                mm[g, q] = meta_mats[0:META, n, :].rearrange("p (a b) -> p a b", a=4)
                n += 1
        for g in (("meta", 0), ("meta", 1)):
            MT[g], NTm[g], Tm[g], Wm[g], Ym[g] = (mm[g, q] for q in ("MT", "NT", "T", "W", "Y"))
        ALLG = GROUPS + [("meta", 0), ("meta", 1)]
        B = Arena(arena_t, 2048)
        NV = {g: B.take(4, RH) for g in GROUPS}
        RQT = B.take(RM, NT, P)
        B = Arena(arena_t, REGION)
        B.at = 4 * 2048
        UA = {g: B.take(4, P) for g in GROUPS}
        B.at = 6 * 2048
        KB, GT, S = B.take(4, RM, RH), B.take(3, RM, RH), B.take(4, RM, RH)
        for par in range(2):
            NV["meta", par] = B.take(4, RH)
            UA["meta", par] = A.view(REGION + 4 * TALL + par * 512, 4, P)
        assert A.at <= ARENA, A.at
        o_at = (REGION + 14 * TALL + 1024 + 4096)
        otm = A.view(o_at, NT * 8, RH)
        otmp = A.view(o_at + 1024, NT * 8, RH)
        oT = A.view(o_at + 2048, RM, TOK)
        hn = A.view(o_at, NT, D)
        hmeta = A.view(o_at + 2048, D)
        hsq = A.view(o_at + 3072, D)


        def one_tensor(pe):
            pe.wait_ge(sem("const_in"), 16)
            pe.wait_ge(sem("hn_ready"), 3)
            for kc in range(KC):
                pe.wait_ge(*banks.take(("xT", kc)))
                out = banks.bank(("xT", kc))
                f = slice(kc * P, (kc + 1) * P)
                nc.tensor.transpose(out[:, 0:META], hmeta[0:META, f], ident[0:META, 0:META])
                nc.tensor.transpose(out[:, META:META + P], hn[:, 0, f], ident)
                nc.tensor.transpose(out[:, META + P:TALL], hn[:, 1, f], ident).then_inc(banks.full_sem(("xT", kc)), 1)
            for kc in range(KC):
                pe.wait_ge(*banks.emptied(("xT", kc)))
            for c in range(CT):
                for name in ("gate", "val"):
                    fm_tile(pe, (name, c), (name, c), xT, TALL)
            for j in range(14):
                fm_tile(pe, ("z", j), ("z", j), xT, TALL)
            pe.wait_ge(sem("conv_tap"), CT * TAPS)
            pe.wait_ge(*banks.take("conv_sum"))
            out = banks.bank("conv_sum")
            for c in range(CT):
                ins = nc.tensor.matmul(out[:, 0:TOK], ones, ycv[:, c, :], start=c == 0, stop=c == CT - 1)
            ins.then_inc(banks.full_sem("conv_sum"), 1)
            for j in range(4):
                fm_tile(pe, ("ab", j), ("ab", j), xT[:, :, META:TALL], TOK)
            pe.wait_ge(sem("conv_sq"), 1)
            pe.wait_ge(*banks.take("conv_var"))
            out = banks.bank("conv_var")
            for c in range(CT):
                ins = nc.tensor.matmul(out[:, 0:TOK], ones, sq[:, c, :], start=c == 0, stop=c == CT - 1)
            ins.then_inc(banks.full_sem("conv_var"), 1)
            pe.wait_ge(*landed("lora"))
            lora = slot("lora")
            pe.wait_ge(sem("lora_in"), 2)
            for m in range(RM):
                f = slice(m * P, (m + 1) * P)
                pe.wait_ge(*banks.take(("decay", m)))
                out = banks.bank(("decay", m))
                nc.tensor.matmul(out[:, 0:TALL], lora[0:64, f], zs[0:64, 12, :],
                                 start=True, stop=True).then_inc(banks.full_sem(("decay", m)), 1)
                pe.wait_ge(*banks.take(("a", m)))
                out = banks.bank(("a", m))
                nc.tensor.matmul(out[:, 0:TALL], lora[64:128, f], zs[64:128, 12, :],
                                 start=True, stop=True).then_inc(banks.full_sem(("a", m)), 1)
            for i in range(NT):
                pe.wait_ge(*banks.take(("g", i)))
                out = banks.bank(("g", i))
                ins = nc.tensor.matmul(out[:, :], zs[:, 13, META + i * P:META + (i + 1) * P], lora[:, 512:1024],
                                       start=True, stop=True)
                ins.then_inc(banks.full_sem(("g", i)), 1)
            last_use(("g", NT - 1))
            pe.wait_ge(sem("kk_sq"), 1)
            for m in range(RM):
                pe.wait_ge(*banks.take(("kk_sum", m)))
                out = banks.bank(("kk_sum", m))
                ins = nc.tensor.matmul(out[:, 0:TALL], k("headsum"), E1[:, m, :], start=True, stop=True)
                ins.then_inc(banks.full_sem(("kk_sum", m)), 1)
            for j in range(4, 16):
                fm_tile(pe, ("ab", j), ("ab", j), xT[:, :, META:TALL], TOK)
            pe.wait_ge(sem("conv_out_in"), CT)
            branch_out(pe, "conv_out", ycv)
            pe.wait_ge(sem("rkr_ready"), 1)
            pe.wait_ge(sem("rksel_ready"), 1)
            for i in range(NT):
                pe.wait_ge(*banks.take(("bonus", i)))
                out = banks.bank(("bonus", i))
                for m in range(RM):
                    ins = nc.tensor.matmul(out[:, 0:8], tt[:, m, META + i * P:META + (i + 1) * P], rksel[:, m, :],
                                           start=m == 0, stop=m == RM - 1)
                ins.then_inc(banks.full_sem(("bonus", i)), 1)
            pe.wait_ge(sem("abkr_ready"), 1)
            fms = (alpha, beta, kappa, zs[:, 8:12, :])
            for i in range(NT):
                for q, src in enumerate(fms):
                    pe.wait_ge(*banks.take(("tm", i, q)))
                    out = banks.bank(("tm", i, q))
                    for m in range(RM):
                        ins = nc.tensor.transpose(out[:, m * P:(m + 1) * P],
                                                  src[:, m, META + i * P:META + (i + 1) * P], ident)
                    ins.then_inc(banks.full_sem(("tm", i, q)), 1)
            for q, src in enumerate(fms):
                pe.wait_ge(*banks.take(("tm", "meta", q)))
                out = banks.bank(("tm", "meta", q))
                for m in range(RM):
                    ins = nc.tensor.transpose(out[0:META, m * P:(m + 1) * P], src[:, m, 0:META], ident)
                ins.then_inc(banks.full_sem(("tm", "meta", q)), 1)
            for i, par in ALLG:
                n = META if i == "meta" else P
                at = 0 if i == "meta" else META + i * P
                r = slice(64 * par, 64 * par + 64)
                for name, lhs, rhs in (("MT", beta, alpha), ("NT", kappa, alpha), ("QK", kappa, rho), ("QB", beta, rho)):
                    if i == "meta" and name[0] == "Q":
                        continue
                    pe.wait_ge(*banks.take((name, i, par)))
                    out = banks.bank((name, i, par))
                    for m in range(RM):
                        ins = nc.tensor.matmul(out[0:n, m * n:(m + 1) * n], lhs[r, m, at:at + n], rhs[r, m, at:at + n],
                                               start=True, stop=True)
                    ins.then_inc(banks.full_sem((name, i, par)), 1)
            for lev in range(LEVELS):
                for n_g, g in enumerate(ALLG):
                    n = META if g[0] == "meta" else P
                    mtl, t, w, y = level_bufs(g, n_g)
                    pe.wait_ge(sem("joins_ready"), lev * len(ALLG) + n_g + 1)
                    if lev == 0:
                        pe.wait_ge(sem("t_ready"), 2 * (n_g + 1))
                    else:
                        pe.wait_ge(*banks.emptied(("X", lev - 1, g)))
                        pe.wait_ge(*banks.emptied(("XT", lev - 1, g)))
                    pe.wait_ge(*banks.take(("Y", lev, g)))
                    out = banks.bank(("Y", lev, g))
                    for m in range(4):
                        ins = nc.tensor.matmul(out[0:n, m * n:(m + 1) * n], mtl[:, m, :], t[:, m, :], start=True, stop=True)
                    ins.then_inc(banks.full_sem(("Y", lev, g)), 1)
                for n_g, g in enumerate(ALLG):
                    n = META if g[0] == "meta" else P
                    mtl, t, w, y = level_bufs(g, n_g)
                    pe.wait_ge(*banks.emptied(("Y", lev, g)))
                    for name, lhs, rhs in (("X", w, y), ("XT", y, w)):
                        pe.wait_ge(*banks.take((name, lev, g)))
                        out = banks.bank((name, lev, g))
                        for m in range(4):
                            ins = nc.tensor.matmul(out[0:n, m * n:(m + 1) * n], lhs[:, m, :], rhs[:, m, :],
                                                   start=True, stop=True)
                        ins.then_inc(banks.full_sem((name, lev, g)), 1)
            for g in ALLG:
                pe.wait_ge(*banks.emptied(("X", LEVELS - 1, g)))
                pe.wait_ge(*banks.emptied(("XT", LEVELS - 1, g)))
            for i in (0, 1, "meta"):
                for n_q in range(4):
                    pe.wait_ge(*banks.emptied(("tm", i, n_q)))
            for g in ALLG:
                pe.wait_ge(*banks.emptied(("NT", *g)))
                i, par = g
                n = META if i == "meta" else P
                pe.wait_ge(*banks.take(("NV", g)))
                out = banks.bank(("NV", g))
                for m in range(RM):
                    ins = nc.tensor.matmul(out[0:n, m * RH:(m + 1) * RH], NTm[g][:, m, :],
                                           tmv(i, 3)[:, (2 * m + par) * RH:(2 * m + par + 1) * RH], start=True, stop=True)
                ins.then_inc(banks.full_sem(("NV", g)), 1)
            for g in ALLG:
                i, par = g
                n = META if i == "meta" else P
                pe.wait_ge(*banks.emptied(("NV", g)))
                pe.wait_ge(*banks.take(("UA", g)))
                out = banks.bank(("UA", g))
                for m in range(RM):
                    hs = slice((2 * m + par) * RH, (2 * m + par + 1) * RH)
                    nc.tensor.matmul(out[0:n, m * P:m * P + RH], Wm[g][:, m, :], NV[g][0:n, m, :], start=True, stop=True)
                    ins = nc.tensor.matmul(out[0:n, m * P + RH:(m + 1) * P], Wm[g][:, m, :], tmv(i, 0)[:, hs],
                                           start=True, stop=True)
                ins.then_inc(banks.full_sem(("UA", g)), 1)
            for g in ALLG:
                pe.wait_ge(*banks.emptied(("UA", g)))
            for c in range(4):
                i = "meta" if c == 0 else (c - 1) // 2
                lo = 0 if c == 0 else 64 * ((c - 1) % 2)
                r = slice(0, META) if c == 0 else slice(lo, lo + 64)
                pe.wait_ge(*banks.take(("KB", c), 1 if c == 0 else 2))
                out = banks.bank(("KB", c))
                for par in range(2):
                    o = slice(64 * par, 64 * par + 64)
                    for m in range(RM):
                        hs = slice((2 * m + par) * RH, (2 * m + par + 1) * RH)
                        ua = UA[i, par]
                        nc.tensor.matmul(out[o, m * RH:(m + 1) * RH], tmv(i, 2)[r, hs], tmv(i, 3)[r, hs],
                                         start=True, stop=False)
                        ins = nc.tensor.matmul(out[o, m * RH:(m + 1) * RH], tmv(i, 1)[r, hs], ua[r, m, 0:RH],
                                               start=False, stop=True)
                        if c:
                            ins = nc.tensor.matmul(out[o, 256 + m * RH:256 + (m + 1) * RH], ua[r, m, RH:P],
                                                   tmv(i, 1)[r, hs], start=True, stop=True)
                ins.then_inc(banks.full_sem(("KB", c)), 1)
            for i in range(NT):
                for par in range(2):
                    pe.wait_ge(*banks.emptied(("QB", i, par)))
                    pe.wait_ge(*banks.emptied(("QK", i, par)))
                pe.wait_ge(*banks.take(("RQ", i)))
                out = banks.bank(("RQ", i))
                for par in range(2):
                    for m in range(RM):
                        ins = nc.tensor.matmul(out[64 * par:64 * par + 64, m * P:(m + 1) * P], UA[i, par][:, m, RH:P],
                                               QB[i, par][:, m, :], start=True, stop=True)
                ins.then_inc(banks.full_sem(("RQ", i)), 1)
            for c in range(1, 4):
                pe.wait_ge(*banks.emptied(("KB", c)))
                if c == 1:
                    pe.wait_ge(*banks.emptied(("KB", 0)))
                else:
                    pe.wait_ge(sem("state_ready"), c - 1)
                for par in range(2):
                    r = slice(64 * par, 64 * par + 64)
                    pe.wait_ge(*banks.take(("S", c, par)))
                    out = banks.bank(("S", c, par))
                    for m in range(RM):
                        ins = nc.tensor.matmul(out[r, m * RH:(m + 1) * RH], GT[r, c - 1, m, :], S[r, c - 1, m, :],
                                               start=True, stop=True)
                    ins.then_inc(banks.full_sem(("S", c, par)), 1)
            for i in range(NT):
                pe.wait_ge(*banks.emptied(("RQ", i)))
            pe.wait_ge(sem("state_ready"), 3)
            for i, par in GROUPS:
                r = slice(64 * par, 64 * par + 64)
                pe.wait_ge(*banks.take(("O", i, par)))
                out = banks.bank(("O", i, par))
                for m in range(RM):
                    hs = slice((2 * m + par) * RH, (2 * m + par + 1) * RH)
                    cs = slice(m * RH, (m + 1) * RH)
                    nc.tensor.matmul(out[:, cs], QK[i, par][:, m, :], tmv(i, 3)[:, hs], start=True, stop=False)
                    nc.tensor.matmul(out[:, cs], QB[i, par][:, m, :], UA[i, par][:, m, 0:RH], start=False, stop=True)
                    for c in range(2):
                        ins = nc.tensor.matmul(out[64 * c:64 * c + 64, cs], RQT[r, m, i, 64 * c:64 * c + 64],
                                               S[r, 2 * i + c, m, :], start=False, stop=True, skip_group_check=True)
                ins.then_inc(banks.full_sem(("O", i, par)), 1)
            pe.wait_ge(sem("rwkv_gated"), 1)
            for i in range(NT):
                pe.wait_ge(*banks.take(("oT", i)))
                out = banks.bank(("oT", i))
                for m in range(RM):
                    ins = nc.tensor.transpose(out[:, m * P:(m + 1) * P], otm[:, i * 8 + 2 * m:i * 8 + 2 * m + 2, :].rearrange("p a b -> p (a b)"), ident)
                ins.then_inc(banks.full_sem(("oT", i)), 1)
            for i in range(NT):
                pe.wait_ge(*banks.emptied(("oT", i)))
            branch_out(pe, "rwkv_out", oT)
            pe.wait_ge(sem("mix_ready"), KC)
            tm_out(pe, "w_o", [gates[:, f, :] for f in range(KC)])

        def tmv(i, q):
            return tmm[0:META, q, :] if i == "meta" else tm[:, i * 4 + q, :]

        def level_bufs(g, n_g):
            n = META if g[0] == "meta" else P
            mtl = mm[g, "MTl"] if g[0] == "meta" else MTl4[n_g]
            return mtl[0:n], Tm[g][0:n], Wm[g][0:n], Ym[g][0:n]

        def branch_out(pe, name, x):
            for j in range(4):
                pe.wait_ge(*landed((name, j)))
                w = slot((name, j))
                for s in range(2):
                    pe.wait_ge(*banks.take((name, 2 * j + s)))
                    out = banks.bank((name, 2 * j + s))
                    for c in range(4):
                        at = (s * 4 + c) * P
                        ins = nc.tensor.matmul(out[:, 0:TOK], w[:, at:at + P], x[:, c, :], start=c == 0, stop=c == 3)
                    ins.then_inc(banks.full_sem((name, 2 * j + s)), 1)
                last_use((name, 2 * j + 1))

        def tm_out(pe, name, x, width=D):
            outs = {}
            for kc in range(KC):
                pe.wait_ge(*landed((name, kc)))
                w = slot((name, kc))
                for i in range(NT):
                    for half in range((width + 511) // 512):
                        if kc == 0:
                            pe.wait_ge(*banks.take((name, i, half)))
                            outs[i, half] = banks.bank((name, i, half))
                        hw = min(512, width - 512 * half)
                        ins = nc.tensor.matmul(outs[i, half][:, 0:hw], x[kc][:, i * P:(i + 1) * P],
                                               w[:, 512 * half:512 * half + hw], start=kc == 0, stop=kc == KC - 1)
                        if kc == KC - 1:
                            ins.then_inc(banks.full_sem((name, i, half)), 1)
                if kc < KC - 1:
                    ins.then_inc(sem("blocks_used"), 1)
                    last_use_here()
                else:
                    last_use((name, i, half))

        def one_scalar(act):
            act.wait_ge(sem("const_in"), 16)
            act.wait_ge(sem("cols_in"), 16)
            act.wait_ge(sem("small_zero"), 1)
            for i in range(NT):
                act.wait_ge(sem(f"h_in_{i}"), 16)
                ins = nc.scalar.activation(hsq[:, :], h[:, i, :], ACT.Square, accum_out=small[:, i:i + 1])
                ins.then_inc(sem("act_step"), 1)
                act.wait_ge(sem("act_step"), i + 1)
            act.wait_ge(sem("meta_in"), 16)
            nc.scalar.activation(hsq[0:META, :], hmeta[0:META, :], ACT.Square,
                                 accum_out=small[0:META, 2:3]).then_inc(sem("in_squares"), 1)
            act.wait_ge(sem("in_rstd"), 1)
            nc.scalar.activation(small[:, 3:6], small[:, 3:6], ACT.Sqrt).then_inc(sem("in_rstd"), 1)
            act.wait_ge(sem("in_rstd"), 2)
            for i in range(NT):
                ins = nc.scalar.activation(hn[:, i, :], h[:, i, :], ACT.Copy, scale=small[:, 3 + i:4 + i])
                ins.then_inc(sem("hn_ready"), 1)
            ins = nc.scalar.activation(hmeta[0:META, :], hmeta[0:META, :], ACT.Copy, scale=small[0:META, 5:6])
            ins.then_inc(sem("hn_ready"), 1)
            for kc in range(KC):
                act.wait_ge(*banks.full(("xT", kc)))
                out = banks.bank(("xT", kc))
                ins = nc.scalar.activation(xT[:, kc, :], out[:, 0:TALL], ACT.Copy, scale=col("g_mix", kc))
                ins.then_inc(banks.emptied_sem(("xT", kc)), 1)
            for c in range(CT):
                act.wait_ge(*banks.full(("gate", c)))
                out = banks.bank(("gate", c))
                ins = nc.scalar.activation(sgate[:, c, :], out[:, 0:TALL], ACT.Sigmoid)
                ins.then_inc(banks.emptied_sem(("gate", c)), 1)
            for j in range(14):
                act.wait_ge(*banks.full(("z", j)))
                out = banks.bank(("z", j))
                ins = nc.scalar.activation(z[:, j, 1:TALL + 1], out[:, 0:TALL], ACT.Copy)
                ins.then_inc(banks.emptied_sem(("z", j)), 1)
            for j in range(4):
                gate_in(act, j)
            act.wait_ge(*banks.emptied("conv_sum"))
            nc.scalar.activation(sq[:, :, :], ycv[:, :, :], ACT.Square).then_inc(sem("conv_sq"), 1)
            act.wait_ge(sem("shifted"), 14)
            nc.scalar.activation(zs[0:64, 12, :], zs[0:64, 12, :], ACT.Tanh).then_inc(sem("lora_in"), 1)
            nc.scalar.activation(zs[:, 13, META:TALL], zs[:, 13, META:TALL], ACT.Sigmoid).then_inc(sem("lora_in"), 1)
            for m in range(RM):
                act.wait_ge(*banks.full(("decay", m)))
                out = banks.bank(("decay", m))
                ins = nc.scalar.activation(sg[:, m, :], out[:, 0:TALL], ACT.Sigmoid, bias=col("w0", m))
                ins.then_inc(banks.emptied_sem(("decay", m)), 1)
                act.wait_ge(*banks.full(("a", m)))
                out = banks.bank(("a", m))
                ins = nc.scalar.activation(av[:, m, :], out[:, 0:TALL], ACT.Sigmoid, bias=col("a0", m))
                ins.then_inc(banks.emptied_sem(("a", m)), 1)
            for i in range(NT):
                act.wait_ge(*banks.full(("g", i)))
                out = banks.bank(("g", i))
                nc.scalar.activation(gtm[:, i, :], out[:, :], ACT.Copy).then_inc(banks.emptied_sem(("g", i)), 1)
            act.wait_ge(sem("conv_rstd"), 1)
            nc.scalar.activation(sq[:, 0, :], sq[:, 0, :], ACT.Sqrt).then_inc(sem("conv_rstd"), 1)
            act.wait_ge(sem("kk_norm"), 1)
            nc.scalar.activation(E2[:, :, :], E2[:, :, :], ACT.Sqrt).then_inc(sem("kk_norm"), 1)
            act.wait_ge(sem("conv_normal"), 1)
            for c in range(CT):
                nc.scalar.activation(ycv[:, c, :], ycv[:, c, :], ACT.Silu, scale=col("conv_ln_g", c),
                                     bias=col("conv_ln_b", c)).then_inc(sem("conv_out_in"), 1)
            act.wait_ge(sem("cum_ready"), 1)
            act.wait_ge(sem("kk_ready"), 1)
            nc.scalar.activation(E1[:, :, :], cum[:, :, :], ACT.Exp, scale=-DECAY).then_inc(sem("decays"), 1)
            nc.scalar.activation(E2[:, :, :], cum[:, :, :], ACT.Exp, scale=DECAY).then_inc(sem("decays"), 1)
            nc.scalar.activation(E3[:, :, :], sg[:, :, :], ACT.Exp, scale=-DECAY).then_inc(sem("decays"), 1)
            for j in range(4, 16):
                gate_in(act, j)
            for i in (0, 1, "meta"):
                for q in range(4):
                    act.wait_ge(*banks.full(("tm", i, q)))
                    out = banks.bank(("tm", i, q))
                    n = META if i == "meta" else P
                    ins = nc.scalar.activation(tmv(i, q), out[0:n, :], ACT.Copy)
                    ins.then_inc(banks.emptied_sem(("tm", i, q)), 1)
            for lev in range(LEVELS):
                for n_g, g in enumerate(ALLG):
                    n = META if g[0] == "meta" else P
                    act.wait_ge(*banks.full(("Y", lev, g)))
                    out = banks.bank(("Y", lev, g))
                    nc.scalar.activation(Ym[g][0:n], out[0:n, 0:4 * n].rearrange("p (a b) -> p a b", a=4),
                                         ACT.Copy).then_inc(banks.emptied_sem(("Y", lev, g)), 1)
            for g in ALLG:
                n = META if g[0] == "meta" else P
                act.wait_ge(*banks.full(("NV", g)))
                out = banks.bank(("NV", g))
                nc.scalar.activation(NV[g][0:n], out[0:n, 0:256].rearrange("p (a b) -> p a b", a=4),
                                     ACT.Copy).then_inc(banks.emptied_sem(("NV", g)), 1)
            for g in ALLG:
                n = META if g[0] == "meta" else P
                act.wait_ge(*banks.full(("UA", g)))
                out = banks.bank(("UA", g))
                nc.scalar.activation(UA[g][0:n], out[0:n, :].rearrange("p (a b) -> p a b", a=4),
                                     ACT.Copy).then_inc(banks.emptied_sem(("UA", g)), 1)
            for i, par in GROUPS:
                act.wait_ge(*banks.full(("O", i, par)))
                out = banks.bank(("O", i, par))
                to = otm[:, i * 8:(i + 1) * 8, :].rearrange("p (m two) v -> p m two v", two=2)[:, :, par, :]
                ins = nc.scalar.activation(to, out[:, 0:256].rearrange("p (a b) -> p a b", a=4), ACT.Copy)
                ins.then_inc(banks.emptied_sem(("O", i, par)), 1)
            act.wait_ge(sem("gn_rstd"), 1)
            nc.scalar.activation(small[:, 16:32], small[:, 16:32], ACT.Sqrt).then_inc(sem("gn_rstd"), 1)
            for i in range(NT):
                act.wait_ge(*banks.full(("oT", i)))
                out = banks.bank(("oT", i))
                nc.scalar.activation(oT[:, :, i * P:(i + 1) * P], out[:, :].rearrange("p (a b) -> p a b", a=4),
                                     ACT.Copy).then_inc(banks.emptied_sem(("oT", i)), 1)

        def gate_in(act, j):
            act.wait_ge(*banks.full(("ab", j)))
            out = banks.bank(("ab", j))
            nc.scalar.activation(gates[:, j, :], out[:, 0:TOK], ACT.Sigmoid).then_inc(banks.emptied_sem(("ab", j)), 1)

        def one_vector(v):
            V = nc.vector
            v.wait_ge(sem("const_in"), 16)
            v.wait_ge(sem("cols_in"), 16)
            v.wait_ge(sem("l1const_in"), 16)
            for b in range(NB):
                V.memset(cum[:, 0, b:b + 1], 0.0).then_inc(sem(f"emptied_{b}"), 1)
            V.memset(small[:, :], 0.0).then_inc(sem("small_zero"), 1)
            v.wait_ge(sem("small_zero"), 1)
            V.memset(z[:, :, 0:1], 0.0).then_inc(sem("zeros"), 1)
            V.memset(u[:, :, 0:TAPS - 1], 0.0).then_inc(sem("zeros"), 1)
            v.wait_ge(sem("in_squares"), 1)
            ins = V.tensor_scalar(small[:, 3:6], small[:, 0:3], 1.0 / D, 1e-6, ALU.mult, ALU.add)
            ins.then_inc(sem("dve_step"), 1)
            v.wait_ge(sem("dve_step"), count("dve_step"))
            V.reciprocal(small[:, 3:6], small[:, 3:6]).then_inc(sem("in_rstd"), 1)
            for m in range(RM):
                ins = V.tensor_scalar(rksel[:, m, :], onehead[:, m, :], col("r_k", m), None, ALU.mult)
            ins.then_inc(sem("rksel_ready"), 1)
            v.wait_ge(sem("zeros"), 2)
            for c in range(CT):
                v.wait_ge(*banks.emptied(("gate", c)))
                v.wait_ge(*banks.full(("val", c)))
                out = banks.bank(("val", c))
                ins = V.tensor_tensor(u[:, c, TAPS - 1:], out[:, 0:TALL], sgate[:, c, :], ALU.mult)
                ins.then_inc(banks.emptied_sem(("val", c)), 1)
            w0 = COLS["conv_w"][0]
            for c in range(CT):
                v.wait_ge(*banks.emptied(("val", c)))
                V.tensor_scalar(ycv[:, c, :], u[:, c, META:META + TOK], cols[:, w0 + c:w0 + c + 1],
                                col("conv_b", c), ALU.mult, ALU.add).then_inc(sem("conv_tap"), 1)
            with v.Fori(1, TAPS) as tap:
                for c in range(CT):
                    v.wait_ge(sem("conv_tap"), tap * CT - (CT - 1 - c))
                    V.scalar_tensor_tensor(ycv[:, c, :], u[:, c, bass.ds(tap + META, TOK)],
                                           cols[:, bass.ds(tap * CT + (w0 + c), 1)], ycv[:, c, :],
                                           ALU.mult, ALU.add).then_inc(sem("conv_tap"), 1)
            v.wait_ge(sem("conv_tap"), CT * TAPS)
            v.wait_ge(*banks.full("conv_sum"))
            out = banks.bank("conv_sum")
            ins = V.scalar_tensor_tensor(ycv[:, :, :], bc(out[:, 0:TOK], (0, CT), (1, TOK)), -1.0 / CONV_C,
                                         ycv[:, :, :], ALU.mult, ALU.add)
            ins.then_inc(banks.emptied_sem("conv_sum"), 1)
            for j in range(14):
                v.wait_ge(*banks.emptied(("z", j)))
            ins = V.tensor_tensor(zs[:, :, :], z[:, :, 0:TALL], z[:, :, 1:TALL + 1], ALU.subtract)
            ins.then_inc(sem("dve_step"), 1)
            v.wait_ge(sem("dve_step"), count("dve_step"))
            for j in range(14):
                V.scalar_tensor_tensor(zs[:, j, :], zs[:, j, :], col("mu", j), z[:, j, 1:TALL + 1],
                                       ALU.mult, ALU.add).then_inc(sem("shifted"), 1)
            v.wait_ge(sem("shifted"), 14)
            for m in range(RM):
                ins = V.tensor_scalar(kk[:, m, :], zs[:, 4 + m, :], col("k_k", m), None, ALU.mult)
                ins.then_inc(sem("dve_step"), 1)
                v.wait_ge(sem("dve_step"), count("dve_step"))
            V.tensor_tensor(E1[:, :, :], kk[:, :, :], kk[:, :, :], ALU.mult).then_inc(sem("kk_sq"), 1)
            v.wait_ge(*banks.full("conv_var"))
            out = banks.bank("conv_var")
            ins = V.tensor_scalar(sq[:, 0, :], out[:, 0:TOK], 1.0 / CONV_C, 1e-5, ALU.mult, ALU.add)
            ins.then_inc(banks.emptied_sem("conv_var"), 1)
            v.wait_ge(*banks.emptied("conv_var"))
            V.reciprocal(sq[:, 0, :], sq[:, 0, :]).then_inc(sem("conv_rstd"), 1)
            for m in range(RM):
                v.wait_ge(*banks.full(("kk_sum", m)))
                out = banks.bank(("kk_sum", m))
                ins = V.tensor_scalar(E2[:, m, :], out[:, 0:TALL], 1e-24, None, ALU.max)
                ins.then_inc(banks.emptied_sem(("kk_sum", m)), 1)
            for m in range(RM):
                v.wait_ge(*banks.emptied(("kk_sum", m)))
            V.reciprocal(E2[:, :, :], E2[:, :, :]).then_inc(sem("kk_norm"), 1)
            for m in range(RM):
                v.wait_ge(*banks.emptied(("decay", m)))
                v.wait_ge(*banks.emptied(("a", m)))
                ins = V.tensor_tensor_scan(cum[:, m, :], k("scan_all"), sg[:, m, :], 0.0, ALU.mult, ALU.add)
                ins.then_inc(sem("dve_step"), 1)
                v.wait_ge(sem("dve_step"), count("dve_step"))
            V.tensor_tensor(sg[:, :, :], cum[:, :, :], sg[:, :, :], ALU.subtract).then_inc(sem("cum_ready"), 1)
            v.wait_ge(sem("conv_rstd"), 2)
            ins = V.tensor_tensor(ycv[:, :, :], ycv[:, :, :], bc(sq[:, 0, :], (0, CT), (1, TOK)), ALU.mult)
            ins.then_inc(sem("conv_normal"), 1)
            for m in range(RM):
                ins = V.tensor_scalar(kp[:, m, :], av[:, m, :], -1.0, col("k_a", m), ALU.add, ALU.mult)
                ins.then_inc(sem("dve_step"), 1)
                v.wait_ge(sem("dve_step"), count("dve_step"))
            ins = V.scalar_tensor_tensor(kp[:, :, :], kp[:, :, :], 1.0, zs[:, 4:8, :], ALU.add, ALU.mult)
            ins.then_inc(sem("dve_step"), 1)
            v.wait_ge(sem("dve_step"), count("dve_step"))
            V.tensor_tensor(tt[:, :, :], kp[:, :, :], zs[:, 0:4, :], ALU.mult).then_inc(sem("rkr_ready"), 1)
            v.wait_ge(sem("kk_norm"), 2)
            V.tensor_tensor(kk[:, :, :], kk[:, :, :], E2[:, :, :], ALU.mult).then_inc(sem("kk_ready"), 1)
            v.wait_ge(sem("kk_ready"), 1)
            V.tensor_tensor(av[:, :, :], av[:, :, :], kk[:, :, :], ALU.mult).then_inc(sem("dve_step"), 1)
            v.wait_ge(sem("dve_step"), count("dve_step"))
            v.wait_ge(sem("decays"), 3)
            V.tensor_tensor(alpha[:, :, :], kk[:, :, :], E3[:, :, :], ALU.mult)
            V.scalar_tensor_tensor(beta[:, :, :], av[:, :, :], -1.0, E2[:, :, :], ALU.mult, ALU.mult)
            V.tensor_tensor(kappa[:, :, :], kp[:, :, :], E2[:, :, :], ALU.mult)
            V.tensor_tensor(rho[:, :, :], zs[:, 0:4, :], E1[:, :, :], ALU.mult).then_inc(sem("dve_step"), 1)
            v.wait_ge(sem("dve_step"), count("dve_step"))
            for c in range(5):
                at = META - 1 + c * CH
                ins = V.tensor_copy(pend[:, c, :], E1[:, :, at])
            ins.then_inc(sem("abkr_ready"), 1)
            branch_in(v, "conv_out", 0)
            for i in range(NT):
                v.wait_ge(*banks.full(("bonus", i)))
                out = banks.bank(("bonus", i))
                ins = V.tensor_copy(small[:, 32 + 8 * i:40 + 8 * i], out[:, 0:8])
                ins.then_inc(banks.emptied_sem(("bonus", i)), 1)
            for n_g, g in enumerate(ALLG):
                n = META if g[0] == "meta" else P
                for name, to, mask in (("MT", MT, "strict"), ("NT", NTm, "strict"), ("QK", QK, "incl"), ("QB", QB, "incl")):
                    if g[0] == "meta" and name[0] == "Q":
                        continue
                    v.wait_ge(*banks.full((name, *g)))
                    out = banks.bank((name, *g))
                    ins = V.tensor_tensor(to[g][0:n], out[0:n, 0:4 * n].rearrange("p (a b) -> p a b", a=4),
                                          bc(k(mask)[0:n, 0:n], (0, 4), (1, n)), ALU.mult)
                    ins.then_inc(banks.emptied_sem((name, *g)), 1)
                for t in (Tm, Wm):
                    V.tensor_copy(t[g][0:n], bc(ident[0:n, 0:n], (0, 4), (1, n))).then_inc(sem("t_ready"), 1)
            for lev in range(LEVELS):
                for g in ALLG:
                    n = META if g[0] == "meta" else P
                    for name, t in (("X", Tm), ("XT", Wm)):
                        v.wait_ge(*banks.full((name, lev, g)))
                        out = banks.bank((name, lev, g))
                        if lev == 0:
                            v.wait_ge(sem("t_ready"), 2 * len(ALLG))
                        else:
                            v.wait_ge(*banks.emptied((name, lev - 1, g)))
                        ins = V.tensor_tensor(t[g][0:n], t[g][0:n], out[0:n, 0:4 * n].rearrange("p (a b) -> p a b", a=4),
                                              ALU.add)
                        ins.then_inc(banks.emptied_sem((name, lev, g)), 1)
            v.wait_ge(*banks.full(("KB", 0)))
            out = banks.bank(("KB", 0))
            ins = V.tensor_tensor(S[:, 0, :, :], out[:, 0:256].rearrange("p (a b) -> p a b", a=4),
                                  bc(pend[:, 0, :], (1, 4), (0, RH)), ALU.mult)
            ins.then_inc(banks.emptied_sem(("KB", 0)), 1)
            for c in range(1, 4):
                v.wait_ge(*banks.full(("KB", c)))
                out = banks.bank(("KB", c))
                ins = V.tensor_copy(KB[:, c, :, :], out[:, 0:256].rearrange("p (a b) -> p a b", a=4))
                ins.then_inc(banks.emptied_sem(("KB", c)), 1)
                ins = V.tensor_tensor(GT[:, c - 1, :, :], out[:, 256:512].rearrange("p (a b) -> p a b", a=4),
                                      bc(k("ident2"), (0, 4), (1, 64)), ALU.add)
                ins.then_inc(banks.emptied_sem(("KB", c)), 1)
            for i in range(NT):
                v.wait_ge(*banks.full(("RQ", i)))
                out = banks.bank(("RQ", i))
                ins = V.tensor_tensor(RQT[:, :, i, :], out[:, :].rearrange("p (a b) -> p a b", a=4),
                                      rho[:, :, META + i * P:META + (i + 1) * P], ALU.add)
                ins.then_inc(banks.emptied_sem(("RQ", i)), 1)
            for c in range(1, 4):
                v.wait_ge(*banks.emptied(("KB", c)))
                for par in range(2):
                    r = slice(64 * par, 64 * par + 64)
                    v.wait_ge(*banks.full(("S", c, par)))
                    out = banks.bank(("S", c, par))
                    ins = V.tensor_tensor(S[r, c, :, :], out[r, 0:256].rearrange("p (a b) -> p a b", a=4), KB[r, c, :, :],
                                          ALU.add)
                    ins.then_inc(banks.emptied_sem(("S", c, par)), 1)
                    v.wait_ge(*banks.emptied(("S", c, par)))
                ins = V.tensor_tensor(S[:, c, :, :], S[:, c, :, :], bc(pend[:, c, :], (1, 4), (0, RH)), ALU.mult)
                ins.then_inc(sem("state_ready"), 1)
            for i, par in GROUPS:
                v.wait_ge(*banks.emptied(("O", i, par)))
            V.tensor_reduce(small[:, 16:32], otm[:, :, :], AX.X, ALU.add).then_inc(sem("dve_step"), 1)
            v.wait_ge(sem("dve_step"), count("dve_step"))
            V.tensor_scalar(small[:, 16:32], small[:, 16:32], 1.0 / RH, None, ALU.mult).then_inc(sem("dve_step"), 1)
            v.wait_ge(sem("dve_step"), count("dve_step"))
            ins = V.tensor_tensor(otm[:, :, :], otm[:, :, :], bc(small[:, 16:32], (1, 16), (0, RH)), ALU.subtract)
            ins.then_inc(sem("dve_step"), 1)
            v.wait_ge(sem("dve_step"), count("dve_step"))
            V.tensor_tensor(otmp[:, :, :], otm[:, :, :], otm[:, :, :], ALU.mult).then_inc(sem("dve_step"), 1)
            v.wait_ge(sem("dve_step"), count("dve_step"))
            V.tensor_reduce(small[:, 16:32], otmp[:, :, :], AX.X, ALU.add).then_inc(sem("dve_step"), 1)
            v.wait_ge(sem("dve_step"), count("dve_step"))
            ins = V.tensor_scalar(small[:, 16:32], small[:, 16:32], 1.0 / RH, 64e-5, ALU.mult, ALU.add)
            ins.then_inc(sem("dve_step"), 1)
            v.wait_ge(sem("dve_step"), count("dve_step"))
            V.reciprocal(small[:, 16:32], small[:, 16:32]).then_inc(sem("gn_rstd"), 1)
            for i in range(NT):
                v.wait_ge(*banks.emptied(("bonus", i)))
            for i in range(NT):
                ins = V.tensor_tensor(otmp[:, i * 8:(i + 1) * 8, :], bc(tmv(i, 3), (64, 8), (1, 64)),
                                      bc(small[:, 32 + 8 * i:40 + 8 * i], (1, 8), (0, RH)), ALU.mult)
            ins.then_inc(sem("dve_step"), 1)
            v.wait_ge(sem("dve_step"), count("dve_step"))
            v.wait_ge(sem("gn_rstd"), 2)
            ins = V.tensor_tensor(otm[:, :, :], otm[:, :, :], bc(small[:, 16:32], (1, 16), (0, RH)), ALU.mult)
            ins.then_inc(sem("dve_step"), 1)
            v.wait_ge(sem("dve_step"), count("dve_step"))
            v.wait_ge(sem("rows_in_0"), 16)
            halves = otm.rearrange("p (i a) b -> p i (a b)", i=NT)
            ins = V.tensor_tensor(halves, halves, bc(rows[:, 0, 0:RW], (0, NT), (1, RW)), ALU.mult)
            ins.then_inc(sem("dve_step"), 1)
            v.wait_ge(sem("dve_step"), count("dve_step"))
            ins = V.tensor_tensor(halves, halves, bc(rows[:, 0, RW:2 * RW], (0, NT), (1, RW)), ALU.add)
            ins.then_inc(sem("dve_step"), 1)
            v.wait_ge(sem("dve_step"), count("dve_step"))
            V.tensor_tensor(otm[:, :, :], otm[:, :, :], otmp[:, :, :], ALU.add).then_inc(sem("dve_step"), 1)
            v.wait_ge(sem("dve_step"), count("dve_step"))
            V.tensor_tensor(halves, halves, gtm[:, :, :], ALU.mult).then_inc(sem("rwkv_gated"), 1)
            branch_in(v, "rwkv_out", 8)
            for f in range(KC):
                v.wait_ge(*banks.emptied(("rwkv_out", f)))
                ins = V.tensor_tensor(gates[:, f, :], gates[:, f, :], gates[:, 8 + f, :], ALU.add)
                ins.then_inc(sem("mix_ready"), 1)
            residual_in(v, "w_o")

        def branch_in(v, name, at):
            for f in range(KC):
                v.wait_ge(*banks.emptied(("ab", at + f)))
                v.wait_ge(*banks.full((name, f)))
                out = banks.bank((name, f))
                ins = nc.vector.tensor_tensor(gates[:, at + f, :], out[:, 0:TOK], gates[:, at + f, :], ALU.mult)
                ins.then_inc(banks.emptied_sem((name, f)), 1)

        def residual_in(v, name, alpha_=1.0):
            for i in range(NT):
                for half in range(2):
                    v.wait_ge(*banks.full((name, i, half)))
                    out = banks.bank((name, i, half))
                    hs = h[:, i, half * 512:(half + 1) * 512]
                    ins = nc.vector.scalar_tensor_tensor(hs, hs, alpha_, out[:, :], ALU.mult, ALU.add)
                    ins.then_inc(banks.emptied_sem((name, i, half)), 1)

        def one_gpsimd(pool):
            pool.wait_ge(sem("l1const_in"), 16)
            for lev in range(LEVELS):
                for n_g, g in enumerate(ALLG):
                    n = META if g[0] == "meta" else P
                    if lev == 0:
                        pool.wait_ge(*banks.emptied(("MT", *g)))
                    else:
                        pool.wait_ge(*banks.full(("Y", lev - 1, g)))
                    mtl = level_bufs(g, n_g)[0]
                    ins = nc.gpsimd.tensor_tensor(mtl, MT[g][0:n], bc(levels[0:n, lev, 0:n], (0, 4), (1, n)), ALU.mult)
                    ins.then_inc(sem("joins_ready"), 1)

        def one_sync(sp):
            sp.dma_start(const[:, :], io["const"][:, 0:NCONST_KEEP]).then_inc(sem("const_in"), 16)
            sp.dma_start(cols[:, :], io["cols"]).then_inc(sem("cols_in"), 16)
            x = io["x"].rearrange("(i p) d -> i p d", p=P)
            for i in range(NT):
                sp.dma_start(h[:, i, :], x[i]).then_inc(sem(f"h_in_{i}"), 16)
            sp.dma_start(hmeta[0:META, :], io["meta"]).then_inc(sem("meta_in"), 16)
            at = CONST["onehead"][0]
            l1 = arena_t[:, L1C:L1C + NCONST - at]
            sp.dma_start(l1, io["const"][:, at:NCONST]).then_inc(sem("l1const_in"), 16)
            sp.dma_start(rows[:, 0, :], io["gn_rows"].partition_broadcast(P)).then_inc(sem("rows_in_0"), 16)
            load_row(sp, 1, 0)

        def sums_of_squares(act, n, bias=None):
            for i in range(NT):
                kw = {} if bias is None else {"bias": small[:, bias + i:bias + i + 1]}
                ins = nc.scalar.activation(actjunk, h[:, i, :], ACT.Square, accum_out=small[:, i:i + 1], **kw)
                ins.then_inc(sem("squares"), 1)
                act.wait_ge(sem("squares"), n * NT + i + 1)

        def root(act, n):
            act.wait_ge(sem("norm_var"), 2 * n + 1)
            nc.scalar.activation(small[:, 2:4], small[:, 2:4], ACT.Sqrt).then_inc(sem("norm_var"), 1)

        def rms_vector(v, n, to, row):
            v.wait_ge(sem("squares"), NT * (n + 1))
            ins = nc.vector.tensor_scalar(small[:, 2:4], small[:, 0:2], 1.0 / D, 1e-6, ALU.mult, ALU.add)
            ins.then_inc(sem("dve_step"), 1)
            v.wait_ge(sem("dve_step"), count("dve_step"))
            nc.vector.reciprocal(small[:, 2:4], small[:, 2:4]).then_inc(sem("norm_var"), 1)
            v.wait_ge(sem("norm_var"), 2 * n + 2)
            for i in range(NT):
                ins = nc.vector.scalar_tensor_tensor(to[:, i, :], h[:, i, :], small[:, 2 + i:3 + i], row, ALU.mult, ALU.mult)
                ins.then_inc(sem("normed"), 1)

        def ln_vector(v, n, m):
            for i in range(NT):
                nc.vector.tensor_reduce(small[:, 4 + i:5 + i], h[:, i, :], AX.X, ALU.add).then_inc(sem("dve_step"), 1)
                v.wait_ge(sem("dve_step"), count("dve_step"))
            ins = nc.vector.tensor_scalar(small[:, 4:6], small[:, 4:6], -1.0 / D, None, ALU.mult)
            ins.then_inc(sem("ln_mean"), 1)
            v.wait_ge(sem("ln_mean"), m + 1)
            v.wait_ge(sem("squares"), NT * (n + 1))
            ins = nc.vector.tensor_scalar(small[:, 2:4], small[:, 0:2], 1.0 / D, 1e-5, ALU.mult, ALU.add)
            ins.then_inc(sem("dve_step"), 1)
            v.wait_ge(sem("dve_step"), count("dve_step"))
            nc.vector.reciprocal(small[:, 2:4], small[:, 2:4]).then_inc(sem("norm_var"), 1)
            for i in range(NT):
                ins = nc.vector.scalar_tensor_tensor(h[:, i, :], h[:, i, :], small[:, 4 + i:5 + i], rows[:, 1, :],
                                                     ALU.add, ALU.mult)
                ins.then_inc(sem("dve_step"), 1)
                v.wait_ge(sem("dve_step"), count("dve_step"))
            v.wait_ge(sem("norm_var"), 2 * n + 2)
            for i in range(NT):
                nc.vector.scalar_tensor_tensor(h[:, i, :], h[:, i, :], small[:, 2 + i:3 + i], rows[:, 0, :],
                                               ALU.mult, ALU.add).then_inc(sem("normed"), 1)

        def fm_tensor(pe, name, src, n):
            for i in range(NT):
                pe.wait_ge(sem("normed"), NT * n + i + 1)
                for half in range(2):
                    pe.wait_ge(*banks.take((name, i, half)))
                    out = banks.bank((name, i, half))
                    for j in range(4):
                        kc = 4 * half + j
                        ins = nc.tensor.transpose(out[:, j * P:(j + 1) * P], src[:, i, kc * P:(kc + 1) * P], ident)
                    ins.then_inc(banks.full_sem((name, i, half)), 1)
            for i in range(NT):
                for half in range(2):
                    pe.wait_ge(*banks.emptied((name, i, half)))

        def fm_scalar(act, name):
            for i in range(NT):
                for half in range(2):
                    act.wait_ge(*banks.full((name, i, half)))
                    out = banks.bank((name, i, half))
                    nc.scalar.activation(xT[:, 4 * half:4 * half + 4, i * P:(i + 1) * P],
                                         out[:, :].rearrange("p (a b) -> p a b", a=4), ACT.Copy).then_inc(banks.emptied_sem((name, i, half)), 1)

        UNITS = NT * PH
        G = Arena(arena_t, ARENA)
        ring_u, ring_v = G.take(RING, D), G.take(RING, D)
        scores = G.take((UNITS + 1) * 2 * NKEYS)
        qT = G.take(16, TOK)
        xn = G.take(NT, D)
        ysum = G.take(NT * D)
        actjunk = G.take(D)
        diag = G.take(PK, P)
        sc, sc2 = G.take(2, NKEYS), G.take(2, NKEYS)
        cand, cand2, eq = (G.take(PK, PK) for _ in range(3))
        top, topi, posf = (G.take(2, PK) for _ in range(3))
        best, expo, gate, dots, actv, coef, e1, e2 = (G.take(PK) for _ in range(8))
        tiny = G.take(4)

        def peer_scores_tensor(pe, n):
            for lo, hi in Q_GROUPS:
                for j in range(lo, hi):
                    fm_tile(pe, ("q", n, j), ("w_q", n, j), xT[:, :, 0:TOK], TOK)
                pe.wait_ge(*landed(("keys", n, lo)))
                w = slot(("keys", n, lo))
                for j in range(lo, hi):
                    pe.wait_ge(*banks.emptied(("q", n, j)))
                for i in range(NT):
                    pe.wait_ge(*banks.take(("score", n, lo, i)))
                    out = banks.bank(("score", n, lo, i))
                    for x in range(hi - lo):
                        ins = nc.tensor.matmul(out[:, x * P:(x + 1) * P], qT[:, lo + x, i * P:(i + 1) * P],
                                               w[:, x * P:(x + 1) * P], start=True, stop=True)
                    ins.then_inc(banks.full_sem(("score", n, lo, i)), 1)
                last_use(("score", n, lo, NT - 1))

        def peer_scores_scalar(act, n):
            for lo, hi in Q_GROUPS:
                for j in range(lo, hi):
                    act.wait_ge(*banks.full(("q", n, j)))
                    out = banks.bank(("q", n, j))
                    nc.scalar.activation(qT[:, j, :], out[:, 0:TOK], ACT.Copy).then_inc(
                        banks.emptied_sem(("q", n, j)), 1)
                for i in range(NT):
                    act.wait_ge(*banks.full(("score", n, lo, i)))
                    out = banks.bank(("score", n, lo, i))
                    at = i * PH * 2 * NKEYS + lo * NKEYS
                    nc.scalar.activation(scores[:, at:at + (hi - lo) * P], out[:, 0:(hi - lo) * P], ACT.Copy).then_inc(
                        banks.emptied_sem(("score", n, lo, i)), 1)
                if lo == 0:
                    act.wait_ge(*banks.emptied(("score", n, lo, 0)))
                    copy_scores(act, n, 0)
                if lo == 6:
                    softmax_exp(act, n * UNITS)
                    act.wait_ge(*banks.emptied(("score", n, 2, 0)))
                    copy_scores(act, n, 1)
            act.wait_ge(sem("pad_zero"), n + 1)
            for lo, hi in Q_GROUPS:
                for i in range(NT):
                    act.wait_ge(*banks.emptied(("score", n, lo, i)))

        def copy_scores(act, n, unit):
            if type(unit) is int and unit == 0:
                if n:
                    act.wait_ge(sem("sc_in"), n * (UNITS + 1))
            else:
                act.wait_ge(sem("sc_read"), unit + n * UNITS)
            nc.scalar.activation(sc[:, :, :], scores[:, bass.ds(unit * 2 * NKEYS, 2 * NKEYS)].rearrange(
                "p (a b) -> p a b", a=2), ACT.Copy).then_inc(sem("sc_in"), 1)

        class Steps:

            def __init__(self, base):
                self.base, self.n = base, 0

            def __call__(self):
                self.n += 1
                return self.base + self.n

        TOPK_STEPS = 25

        def topk_find(v, step, n, unit):
            V = nc.vector
            v.wait_ge(sem("sc_in"), unit + (n * (UNITS + 1) + 1))
            v.sem_inc(sem("waits_passed"), 1)
            for c in range(2):
                V.max(out=top[:, c, 0:8], in_=sc[:, c, :]).then_inc(sem("topk_step"), 1)
                v.wait_ge(sem("topk_step"), step())
                v.sem_inc(sem("waits_passed"), 1)
                ins = V.max_index(out=idx_best[:, c, 0:8], in_max=top[:, c, 0:8], in_values=sc[:, c, :])
                ins.then_inc(sem("topk_step"), 1)
                v.wait_ge(sem("topk_step"), step())
                v.sem_inc(sem("waits_passed"), 1)
                V.match_replace(out=sc2[:, c, :], in_to_replace=top[:, c, 0:8], in_values=sc[:, c, :],
                                imm_value=-3.0e38).then_inc(sem("topk_step"), 1)
                v.wait_ge(sem("topk_step"), step())
                v.sem_inc(sem("waits_passed"), 1)
                V.max(out=top[:, c, 8:16], in_=sc2[:, c, :]).then_inc(sem("topk_step"), 1)
                v.wait_ge(sem("topk_step"), step())
                v.sem_inc(sem("waits_passed"), 1)
                ins = V.max_index(out=idx_best[:, c, 8:16], in_max=top[:, c, 8:16], in_values=sc2[:, c, :])
                if c == 0:
                    ins.then_inc(sem("topk_step"), 1)
                    v.wait_ge(sem("topk_step"), step())
                    v.sem_inc(sem("waits_passed"), 1)
            ins.then_inc(sem("sc_read"), 1)
            v.wait_ge(sem("sc_read"), unit + (n * UNITS + 1))
            v.sem_inc(sem("waits_passed"), 1)
            V.tensor_copy(topi[:, :, :], idx_best[:, :, :])
            flat, flat2 = cand.rearrange("p a b -> p (a b)"), cand2.rearrange("p a b -> p (a b)")
            ins = V.tensor_tensor(cand[:, :, :], bc(top[:, 0, :], (1, PK), (0, PK)), bc(top[:, 1, :], (0, PK), (1, PK)), ALU.add)
            ins.then_inc(sem("topk_step"), 1)
            v.wait_ge(sem("topk_step"), step())
            v.sem_inc(sem("waits_passed"), 1)
            V.max(out=best[:, 0:8], in_=flat).then_inc(sem("topk_step"), 1)
            v.wait_ge(sem("topk_step"), step())
            v.sem_inc(sem("waits_passed"), 1)
            V.max_index(out=idx_pos[:, 0, 0:8], in_max=best[:, 0:8], in_values=flat).then_inc(sem("topk_step"), 1)
            v.wait_ge(sem("topk_step"), step())
            v.sem_inc(sem("waits_passed"), 1)
            ins = V.match_replace(out=flat2, in_to_replace=best[:, 0:8], in_values=flat, imm_value=-3.0e38)
            ins.then_inc(sem("topk_step"), 1)
            v.wait_ge(sem("topk_step"), step())
            v.sem_inc(sem("waits_passed"), 1)
            V.max(out=best[:, 8:16], in_=flat2).then_inc(sem("topk_step"), 1)
            v.wait_ge(sem("topk_step"), step())
            v.sem_inc(sem("waits_passed"), 1)
            V.max_index(out=idx_pos[:, 0, 8:16], in_max=best[:, 8:16], in_values=flat2).then_inc(sem("topk_step"), 1)
            v.wait_ge(sem("topk_step"), step())
            v.sem_inc(sem("waits_passed"), 1)
            V.tensor_scalar(tiny[:, 0:1], best[:, 0:1], -1.0, None, ALU.mult).then_inc(sem("best_found"), 1)

        def topk_numbers(v, step, n, unit):
            V = nc.vector
            V.tensor_scalar(idx_pos[:, 1, :], idx_pos[:, 0, :], 4, None, ALU.logical_shift_right)
            ins = V.tensor_scalar(idx_pos[:, 2, :], idx_pos[:, 0, :], 15, None, ALU.bitwise_and)
            ins.then_inc(sem("topk_step"), 1)
            v.wait_ge(sem("topk_step"), step())
            v.sem_inc(sem("waits_passed"), 1)
            V.tensor_copy(posf[:, :, :], idx_pos[:, 1:3, :]).then_inc(sem("topk_step"), 1)
            v.wait_ge(sem("topk_step"), step())
            v.sem_inc(sem("waits_passed"), 1)
            for c, e in ((0, e1), (1, e2)):
                V.tensor_tensor(eq[:, :, :], bc(posf[:, c, :], (1, PK), (0, PK)), bc(k("iota"), (0, PK), (1, PK)),
                                ALU.is_equal).then_inc(sem("topk_step"), 1)
                v.wait_ge(sem("topk_step"), step())
                v.sem_inc(sem("waits_passed"), 1)
                ins = V.tensor_tensor(eq[:, :, :], eq[:, :, :], bc(topi[:, c, :], (0, PK), (1, PK)), ALU.mult)
                ins.then_inc(sem("topk_step"), 1)
                v.wait_ge(sem("topk_step"), step())
                v.sem_inc(sem("waits_passed"), 1)
                V.tensor_reduce(e, eq[:, :, :], AX.X, ALU.add).then_inc(sem("topk_step"), 1)
                v.wait_ge(sem("topk_step"), step())
                v.sem_inc(sem("waits_passed"), 1)
            if type(unit) is not int or unit + n:
                v.wait_ge(sem("idx_taken"), unit + n * UNITS)
            V.scalar_tensor_tensor(idx_next[:, :], e1, float(NKEYS), e2, ALU.mult, ALU.add).then_inc(sem("topk_done"), 1)

        def topk_gate(v, step, n, unit):
            V = nc.vector
            v.wait_ge(sem("exp_done"), unit + (n * UNITS + 1))
            V.reciprocal(tiny[:, 2:3], tiny[:, 1:2]).then_inc(sem("topk_step"), 1)
            v.wait_ge(sem("topk_step"), step())
            v.sem_inc(sem("waits_passed"), 1)
            V.tensor_scalar(gate, expo, tiny[:, 2:3], None, ALU.mult).then_inc(sem("topk_step"), 1)
            v.wait_ge(sem("topk_step"), step())
            v.sem_inc(sem("waits_passed"), 1)

        def softmax_exp(act, topk_n):
            act.wait_ge(sem("best_found"), topk_n + 1)
            ins = nc.scalar.activation(expo, best, ACT.Exp, bias=tiny[:, 0:1], accum_out=tiny[:, 1:2])
            ins.then_inc(sem("exp_done"), 1)

        def peer_vector(v, n):
            V = nc.vector
            base = n * UNITS
            x = xn if n == 0 else h

            def dots_of(t, tile, lo, hi):
                for kx in range(lo, hi):
                    s = kx % RING
                    v.wait_ge(sem(f"u_landed_{s}"), (t + base) * 32 + 16 * (kx // RING + 1))
                    V.tensor_tensor_reduce(out=ring_u[:, s, :], in0=ring_u[:, s, :], in1=x[:, tile, :], scale=1.0,
                                           scalar=0.0, op0=ALU.mult, op1=ALU.add,
                                           accum_out=dots[:, kx:kx + 1]).then_inc(sem("u_free"), 1)

            def coefficients(t):
                v.wait_ge(sem("gelu_done"), t + (base + 1))
                if type(t) is not int or t + n:
                    v.wait_ge(sem("diag_ready"), (t + base) * PK)
                V.tensor_tensor(coef, actv, gate, ALU.mult).then_inc(sem("coef_ready"), 1)
                v.wait_ge(sem("coef_ready"), t + (base + 1))

            def add_sum(t, tile):
                v.wait_ge(sem("v_free"), (t + base) * PK + 2 * PK)
                for half, bank in enumerate((acc_lo, acc_hi)):
                    y = ysum[:, tile * D + half * 512:tile * D + half * 512 + 512]
                    if type(t) is not int or t + n:
                        v.wait_ge(sem("y_added"), (t + base) * 2 + (half + 1))
                    V.tensor_tensor(y, y, bank[:, :], ALU.add).then_inc(sem("y_added"), 1)

            def unit_step(t, x_tile, y_tile):
                step = Steps((t + (base + 1)) * TOPK_STEPS)
                topk_find(v, step, n, t + 1)
                dots_of(t, x_tile, 0, PK // 2)
                topk_numbers(v, step, n, t + 1)
                dots_of(t, x_tile, PK // 2, PK)
                coefficients(t)
                topk_gate(v, step, n, t + 1)
                if y_tile is not None:
                    add_sum(t - 1, y_tile)

            if n == 0:
                V.memset(tiny[:, 3:4], 0.0).then_inc(sem("u_free"), RING)
                V.memset(small[:, 6:7], 0.0).then_inc(sem("y_added"), 2)
            V.memset(scores[:, UNITS * 2 * NKEYS:], 0.0).then_inc(sem("pad_zero"), 1)
            V.memset(ysum[:, :], 0.0).then_inc(sem("y_zero"), 1)
            v.wait_ge(sem("y_zero"), n + 1)
            step = Steps(base * TOPK_STEPS)
            topk_find(v, step, n, 0)
            topk_numbers(v, step, n, 0)
            topk_gate(v, step, n, 0)
            assert step.n == TOPK_STEPS, step.n
            unit_step(0, 0, None)
            with v.Fori(1, PH) as t:
                unit_step(t, 0, 0)
            unit_step(PH, 1, 0)
            with v.Fori(PH + 1, UNITS - 1) as t:
                unit_step(t, 1, 1)
            dots_of(UNITS - 1, 1, 0, PK)
            coefficients(UNITS - 1)
            add_sum(UNITS - 2, 1)
            add_sum(UNITS - 1, 1)
            v.wait_ge(sem("y_added"), 2 * UNITS * (n + 1) + 2)

        def peer_scalar(act, n):
            base = n * UNITS

            def coefficients(t):
                act.wait_ge(sem("u_free"), (t + base) * PK + (PK + RING))
                nc.scalar.activation(actv, dots, ACT.Gelu).then_inc(sem("gelu_done"), 1)
                act.wait_ge(sem("coef_ready"), t + (base + 1))
                for kx in range(PK):
                    act.wait_ge(sem("v_free"), (t + base) * PK + (kx + 1))
                    ins = nc.scalar.activation(diag[:, kx, :], ident, ACT.Copy, scale=coef[:, kx:kx + 1])
                    ins.then_inc(sem("diag_ready"), 1)

            with act.Fori(0, UNITS - 1) as t:
                softmax_exp(act, t + (base + 1))
                copy_scores(act, n, t + 2)
                coefficients(t)
            coefficients(UNITS - 1)

        def peer_tensor(pe, n):
            base = n * UNITS
            with pe.Fori(0, UNITS) as t:
                pe.wait_ge(sem("y_added"), (t + base) * 2 + 2)
                for kx in range(PK):
                    s = kx % RING
                    pe.wait_ge(sem("diag_ready"), (t + base) * PK + (kx + 1))
                    pe.wait_ge(sem(f"v_landed_{s}"), (t + base) * 32 + 16 * (kx // RING + 1))
                    nc.tensor.matmul(acc_lo[:, :], diag[:, kx, :], ring_v[:, s, 0:512], start=kx == 0, stop=kx == PK - 1)
                    nc.tensor.matmul(acc_hi[:, :], diag[:, kx, :], ring_v[:, s, 512:1024], start=kx == 0,
                                     stop=kx == PK - 1).then_inc(sem("v_free"), 1)

        def peer_gpsimd(pool, n):
            base = n * UNITS

            def take_numbers(t, at):
                pool.wait_ge(sem("topk_done"), t + (base + 1))
                pool.sem_inc(sem("waits_passed"), 1)
                nc.gpsimd.tensor_copy(idx[:, at, :], idx_next[:, :]).then_inc(sem("idx_taken"), 1)
                pool.wait_ge(sem("idx_taken"), t + (base + 1))
                pool.sem_inc(sem("waits_passed"), 1)

            def gather(name, t, at, kx):
                table, ring = (io[f"u{n}"], ring_u) if name == "u" else (io[f"v{n}"], ring_v)
                s = kx % RING
                pool.wait_ge(sem(f"{name}_free"), (t + base) * PK + (kx + 1 + (PK - RING if name == "v" else 0)))
                pool.sem_inc(sem("waits_passed"), 1)
                nc.gpsimd.indirect_dma_start(out=ring[:, s, :], out_offset=None, in_=table,
                                             in_offset=bass.IndirectOffsetOnAxis(ap=idx[:, at, kx:kx + 1], axis=0)
                                             ).then_inc(sem(f"{name}_landed_{s}"), 16)

            if n == 0:
                nc.gpsimd.memset(idx[:, 1, :], 0).then_inc(sem("v_free"), PK)
            take_numbers(0, 0)
            for kx in range(PK):
                gather("u", 0, 0, kx)
            with pool.Fori(0, (UNITS - 1) // 3) as three:
                for at in range(3):
                    t = three * 3 + at
                    take_numbers(t + 1, (at + 1) % 3)
                    for kx in range(PK):
                        gather("u", t + 1, (at + 1) % 3, kx)
                        gather("v", t, at, kx)
            for kx in range(PK):
                gather("v", UNITS - 1, (UNITS - 1) % 3, kx)

        def load_row(sp, slot, which):
            sp.dma_start(rows[:, slot, :], io["rows"][which].partition_broadcast(P)).then_inc(sem(f"rows_in_{slot}"), 16)

        def residual_peer(v, alpha_):
            for i in range(NT):
                nc.vector.scalar_tensor_tensor(h[:, i, :], h[:, i, :], alpha_, ysum[:, i * D:(i + 1) * D], ALU.mult,
                                               ALU.add).then_inc(sem("peer_added"), 1)
            v.wait_ge(sem("peer_added"), count("peer_added", NT))

        T2 = Arena(arena_t, 29952)
        memT = T2.take(KC, 256)
        kmT = T2.take(2, 256)
        vm = T2.take(2, 256)
        cat = T2.take(KC, TOK)
        qf, kf = T2.take(6, TOK), T2.take(6, TOK)
        qm = T2.take(2, TOK)
        vt = T2.take(NT, 768)
        probs = T2.take(NT * MEM_H, 256)
        probsT = T2.take(NT * MEM_H * 2, P)
        two_at = T2.at
        rf = T2.take(6, TOK)
        glr = T2.take(TOK)
        gate2 = T2.take(384)
        lg, bsum, eb, enb, ke, tmp2 = (T2.take(12, CH) for _ in range(6))
        keT = T2.take(NT, 384)
        attn = T2.take(NT * 2, 3, P)
        states = T2.take(4, 3, P)
        rs = T2.take(6, TOK)
        T3 = Arena(arena_t, 29952)
        T3.at = two_at
        zb, lb, sp_ = (T3.take(4, 3 * P) for _ in range(3))
        att = T3.take(12, 3 * P)
        mask3 = T3.take(3 * P)

        def mem_kv_tensor(pe, n):
            pe.wait_ge(sem("memT_in"), 16 * (n + 1))
            for j in range(2):
                fm_tile(pe, ("mk", n, j), ("mem_k", n, j), memT, 256)
            outs = []
            for i in range(2):
                pe.wait_ge(*banks.take(("mv", n, i)))
                outs.append(banks.bank(("mv", n, i)))
            for j in range(2):
                pe.wait_ge(*landed(("mem_v", n, j)))
                w = slot(("mem_v", n, j))
                for i in range(2):
                    for x in range(4):
                        kc = 4 * j + x
                        ins = nc.tensor.matmul(outs[i][:, 0:256], memT[:, kc, i * P:(i + 1) * P],
                                               w[:, x * 256:(x + 1) * 256], start=kc == 0, stop=kc == KC - 1)
                    if j == 1:
                        ins.then_inc(banks.full_sem(("mv", n, i)), 1)
                if j == 0:
                    ins.then_inc(sem("blocks_used"), 1)
                    last_use_here()
                else:
                    last_use(("mv", n, 1))

        def mem_kv_scalar(act, n):
            for name, to in (("mk", kmT), ("mv", vm)):
                for j in range(2):
                    act.wait_ge(*banks.full((name, n, j)))
                    out = banks.bank((name, n, j))
                    ins = nc.scalar.activation(to[:, j, :], out[:, 0:256], ACT.Copy)
                    ins.then_inc(banks.emptied_sem((name, n, j)), 1)

        def memory_tensor(pe, n):
            for j in range(2):
                pe.wait_ge(*banks.emptied(("mk", n, j)))
                pe.wait_ge(*banks.emptied(("qm", n, j)))
                pe.wait_ge(*banks.emptied(("mv", n, j)))
            for i in range(NT):
                for par in range(2):
                    r = slice(64 * par, 64 * par + 64)
                    pe.wait_ge(*banks.take(("ms", n, i, par)))
                    out = banks.bank(("ms", n, i, par))
                    for j in range(2):
                        ins = nc.tensor.matmul(out[:, j * 256:(j + 1) * 256], qm[r, j, i * P:(i + 1) * P], kmT[r, j, :],
                                               start=True, stop=True)
                    ins.then_inc(banks.full_sem(("ms", n, i, par)), 1)

        def memory_values_tensor(pe, n):
            pe.wait_ge(sem("probs_ready"), n + 1)
            for i in range(NT):
                for par in range(2):
                    pe.wait_ge(*banks.take(("pT", n, i, par)))
                    out = banks.bank(("pT", n, i, par))
                    for x in range(4):
                        p_at = probs[:, (i * 2 + par) * 2 + x // 2, (x % 2) * P:(x % 2 + 1) * P]
                        ins = nc.tensor.transpose(out[:, x * P:(x + 1) * P], p_at, ident)
                    ins.then_inc(banks.full_sem(("pT", n, i, par)), 1)
            for i in range(NT):
                for par in range(2):
                    pe.wait_ge(*banks.emptied(("pT", n, i, par)))
            for i in range(NT):
                pe.wait_ge(*banks.take(("mo", n, i)))
                out = banks.bank(("mo", n, i))
                for par in range(2):
                    for j in range(2):
                        m = 2 * j + par
                        for mt in range(2):
                            ins = nc.tensor.matmul(out[64 * par:64 * par + 64, j * P:(j + 1) * P],
                                                   vm[:, mt, m * 64:(m + 1) * 64],
                                                   probsT[:, ((i * 2 + par) * 2 + j) * 2 + mt, :],
                                                   start=mt == 0, stop=mt == 1)
                ins.then_inc(banks.full_sem(("mo", n, i)), 1)

        def memory_max_vector(v, n):
            for i in range(NT):
                for par in range(2):
                    v.wait_ge(*banks.full(("ms", n, i, par)))
                    out = banks.bank(("ms", n, i, par))
                    at = 16 + 2 * (2 * i + par)
                    nc.vector.tensor_reduce(small[:, at:at + 2], out[:, :].rearrange("p (a b) -> p a b", a=2),
                                            AX.X, ALU.max).then_inc(sem("dve_step"), 1)
                    v.wait_ge(sem("dve_step"), count("dve_step"))
                    ins = nc.vector.tensor_scalar(small[:, at:at + 2], small[:, at:at + 2], -0.125, None, ALU.mult)
                    ins.then_inc(sem("mem_max"), 1)

        def memory_norm_vector(v, n):
            v.wait_ge(sem("mem_exp"), 8 * (n + 1))
            nc.vector.reciprocal(small[:, 24:32], small[:, 24:32]).then_inc(sem("dve_step"), 1)
            v.wait_ge(sem("dve_step"), count("dve_step"))
            ins = nc.vector.tensor_tensor(probs[:, :, :], probs[:, :, :], bc(small[:, 24:32], (1, 8), (0, 256)), ALU.mult)
            ins.then_inc(sem("probs_ready"), 1)

        def memory_exp_scalar(act, n):
            for i in range(NT):
                for par in range(2):
                    act.wait_ge(sem("mem_max"), 4 * n + 2 * i + par + 1)
                    act.wait_ge(*banks.full(("ms", n, i, par)))
                    out = banks.bank(("ms", n, i, par))
                    for j in range(2):
                        at = 2 * (2 * i + par) + j
                        ins = nc.scalar.activation(probs[:, at, :], out[:, j * 256:(j + 1) * 256], ACT.Exp, scale=0.125,
                                                   bias=small[:, 16 + at:17 + at], accum_out=small[:, 24 + at:25 + at])
                        if j == 0:
                            ins.then_inc(sem("mem_exp"), 1)
                    ins.then_inc(banks.emptied_sem(("ms", n, i, par)), 1)
            for i in range(NT):
                for par in range(2):
                    act.wait_ge(*banks.emptied(("ms", n, i, par)))
            nc.scalar.activation(small[:, 6:8], small[:, 6:8], ACT.Copy).then_inc(sem("mem_exp"), 4)

        def memory_out_scalar(act, n):
            for i in range(NT):
                for par in range(2):
                    act.wait_ge(*banks.full(("pT", n, i, par)))
                    out = banks.bank(("pT", n, i, par))
                    at = (i * 2 + par) * 4
                    nc.scalar.activation(probsT[:, at:at + 4, :], out[:, :].rearrange(
         "p (a b) -> p a b", a=4), ACT.Copy).then_inc(banks.emptied_sem(("pT", n, i, par)), 1)
            for i in range(NT):
                act.wait_ge(*banks.full(("mo", n, i)))
                out = banks.bank(("mo", n, i))
                nc.scalar.activation(cat[:, 6:8, i * P:(i + 1) * P], out[:, 0:256].rearrange(
     "p (a b) -> p a b", a=2), ACT.Copy).then_inc(banks.emptied_sem(("mo", n, i)), 1)

        def two_tensor(pe):
            mem_kv_tensor(pe, 0)
            pe.wait_ge(*landed("glr"))
            w = slot("glr")
            pe.wait_ge(*banks.take("glr"))
            out = banks.bank("glr")
            for kc in range(KC):
                ins = nc.tensor.matmul(out[0:16, 0:TOK], w[:, kc * 16:(kc + 1) * 16], xT[:, kc, 0:TOK],
                                       start=kc == 0, stop=kc == KC - 1)
            ins.then_inc(banks.full_sem("glr"), 1)
            last_use("glr")
            x = xT[:, :, 0:TOK]
            fm_tile(pe, ("q2", 0), ("a_q", 0), x, TOK)
            pe.wait_ge(*banks.emptied("glr"))
            pe.wait_ge(sem("gate2_in"), 16)
            for j in range(3):
                pe.wait_ge(*banks.take(("lg", j)))
                out = banks.bank(("lg", j))
                nc.tensor.matmul(out[:, 0:TOK], gate2[0:16, j * P:(j + 1) * P], glr[0:16, :],
                                 start=True, stop=True).then_inc(banks.full_sem(("lg", j)), 1)
            fm_tile(pe, ("k2", 0), ("a_k", 0), x, TOK)
            for j in range(1, 3):
                fm_tile(pe, ("q2", j), ("a_q", j), x, TOK)
                fm_tile(pe, ("k2", j), ("a_k", j), x, TOK)
            tm_out(pe, "a_v", [xT[:, kc, 0:TOK] for kc in range(KC)], 768)
            for j in range(6):
                fm_tile(pe, ("r2", j), ("a_r", j), x, TOK)
            for j in range(2):
                fm_tile(pe, ("qm", 0, j), ("a_qm", j), x, TOK)
            memory_tensor(pe, 0)
            pe.wait_ge(sem("ke_ready"), 1)
            for i in range(NT):
                pe.wait_ge(*banks.take(("keT", i)))
                out = banks.bank(("keT", i))
                for j in range(3):
                    ins = nc.tensor.transpose(out[:, j * P:(j + 1) * P],
                                              ke[:, 4 * j + 2 * i:4 * j + 2 * i + 2, :].rearrange("p a b -> p (a b)"), ident)
                ins.then_inc(banks.full_sem(("keT", i)), 1)
            for i in range(NT):
                for par in range(2):
                    r = slice(64 * par, 64 * par + 64)
                    pe.wait_ge(*banks.take(("attn", i, par)))
                    out = banks.bank(("attn", i, par))
                    for j in range(3):
                        ins = nc.tensor.matmul(out[:, j * P:(j + 1) * P], kf[r, j, i * P:(i + 1) * P],
                                               qf[r, j, i * P:(i + 1) * P], start=True, stop=True)
                    ins.then_inc(banks.full_sem(("attn", i, par)), 1)
            for i in range(NT):
                pe.wait_ge(*banks.emptied(("keT", i)))
                for half in range(2):
                    pe.wait_ge(*banks.emptied(("a_v", i, half)))
            for c in range(3):
                r = slice(64 * (c % 2), 64 * (c % 2) + 64)
                pe.wait_ge(*banks.take(("du", c), 3))
                out = banks.bank(("du", c))
                for par in range(2):
                    for j in range(3):
                        hd = 2 * j + par
                        ins = nc.tensor.matmul(out[64 * par:64 * par + 64, j * P:(j + 1) * P],
                                               keT[r, c // 2, hd * 64:(hd + 1) * 64], vt[r, c // 2, hd * P:(hd + 1) * P],
                                               start=True, stop=True)
                ins.then_inc(banks.full_sem(("du", c)), 1)
            memory_values_tensor(pe, 0)
            for c in range(3):
                pe.wait_ge(*banks.emptied(("du", c)))
            for i in range(NT):
                for par in range(2):
                    r = slice(64 * par, 64 * par + 64)
                    pe.wait_ge(*banks.emptied(("attn", i, par)))
                    pe.wait_ge(*banks.take(("o2", i, par)))
                    out = banks.bank(("o2", i, par))
                    for j in range(3):
                        hd = 2 * j + par
                        ins = nc.tensor.matmul(out[:, j * P:(j + 1) * P], vt[:, i, hd * P:(hd + 1) * P],
                                               attn[:, 2 * i + par, j, :], start=True, stop=True)
                        for c in range(2):
                            if 2 * i + c:
                                at = i * P + c * CH
                                ins = nc.tensor.matmul(out[:, j * P + c * CH:j * P + (c + 1) * CH],
                                                       states[r, 2 * i + c, j, :], qf[r, j, at:at + CH],
                                                       start=False, stop=True, skip_group_check=True)
                    ins.then_inc(banks.full_sem(("o2", i, par)), 1)
            pe.wait_ge(sem("o_squares"), 1)
            for x_ in range(3):
                pe.wait_ge(*banks.take(("os", x_)))
                out = banks.bank(("os", x_))
                nc.tensor.matmul(out[:, :], ones, rs[:, 2 * x_:2 * x_ + 2, :].rearrange("p a b -> p (a b)"),
                                 start=True, stop=True).then_inc(banks.full_sem(("os", x_)), 1)
            pe.wait_ge(sem("o_gated"), 1)
            for i in range(NT):
                pe.wait_ge(*banks.emptied(("mo", 0, i)))
            tm_out(pe, "a_out", [cat[:, kc, :] for kc in range(KC)])

        def two_scalar(act):
            mem_kv_scalar(act, 0)
            act.wait_ge(*banks.full("glr"))
            out = banks.bank("glr")
            nc.scalar.activation(glr[0:16, :], out[0:16, 0:TOK], ACT.Copy).then_inc(banks.emptied_sem("glr"), 1)

            def plain(name, to, scale=1.0):
                act.wait_ge(*banks.full(name))
                out = banks.bank(name)
                nc.scalar.activation(to, out[:, 0:TOK], ACT.Copy, scale=scale).then_inc(banks.emptied_sem(name), 1)

            plain(("q2", 0), qf[:, 0, :], 0.125)
            plain(("k2", 0), kf[:, 0, :])
            for j in range(1, 3):
                plain(("q2", j), qf[:, j, :], 0.125)
                plain(("k2", j), kf[:, j, :])
            act.wait_ge(sem("gate_abs"), 1)
            nc.scalar.activation(eb[:, :, :], eb[:, :, :], ACT.Exp).then_inc(sem("gate_exp"), 1)
            act.wait_ge(sem("gate_exp"), 1)
            nc.scalar.activation(eb[:, :, :], eb[:, :, :], ACT.Ln, bias=ones[:, 0:1]).then_inc(sem("gate_ln"), 1)
            for i in range(NT):
                for half, w in ((0, 512), (1, 256)):
                    act.wait_ge(*banks.full(("a_v", i, half)))
                    out = banks.bank(("a_v", i, half))
                    ins = nc.scalar.activation(vt[:, i, half * 512:half * 512 + w], out[:, 0:w], ACT.Copy)
                    ins.then_inc(banks.emptied_sem(("a_v", i, half)), 1)
            act.wait_ge(sem("gate_sums"), 1)
            nc.scalar.activation(eb[:, :, :], bsum[:, :, :], ACT.Exp, scale=1.0 / 16).then_inc(sem("gla_decays"), 1)
            nc.scalar.activation(enb[:, :, :], bsum[:, :, :], ACT.Exp, scale=-1.0 / 16).then_inc(sem("gla_decays"), 1)
            act.wait_ge(sem("to_end"), 1)
            nc.scalar.activation(ke[:, :, :], ke[:, :, :], ACT.Exp, scale=1.0 / 16).then_inc(sem("gla_decays"), 1)
            ins = nc.scalar.activation(small[:, 32:44], bsum[:, :, CH - 1], ACT.Exp, scale=1.0 / 16)
            ins.then_inc(sem("gla_decays"), 1)
            for j in range(6):
                act.wait_ge(*banks.full(("r2", j)))
                out = banks.bank(("r2", j))
                nc.scalar.activation(rf[:, j, :], out[:, 0:TOK], ACT.Silu).then_inc(banks.emptied_sem(("r2", j)), 1)
            for j in range(2):
                plain(("qm", 0, j), qm[:, j, :])
            memory_exp_scalar(act, 0)
            for i in range(NT):
                act.wait_ge(*banks.full(("keT", i)))
                out = banks.bank(("keT", i))
                nc.scalar.activation(keT[:, i, :], out[:, 0:384], ACT.Copy).then_inc(banks.emptied_sem(("keT", i)), 1)
            memory_out_scalar(act, 0)
            for i in range(NT):
                for par in range(2):
                    act.wait_ge(*banks.full(("o2", i, par)))
                    out = banks.bank(("o2", i, par))
                    to = cat[:, 0:6, i * P:(i + 1) * P].rearrange("p (j two) t -> p j two t", two=2)[:, :, par, :]
                    ins = nc.scalar.activation(to, out[:, 0:384].rearrange("p (a b) -> p a b", a=3), ACT.Copy)
                    ins.then_inc(banks.emptied_sem(("o2", i, par)), 1)
            for i in range(NT):
                for par in range(2):
                    act.wait_ge(*banks.emptied(("o2", i, par)))
            nc.scalar.activation(rs[:, :, :], cat[:, 0:6, :], ACT.Square).then_inc(sem("o_squares"), 1)
            act.wait_ge(sem("o_rstd"), 1)
            nc.scalar.activation(rs[:, :, :], rs[:, :, :], ACT.Sqrt).then_inc(sem("o_rstd"), 1)

        def two_vector(v):
            V = nc.vector

            V.memset(attn.rearrange("p a b c -> p (a b c)"), 0.0).then_inc(sem("dve_step"), 1)
            v.wait_ge(sem("dve_step"), count("dve_step"))
            lgj, tj, ebj = (x.rearrange("p (j c) t -> p j (c t)", j=3) for x in (lg, tmp2, eb))
            bj = bsum.rearrange("p (j c) t -> p j (c t)", j=3)
            for j in range(3):
                v.wait_ge(*banks.full(("lg", j)))
                out = banks.bank(("lg", j))
                ins = V.tensor_scalar(lgj[:, j, :], out[:, 0:TOK], col("b_gate", j), None, ALU.add)
                ins.then_inc(banks.emptied_sem(("lg", j)), 1)
            for j in range(3):
                v.wait_ge(*banks.emptied(("lg", j)))
            V.tensor_scalar(tmp2[:, :, :], lg[:, :, :], 0.0, None, ALU.min).then_inc(sem("dve_step"), 1)
            v.wait_ge(sem("dve_step"), count("dve_step"))
            ins = V.scalar_tensor_tensor(eb[:, :, :], lg[:, :, :], -1.0, lg[:, :, :], ALU.mult, ALU.min)
            ins.then_inc(sem("gate_abs"), 1)
            v.wait_ge(sem("gate_ln"), 1)
            V.tensor_tensor(lg[:, :, :], tmp2[:, :, :], eb[:, :, :], ALU.subtract).then_inc(sem("dve_step"), 1)
            v.wait_ge(sem("dve_step"), count("dve_step"))
            for j in range(3):
                ins = V.tensor_tensor_scan(bj[:, j, :], k("scan"), lgj[:, j, :], 0.0, ALU.mult, ALU.add)
            ins.then_inc(sem("gate_sums"), 1)
            v.wait_ge(sem("gate_sums"), 1)
            ins = V.tensor_tensor(ke[:, :, :], bc(bsum[:, :, CH - 1:CH], (CH, 12), (0, CH)), bsum[:, :, :], ALU.subtract)
            ins.then_inc(sem("to_end"), 1)
            for j in range(3):
                v.wait_ge(*banks.emptied(("q2", j)))
                v.wait_ge(*banks.emptied(("k2", j)))
            v.wait_ge(sem("gla_decays"), 4)
            kv = kf[:, 0:3, :].rearrange("p j t -> p (j t)")
            qv = qf[:, 0:3, :].rearrange("p j t -> p (j t)")
            flat = lambda x: x.rearrange("p a b -> p (a b)")
            V.tensor_tensor(flat(ke), flat(ke), kv, ALU.mult).then_inc(sem("dve_step"), 1)
            v.wait_ge(sem("dve_step"), count("dve_step"))
            V.tensor_tensor(qv, qv, flat(eb), ALU.mult).then_inc(sem("dve_step"), 1)
            v.wait_ge(sem("dve_step"), count("dve_step"))
            V.tensor_tensor(kv, kv, flat(enb), ALU.mult).then_inc(sem("ke_ready"), 1)
            memory_max_vector(v, 0)
            memory_norm_vector(v, 0)
            for i in range(NT):
                for par in range(2):
                    v.wait_ge(*banks.full(("attn", i, par)))
                    out = banks.bank(("attn", i, par))
                    ins = V.copy_predicated(attn[:, 2 * i + par, :, :], bc(k("incl"), (0, 3), (1, P)).bitcast(U32),
                                            out[:, 0:384].rearrange("p (a b) -> p a b", a=3))
                    ins.then_inc(banks.emptied_sem(("attn", i, par)), 1)
            for c in range(3):
                v.wait_ge(*banks.full(("du", c)))
                out = banks.bank(("du", c))
                if c:
                    v.wait_ge(*banks.emptied(("du", c - 1)))
                for j in range(3):
                    f = slice(j * P, (j + 1) * P)
                    if c == 0:
                        ins = V.tensor_copy(states[:, 1, j, :], out[:, f])
                    else:
                        ins = V.scalar_tensor_tensor(states[:, c + 1, j, :], states[:, c, j, :],
                                                     small[:, 32 + 4 * j + c:33 + 4 * j + c], out[:, f], ALU.mult, ALU.add)
                    ins.then_inc(banks.emptied_sem(("du", c)), 1)
            for x_ in range(3):
                v.wait_ge(*banks.full(("os", x_)))
                out = banks.bank(("os", x_))
                V.tensor_scalar(rs[:, 2 * x_:2 * x_ + 2, :], out[:, :].rearrange("p (a b) -> p a b", a=2),
                                1.0 / GLA_DV, 1e-5, ALU.mult, ALU.add).then_inc(banks.emptied_sem(("os", x_)), 1)
            for x_ in range(3):
                v.wait_ge(*banks.emptied(("os", x_)))
            V.reciprocal(rs[:, :, :], rs[:, :, :]).then_inc(sem("o_rstd"), 1)
            for hd in range(6):
                v.wait_ge(*banks.emptied(("r2", hd)))
                ins = V.scalar_tensor_tensor(rf[:, hd, :], cat[:, hd, :], col("head_g", hd), rf[:, hd, :], ALU.mult, ALU.mult)
            ins.then_inc(sem("dve_step"), 1)
            v.wait_ge(sem("dve_step"), count("dve_step"))
            v.wait_ge(sem("o_rstd"), 2)
            V.tensor_tensor(cat[:, 0:6, :], rf[:, :, :], rs[:, :, :], ALU.mult).then_inc(sem("o_gated"), 1)
            residual_in(v, "a_out", ALPHA)

        def three_tensor(pe):
            mem_kv_tensor(pe, 1)
            x = xT[:, :, 0:TOK]
            for j in range(6):
                fm_tile(pe, ("q3", j), ("b_q", j), x, TOK)
                fm_tile(pe, ("k3", j), ("b_k", j), x, TOK)
                if j % 2:
                    sb_scores_tensor(pe, j // 2)
            tm_out(pe, "b_v", [xT[:, kc, 0:TOK] for kc in range(KC)], 768)
            for j in range(2):
                fm_tile(pe, ("qm", 1, j), ("b_qm", j), x, TOK)
            memory_tensor(pe, 1)
            memory_values_tensor(pe, 1)
            for i in range(NT):
                for half in range(2):
                    pe.wait_ge(*banks.emptied(("b_v", i, half)))
            for q in range(3):
                pe.wait_ge(sem("att_ready"), q + 1)
                pe.wait_ge(*banks.take(("o3", q)))
                out = banks.bank(("o3", q))
                for x_ in range(4):
                    hd = 4 * q + x_
                    o = slice(64 * (hd % 2), 64 * (hd % 2) + 64)
                    at = (x_ // 2) * TOK
                    hs = slice(hd * 64, (hd + 1) * 64)
                    nc.tensor.matmul(out[o, at:at + TOK], vt[:, 0, hs], att[:, hd, 0:TOK], start=True, stop=True)
                    ins = nc.tensor.matmul(out[o, at + P:at + TOK], vt[:, 1, hs], att[:, hd, TOK:3 * P],
                                           start=False, stop=True, skip_group_check=True)
                ins.then_inc(banks.full_sem(("o3", q)), 1)
            for q in range(3):
                pe.wait_ge(*banks.emptied(("o3", q)))
            for i in range(NT):
                pe.wait_ge(*banks.emptied(("mo", 1, i)))
            tm_out(pe, "b_out", [cat[:, kc, :] for kc in range(KC)])

        def sb_scores_tensor(pe, q):
            for j in (2 * q, 2 * q + 1):
                pe.wait_ge(*banks.emptied(("q3", j)))
                pe.wait_ge(*banks.emptied(("k3", j)))
            for x_ in range(4):
                hd = 4 * q + x_
                j, r = hd // 2, slice(64 * (hd % 2), 64 * (hd % 2) + 64)
                pe.wait_ge(*banks.take(("sb", hd)))
                out = banks.bank(("sb", hd))
                nc.tensor.matmul(out[:, 0:TOK], kf[r, j, 0:P], qf[r, j, :], start=True, stop=True)
                ins = nc.tensor.matmul(out[:, TOK:3 * P], kf[r, j, P:TOK], qf[r, j, P:TOK], start=True, stop=True)
                ins.then_inc(banks.full_sem(("sb", hd)), 1)
            pe.wait_ge(sem("softplus_ready"), q + 1)
            for x_ in range(4):
                hd = 4 * q + x_
                pe.wait_ge(*banks.take(("above", hd)))
                out = banks.bank(("above", hd))
                nc.tensor.matmul(out[:, 0:TOK], k("below"), lb[:, x_, 0:TOK], start=True, stop=True)
                nc.tensor.matmul(out[:, P:TOK], ones, lb[:, x_, TOK:3 * P], start=False, stop=True, skip_group_check=True)
                ins = nc.tensor.matmul(out[:, TOK:3 * P], k("below"), lb[:, x_, TOK:3 * P], start=True, stop=True)
                ins.then_inc(banks.full_sem(("above", hd)), 1)

        def three_scalar(act):
            mem_kv_scalar(act, 1)

            def plain(name, to, scale=1.0):
                act.wait_ge(*banks.full(name))
                out = banks.bank(name)
                nc.scalar.activation(to, out[:, 0:TOK], ACT.Copy, scale=scale).then_inc(banks.emptied_sem(name), 1)

            for q in range(3):
                for j in (2 * q, 2 * q + 1):
                    plain(("q3", j), qf[:, j, :], 0.125)
                    plain(("k3", j), kf[:, j, :])
                if q:
                    act.wait_ge(sem("att_before"), q)
                for x_ in range(4):
                    act.wait_ge(*banks.full(("sb", 4 * q + x_)))
                    out = banks.bank(("sb", 4 * q + x_))
                    ins = nc.scalar.activation(zb[:, x_, :], out[:, 0:3 * P], ACT.Copy)
                    ins.then_inc(banks.emptied_sem(("sb", 4 * q + x_)), 1)
                act.wait_ge(sem("z_abs"), q + 1)
                nc.scalar.activation(lb[:, :, :], lb[:, :, :], ACT.Exp).then_inc(sem("sb_exp"), 1)
                act.wait_ge(sem("sb_exp"), q + 1)
                nc.scalar.activation(lb[:, :, :], lb[:, :, :], ACT.Ln, bias=ones[:, 0:1]).then_inc(sem("sb_ln"), 1)
                act.wait_ge(sem("log_a"), q + 1)
                nc.scalar.activation(att[:, 4 * q:4 * q + 4, :], sp_[:, :, :], ACT.Exp).then_inc(sem("att_exp"), 1)
            for i in range(NT):
                for half, w in ((0, 512), (1, 256)):
                    act.wait_ge(*banks.full(("b_v", i, half)))
                    out = banks.bank(("b_v", i, half))
                    ins = nc.scalar.activation(vt[:, i, half * 512:half * 512 + w], out[:, 0:w], ACT.Copy)
                    ins.then_inc(banks.emptied_sem(("b_v", i, half)), 1)
            for j in range(2):
                plain(("qm", 1, j), qm[:, j, :])
            memory_exp_scalar(act, 1)
            memory_out_scalar(act, 1)
            for q in range(3):
                act.wait_ge(*banks.full(("o3", q)))
                out = banks.bank(("o3", q))
                nc.scalar.activation(cat[:, 2 * q:2 * q + 2, :], out[:, :].rearrange(
     "p (a b) -> p a b", a=2), ACT.Copy).then_inc(banks.emptied_sem(("o3", q)), 1)

        def three_vector(v):
            V = nc.vector

            V.tensor_copy(mask3[:, 0:P], k("sbmask"))
            V.memset(mask3[:, P:TOK], 1.0)
            V.tensor_copy(mask3[:, TOK:3 * P], k("sbmask")).then_inc(sem("dve_step"), 1)
            v.wait_ge(sem("dve_step"), count("dve_step"))
            m4 = bc(mask3, (0, 4), (1, 3 * P))
            for q in range(3):
                for x_ in range(4):
                    v.wait_ge(*banks.emptied(("sb", 4 * q + x_)))
                ins = V.scalar_tensor_tensor(lb[:, :, :], zb[:, :, :], -1.0, zb[:, :, :], ALU.mult, ALU.min)
                ins.then_inc(sem("z_abs"), 1)
                v.wait_ge(sem("sb_ln"), q + 1)
                ins = V.scalar_tensor_tensor(sp_[:, :, :], zb[:, :, :], 0.0, lb[:, :, :], ALU.max, ALU.add)
                ins.then_inc(sem("dve_step"), 1)
                v.wait_ge(sem("dve_step"), count("dve_step"))
                V.tensor_tensor(lb[:, :, :], sp_[:, :, :], m4, ALU.mult).then_inc(sem("softplus_ready"), 1)
                V.tensor_tensor(sp_[:, :, :], zb[:, :, :], sp_[:, :, :], ALU.subtract).then_inc(sem("dve_step"), 1)
                v.wait_ge(sem("dve_step"), count("dve_step"))
                for x_ in range(4):
                    v.wait_ge(*banks.full(("above", 4 * q + x_)))
                    out = banks.bank(("above", 4 * q + x_))
                    ins = V.tensor_tensor(sp_[:, x_, :], sp_[:, x_, :], out[:, 0:3 * P], ALU.subtract)
                    ins.then_inc(banks.emptied_sem(("above", 4 * q + x_)), 1)
                for x_ in range(4):
                    v.wait_ge(*banks.emptied(("above", 4 * q + x_)))
                V.tensor_scalar(sp_[:, :, :], sp_[:, :, :], 0.0, None, ALU.min).then_inc(sem("log_a"), 1)
                v.wait_ge(sem("att_exp"), q + 1)
                a = att[:, 4 * q:4 * q + 4, :]
                V.tensor_tensor(a, a, m4, ALU.mult).then_inc(sem("att_ready"), 1)
                if q < 2:
                    V.memset(small[:, 44:45], 0.0).then_inc(sem("att_before"), 1)
            memory_max_vector(v, 1)
            memory_norm_vector(v, 1)
            residual_in(v, "b_out", ALPHA)

        def wait_rows(v, norm):
            v.wait_ge(sem("rows_in_1"), 16 * norm)
            v.wait_ge(sem("rows_in_0"), 16 * (norm + 1))

        def ln_scalar(act, n, m):
            act.wait_ge(sem("ln_mean"), m + 1)
            sums_of_squares(act, n, 4)
            root(act, n)

        def wait_residual(eng, name):
            for i in range(NT):
                for half in range(2):
                    eng.wait_ge(*banks.emptied((name, i, half)))

        blk = ctx.enter_context(nc.Block())

        @blk.tensor
        def _(pe):
            one_tensor(pe)
            fm_tensor(pe, "xT0", xn, 0)
            peer_scores_tensor(pe, 0)
            peer_tensor(pe, 0)
            fm_tensor(pe, "xT1", h, 1)
            two_tensor(pe)
            fm_tensor(pe, "xT2", h, 2)
            peer_scores_tensor(pe, 1)
            peer_tensor(pe, 1)
            fm_tensor(pe, "xT3", h, 3)
            three_tensor(pe)
            fm_tensor(pe, "xT4", h, 4)
            peer_scores_tensor(pe, 2)
            peer_tensor(pe, 2)

        @blk.vector
        def _(v):
            one_vector(v)
            wait_residual(v, "w_o")
            v.wait_ge(sem("rows_in_1"), 16)
            rms_vector(v, 0, xn, rows[:, 1, :])
            peer_vector(v, 0)
            residual_peer(v, 1.0)
            v.wait_ge(sem("rows_in_0"), 32)
            rms_vector(v, 1, h, rows[:, 0, :])
            two_vector(v)
            wait_residual(v, "a_out")
            wait_rows(v, 2)
            ln_vector(v, 2, 0)
            peer_vector(v, 1)
            residual_peer(v, ALPHA)
            wait_rows(v, 3)
            ln_vector(v, 3, 1)
            three_vector(v)
            wait_residual(v, "b_out")
            wait_rows(v, 4)
            ln_vector(v, 4, 2)
            peer_vector(v, 2)
            residual_peer(v, ALPHA)
            wait_rows(v, 5)
            ln_vector(v, 5, 3)

        @blk.scalar
        def _(act):
            one_scalar(act)
            wait_residual(act, "w_o")
            sums_of_squares(act, 0)
            root(act, 0)
            fm_scalar(act, "xT0")
            peer_scores_scalar(act, 0)
            peer_scalar(act, 0)
            act.wait_ge(sem("peer_added"), NT)
            sums_of_squares(act, 1)
            root(act, 1)
            fm_scalar(act, "xT1")
            two_scalar(act)
            ln_scalar(act, 2, 0)
            fm_scalar(act, "xT2")
            peer_scores_scalar(act, 1)
            peer_scalar(act, 1)
            ln_scalar(act, 3, 1)
            fm_scalar(act, "xT3")
            three_scalar(act)
            ln_scalar(act, 4, 2)
            fm_scalar(act, "xT4")
            peer_scores_scalar(act, 2)
            peer_scalar(act, 2)
            ln_scalar(act, 5, 3)

        @blk.gpsimd
        def _(pool):
            one_gpsimd(pool)
            for n in range(3):
                peer_gpsimd(pool, n)

        @blk.sync
        def _(sp):
            first = {b[0]: n for n, b in reversed(list(enumerate(plan)))}
            one_sync(sp)
            at = first["w_q", 0, 0]
            load_blocks(sp, 0, at)
            sp.wait_ge(*banks.full(("rwkv_out", 0)))
            load_row(sp, 0, 1)
            for norm, layer in ((2, 0), (4, 1)):
                load_blocks(sp, at, first["mem_k", layer, 0] + SLOTS)
                at = first["mem_k", layer, 0] + SLOTS
                sp.wait_ge(sem("normed"), NT * norm)
                sp.dma_start(memT.rearrange("p a b -> p (a b)"), io["memT"]).then_inc(sem("memT_in"), 16)
                if layer == 0:
                    sp.dma_start(gate2[0:16, :], io["a_gate2"]).then_inc(sem("gate2_in"), 16)
                load_row(sp, 1, 2 * norm - 2)
                load_row(sp, 0, 2 * norm - 1)
                load_blocks(sp, at, first["w_q", layer + 1, 0] + SLOTS)
                at = first["w_q", layer + 1, 0] + SLOTS
                sp.wait_ge(sem("normed"), NT * (norm + 1))
                load_row(sp, 1, 2 * norm)
                load_row(sp, 0, 2 * norm + 1)
            load_blocks(sp, at, len(plan))
            out = io["out"].rearrange("(i p) d -> i p d", p=P)
            for i in range(NT):
                sp.wait_ge(sem("normed"), NT * 5 + i + 1)
                sp.dma_start(out[i], h[:, i, :]).then_inc(sem("out_written"), 16)
            sp.wait_ge(sem("out_written"), 16 * NT)


def fm_blocks(w):
    n = w.shape[1] // P
    return np.ascontiguousarray(w.reshape(KC, P, n, P).transpose(2, 1, 0, 3).reshape(n, P, KC * P))


def half_fm_blocks(w):
    return np.ascontiguousarray(w.reshape(4, P, 4, 2, P).transpose(2, 1, 3, 0, 4).reshape(4, P, D))


def column(a):
    return a.reshape(-1, P).T


def lay_out(i):
    a = {}
    a["const"] = constants()
    a["x"] = i["x"][0]
    a["meta"] = i["meta_tokens"]
    a["w_in"] = fm_blocks(i["w_in"][0])
    a["lora"] = np.concatenate([np.concatenate([i["w_up"][0], i["a_up"][0]], 0), i["g_up"][0]], 1)
    a["cols"] = np.concatenate([column(i["g_mix"][0]), column(i["mu_shift"][0]), column(i["w0"][0]),
                                column(i["a0"][0]), column(i["k_k"][0]), column(i["k_a"][0]),
                                column(i["r_k"][0].reshape(-1)), column(i["conv_b"][0]), column(i["conv_ln_g"][0]),
                                column(i["conv_ln_b"][0]),
                                i["conv_w"][0].reshape(TAPS, CT, P).transpose(2, 0, 1).reshape(P, -1),
                                column(i["a_b_gate_2"][0]), column(i["a_head_g_2"][0].reshape(-1))], 1)
    a["w_conv_out"] = half_fm_blocks(i["w_conv_out"][0])
    a["w_rwkv_out"] = half_fm_blocks(i["w_rwkv_out"][0])
    a["w_o"] = i["w_o"][0].reshape(KC, P, D)
    a["gn_rows"] = np.concatenate([i["gn_g"][0], i["gn_b"][0]])
    w_q = np.concatenate([i["w_q"], i["peer_w_q_2"]])
    a["w_q"] = np.stack([fm_blocks(w) for w in w_q])
    keys = np.concatenate([i["sub_keys"], i["peer_subkeys_2"]])
    a["keys"] = keys.reshape(3, 2 * PH, P, P).transpose(0, 3, 1, 2).reshape(3, P, 2 * PH * P)
    kv = np.concatenate([i["a_w_mem_kv_2"], i["b_w_mem_kv_2"]])
    a["mem_k"] = np.stack([fm_blocks(w[:, :256]) for w in kv])
    a["mem_v"] = kv[:, :, 256:].reshape(2, 2, 4, P, 256).transpose(0, 1, 3, 2, 4).reshape(2, 2, P, D)
    a["memT"] = i["mem_2"][0].T.reshape(KC, P, 256).transpose(1, 0, 2).reshape(P, KC * 256)
    w = i["a_w_in_2"][0]
    a["a_fm"] = fm_blocks(np.concatenate([w[:, :768], w[:, 1536:2304], w[:, 2320:]], 1))
    a["a_glr"] = w[:, 2304:2320].reshape(KC, P, 16).transpose(1, 0, 2).reshape(P, P)
    a["a_v"] = w[:, 768:1536].reshape(KC, P, 768)
    a["a_gate2"] = i["a_w_gate2_2"][0]
    a["a_out"] = i["a_w_out_2"][0].reshape(KC, P, D)
    a["b_fm"] = fm_blocks(i["b_w_in_2"][0])
    a["sb_k"] = fm_blocks(i["sb_w_kv_2"][:, :768])
    a["sb_v"] = i["sb_w_kv_2"][:, 768:].reshape(KC, P, 768)
    a["b_out"] = i["b_w_out_2"][0].reshape(KC, P, D)
    a["rows"] = np.stack([i["g_ffn"][0], i["g_final"], i["ln_g_2"][0, 0], i["ln_b_2"][0, 0], i["ln_g_2"][0, 1],
                          i["ln_b_2"][0, 1], i["ln_g_2"][1, 0], i["ln_b_2"][1, 0], i["ln_g_2"][1, 1], i["ln_b_2"][1, 1]])
    a["u0"], a["v0"] = i["expert_u"][0], i["expert_v"][0]
    for n in range(2):
        a[f"u{n + 1}"], a[f"v{n + 1}"] = i["peer_u_2"][n], i["peer_v_2"][n]
    return {name: np.ascontiguousarray(v) for name, v in a.items()}


def kernel(**inputs):
    import concourse.bacc as bacc
    from concourse.bass_utils import run_bass_kernel_spmd

    arrays = lay_out({name: np.asarray(v) for name, v in inputs.items()})
    nc = bacc.Bacc("TRN2", target_bir_lowering=False, num_devices=1)
    io = {name: nc.dram_tensor(f"in_{name}", v.shape, F32, kind="ExternalInput").ap() for name, v in arrays.items()}
    io["out"] = nc.dram_tensor("out", (TOK, D), F32, kind="ExternalOutput").ap()
    build(nc, io)
    r = run_bass_kernel_spmd(nc, [{f"in_{name}": v for name, v in arrays.items()}], core_ids=[0])
    return r.results[0]["out"].reshape(1, TOK, D)
```

```python
from contextlib import ExitStack

import numpy as np

import concourse.bass as bass
from concourse import mybir

ALU = mybir.AluOpType
ACT = mybir.ActivationFunctionType
AX = mybir.AxisListType
F32 = mybir.dt.float32
U32 = mybir.dt.uint32

P = 128
D = 1024
KC = D // P
TOK = 256
NT = TOK // P
META = 16
TALL = TOK + META
CONV_C = 512
TAPS = 31
CT = CONV_C // P
RW = 512
RH = 64
RM = RW // P
CH = 64
LEVELS = 6
GATES_AT = {"NV": 10, "UA": 11, "S": 12, "O": 13}
PH = 8
PK = 16
NKEYS = 128
Q_GROUPS = ((0, 2), (2, 6), (6, 10), (10, 14), (14, 16))
SLOTS = 6
RING = 8
DECAY = float(np.exp(-0.5))
GLA_H, GLA_DK, GLA_DV = 6, 64, 128
SB_H = 12
MEM_H = 4
OUT_ORDER = (6, 7, 0, 1, 2, 3, 4, 5)
ALPHA = float((2.0 * 2) ** 0.25)

CONST = {}
_n = 0
for _name, _w in (("ident", P), ("ones", P), ("headsum", P), ("strict", P), ("incl", P), ("ident2", 64),
                  ("scan_all", TALL), ("scan", TOK), ("below", P), ("sbmask", P), ("iota", PK),
                  ("onehead", RM * 8), ("levels", LEVELS * P)):
    CONST[_name] = (_n, _w)
    _n += _w
NCONST = _n
NCONST_KEEP = CONST["onehead"][0]

COLS = {}
_n = 0
for _name, _w in (("g_mix", 8), ("mu", 14), ("w0", 4), ("a0", 4), ("k_k", 4), ("k_a", 4), ("r_k", 4),
                  ("conv_b", 4), ("conv_ln_g", 4), ("conv_ln_b", 4), ("conv_w", CT * TAPS),
                  ("b_gate", 3), ("head_g", 6)):
    COLS[_name] = (_n, _w)
    _n += _w
NCOLS = _n


def constants():
    c = np.zeros((P, NCONST), np.float32)
    p = np.arange(P)[:, None]
    f = np.arange(P)[None, :]

    def put(name, value):
        at, w = CONST[name]
        c[:, at:at + w] = value

    put("ident", p == f)
    put("ones", 1.0)
    put("headsum", p // RH == f // RH)
    put("strict", (p // CH == f // CH) & (p < f))
    put("incl", (p // CH == f // CH) & (p <= f))
    put("ident2", p % 64 == f[:, :64])
    t = np.arange(TALL)[None, :] + 0 * p
    put("scan_all", (t != 0) & ((t - META) % CH != 0))
    put("scan", t[:, :TOK] % CH != 0)
    put("below", p > f)
    put("sbmask", p < f)
    put("iota", np.arange(PK)[None, :] + 0 * p)
    m = np.arange(RM)[None, :, None]
    h = np.arange(8)[None, None, :]
    put("onehead", (2 * m + p[:, :, None] // RH == h).reshape(P, RM * 8))
    lev = [((p // (2 * s) == f // (2 * s)) & (p // s % 2 == 0) & (f // s % 2 == 1)) for s in (1, 2, 4, 8, 16, 32)]
    put("levels", np.concatenate(lev, 1))
    return c


class Banks:

    def __init__(self, banks, full, emptied):
        self.banks, self.sem_full, self.sem_emptied = banks, full, emptied
        self.fills = [0] * len(banks)
        self.reads = [0] * len(banks)
        self.jobs = {}
        self.n = 0

    def take(self, name, reads=1):
        b = self.n % len(self.banks)
        self.n += 1
        before = self.reads[b] + 1
        self.fills[b] += 1
        self.reads[b] += reads
        self.jobs[name] = (b, self.fills[b], self.reads[b] + 1)
        return self.sem_emptied[b], before

    def bank(self, name):
        return self.banks[self.jobs[name][0]]

    def full_sem(self, name):
        return self.sem_full[self.jobs[name][0]]

    def emptied_sem(self, name):
        return self.sem_emptied[self.jobs[name][0]]

    def full(self, name):
        b, fills, _ = self.jobs[name]
        return self.sem_full[b], fills

    def emptied(self, name):
        b, _, reads = self.jobs[name]
        return self.sem_emptied[b], reads


class Arena:

    def __init__(self, tensor, size):
        self.t, self.size, self.at = tensor, size, 0

    def view(self, at, *dims):
        n = int(np.prod(dims))
        assert at + n <= self.size, (at, n, self.size)
        ap = self.t[:, at:at + n]
        if len(dims) == 2:
            ap = ap.rearrange("p (a b) -> p a b", a=dims[0])
        elif len(dims) == 3:
            ap = ap.rearrange("p (a b c) -> p a b c", a=dims[0], b=dims[1])
        return ap

    def take(self, *dims):
        v = self.view(self.at, *dims)
        self.at += int(np.prod(dims))
        return v


def bc(ap, *dims):
    return bass.AP(tensor=ap.tensor, offset=ap.offset, ap=[list(ap.ap[0])] + [list(d) for d in dims])


def build(nc, io):
    with ExitStack() as ctx:
        def sbuf(name, shape, dt=F32):
            return ctx.enter_context(nc.sbuf_tensor(name, shape, dt))

        sems = {}

        def sem(name):
            if name not in sems:
                sems[name] = ctx.enter_context(nc.semaphore(name))
            return sems[name]

        counts = {}

        def count(name, by=1):
            counts[name] = counts.get(name, 0) + by
            return counts[name]

        const = sbuf("const", [P, NCONST_KEEP])
        cols = sbuf("cols", [P, NCOLS])
        h = sbuf("h", [P, NT, D])
        xT = sbuf("xT", [P, KC, TALL])
        weights = sbuf("weights", [P, SLOTS, D])
        rows = sbuf("rows", [P, 2, D])
        small = sbuf("small", [P, 64])
        idx_best = sbuf("idx_best", [P, 2, PK], U32)
        idx_pos = sbuf("idx_pos", [P, 3, PK], U32)
        idx_next = sbuf("idx_next", [P, PK], U32)
        idx = sbuf("idx", [P, 3, PK], U32)
        ARENA = 38600
        arena_t = sbuf("arena", [P, ARENA])

        def k(name, parts=P):
            at, w = CONST[name]
            return const[0:parts, at:at + w]

        def col(name, j, lo=0, hi=P):
            at, _ = COLS[name]
            return cols[lo:hi, at + j:at + j + 1]

        ident = k("ident")
        ones = k("ones")

        psum = [ctx.enter_context(nc.psum_tensor(f"bank{b}", [P, 512], F32)) for b in range(8)]
        NB = 6
        banks = Banks(psum[:NB], [sem(f"full_{b}") for b in range(NB)], [sem(f"emptied_{b}") for b in range(NB)])
        acc_lo, acc_hi = psum[6], psum[7]

        plan = []

        def block_of(name, src, width=D, parts=P):
            plan.append((name, src, width, parts))

        for c in range(CT):
            block_of(("gate", c), io["w_in"][4 + c])
            block_of(("val", c), io["w_in"][c])
        for j in range(14):
            block_of(("z", j), io["w_in"][8 + j])
        for j in range(4):
            block_of(("ab", j), io["w_in"][22 + j])
        block_of("lora", io["lora"])
        for j in range(4, GATES_AT["NV"]):
            block_of(("ab", j), io["w_in"][22 + j])
        for j in range(4):
            block_of(("conv_out", j), io["w_conv_out"][j])
        for j in range(GATES_AT["NV"], 16):
            block_of(("ab", j), io["w_in"][22 + j])
        for j in range(4):
            block_of(("rwkv_out", j), io["w_rwkv_out"][j])
        for j in range(KC):
            block_of(("w_o", j), io["w_o"][j])

        def plan_peer(n):
            for lo, hi in Q_GROUPS:
                for j in range(lo, hi):
                    block_of(("w_q", n, j), io["w_q"][n][j])
                block_of(("keys", n, lo), io["keys"][n][:, lo * P:hi * P], (hi - lo) * P)

        def plan_mem(n):
            for j in range(2):
                block_of(("mem_k", n, j), io["mem_k"][n][j])
            for j in range(2):
                block_of(("mem_v", n, j), io["mem_v"][n][j])

        plan_peer(0)
        plan_mem(0)
        block_of("glr", io["a_glr"], P // 8 * KC)
        for j in range(3):
            block_of(("a_q", j), io["a_fm"][j])
            block_of(("a_k", j), io["a_fm"][3 + j])
        for j in range(KC):
            block_of(("a_v", j), io["a_v"][j], 768)
        for j in range(2):
            block_of(("a_qm", j), io["a_fm"][12 + j])
        for j in range(6):
            block_of(("a_r", j), io["a_fm"][6 + j])
        for j in OUT_ORDER:
            block_of(("a_out", j), io["a_out"][j])
        plan_peer(1)
        plan_mem(1)
        for j in range(6):
            block_of(("b_q", j), io["b_fm"][j])
            block_of(("b_k", j), io["sb_k"][j])
        for j in range(2):
            block_of(("b_qm", j), io["b_fm"][6 + j])
        for j in range(KC):
            block_of(("b_v", j), io["sb_v"][j], 768)
        for j in OUT_ORDER:
            block_of(("b_out", j), io["b_out"][j])
        plan_peer(2)

        LAYER_START = ("glr", ("b_q", 0))
        taken = []

        def landed(name):
            n = len(taken)
            assert plan[n][0] == name, (plan[n][0], name)
            taken.append(name)
            return sem(f"landed_{n % SLOTS}"), 16 * (n // SLOTS + 1)

        def slot(name):
            return weights[:, taken.index(name) % SLOTS, :]

        released = {}

        def last_use(job):
            released[len(taken) - 1] = job

        def last_use_here():
            released[len(taken) - 1] = count("blocks_used")

        def load_blocks(sp, lo, hi):
            for n in range(lo, min(hi, len(plan))):
                _, src, width, parts = plan[n]
                if n >= SLOTS:
                    by = released[n - SLOTS]
                    if type(by) is int:
                        sp.wait_ge(sem("blocks_used"), by)
                    else:
                        sp.wait_ge(*banks.full(by))
                sp.dma_start(weights[0:parts, n % SLOTS, 0:width], src).then_inc(sem(f"landed_{n % SLOTS}"), 16)

        def fm_tile(pe, job, block, x, n):
            pe.wait_ge(*landed(block))
            w = slot(block)
            pe.wait_ge(*banks.take(job))
            out = banks.bank(job)
            for kc in range(KC):
                ins = nc.tensor.matmul(out[:, 0:n], w[:, kc * P:(kc + 1) * P], x[:, kc, :],
                                       start=kc == 0, stop=kc == KC - 1)
            ins.then_inc(banks.full_sem(job), 1)
            last_use(job)

        REGION = 8 * 2048
        A = Arena(arena_t, ARENA)
        region = A.take(REGION)
        zs = A.take(14, TALL)
        ycv = A.take(CT, TOK)
        gates = A.take(16, TOK)
        alpha, beta, kappa, rho = (A.take(RM, TALL) for _ in range(4))
        tm = A.take(NT * 4, RW)
        tmm = A.take(4, RW)
        gtm = A.take(NT, RW)
        L1C = A.at
        onehead = A.take(RM, 8)
        levels = A.take(LEVELS, P)
        meta_mats = A.take(12, 64)
        rksel = A.take(RM, 8)
        pend = A.take(5, RM)
        front_end = A.at
        B = Arena(arena_t, REGION)
        z = B.take(14, TALL + 1)
        sg, av, kk, kp, cum, tt = (B.take(RM, TALL) for _ in range(6))
        sgate = B.take(CT, TALL)
        u = B.take(CT, TALL + TAPS - 1)
        sq = B.take(CT, TOK)
        E1, E2, E3 = (A.view(i * RM * TALL, RM, TALL) for i in range(3))
        B = Arena(arena_t, REGION)
        GROUPS = [(i, par) for i in range(NT) for par in range(2)]
        MT, NTm, QK, QB, Tm, Wm = ({g: B.take(4, P) for g in GROUPS} for _ in range(6))
        MTl4 = [B.take(4, P) for _ in range(4)]
        Ym = {g: B.take(4, P) for g in GROUPS}
        mm = {}
        n = 0
        for g in (("meta", 0), ("meta", 1)):
            for q in ("MT", "NT", "T", "W", "MTl", "Y"):
                mm[g, q] = meta_mats[0:META, n, :].rearrange("p (a b) -> p a b", a=4)
                n += 1
        for g in (("meta", 0), ("meta", 1)):
            MT[g], NTm[g], Tm[g], Wm[g], Ym[g] = (mm[g, q] for q in ("MT", "NT", "T", "W", "Y"))
        ALLG = GROUPS + [("meta", 0), ("meta", 1)]
        LEVELS_OF = {0: LEVELS, 1: LEVELS, "meta": 4}
        JOINS = {}
        for lev in range(LEVELS):
            for g in ALLG:
                if lev < LEVELS_OF[g[0]]:
                    JOINS[lev, g] = len(JOINS) + 1
        B = Arena(arena_t, 2048)
        NV = {g: B.take(4, RH) for g in GROUPS}
        RQT = B.take(RM, NT, P)
        B = Arena(arena_t, REGION)
        B.at = 4 * 2048
        UA = {g: B.take(4, P) for g in GROUPS}
        B.at = 6 * 2048
        KB, GT, S = B.take(4, RM, RH), B.take(3, RM, RH), B.take(4, RM, RH)
        for par in range(2):
            NV["meta", par] = B.take(4, RH)
            UA["meta", par] = A.view(REGION + 4 * TALL + par * 512, 4, P)
        assert A.at <= ARENA, A.at
        o_at = (REGION + 14 * TALL + 1024 + 4096)
        otm = A.view(o_at, NT * 8, RH)
        otmp = A.view(o_at + 1024, NT * 8, RH)
        oT = A.view(o_at + 2048, RM, TOK)
        hn = A.view(o_at, NT, D)
        hmeta = A.view(o_at + 2048, D)
        hsq = A.view(o_at + 3072, D)


        def one_tensor(pe):
            pe.wait_ge(sem("const_in"), 16)
            pe.wait_ge(sem("hn_ready"), 3)
            for kc in range(KC):
                pe.wait_ge(*banks.take(("xT", kc)))
                out = banks.bank(("xT", kc))
                f = slice(kc * P, (kc + 1) * P)
                nc.tensor.transpose(out[:, 0:META], hmeta[0:META, f], ident[0:META, 0:META])
                nc.tensor.transpose(out[:, META:META + P], hn[:, 0, f], ident)
                nc.tensor.transpose(out[:, META + P:TALL], hn[:, 1, f], ident).then_inc(banks.full_sem(("xT", kc)), 1)
            for kc in range(KC):
                pe.wait_ge(*banks.emptied(("xT", kc)))
            for c in range(CT):
                for name in ("gate", "val"):
                    fm_tile(pe, (name, c), (name, c), xT, TALL)
            for j in range(14):
                fm_tile(pe, ("z", j), ("z", j), xT, TALL)
            pe.wait_ge(sem("conv_tap"), CT * TAPS)
            pe.wait_ge(*banks.take("conv_sum"))
            out = banks.bank("conv_sum")
            for c in range(CT):
                ins = nc.tensor.matmul(out[:, 0:TOK], ones, ycv[:, c, :], start=c == 0, stop=c == CT - 1)
            ins.then_inc(banks.full_sem("conv_sum"), 1)
            for j in range(4):
                gate_tile(pe, j)
            pe.wait_ge(sem("conv_sq"), 1)
            pe.wait_ge(*banks.take("conv_var"))
            out = banks.bank("conv_var")
            for c in range(CT):
                ins = nc.tensor.matmul(out[:, 0:TOK], ones, sq[:, c, :], start=c == 0, stop=c == CT - 1)
            ins.then_inc(banks.full_sem("conv_var"), 1)
            pe.wait_ge(*landed("lora"))
            lora = slot("lora")
            pe.wait_ge(sem("lora_in"), 2)
            for m in range(RM):
                f = slice(m * P, (m + 1) * P)
                pe.wait_ge(*banks.take(("decay", m)))
                out = banks.bank(("decay", m))
                nc.tensor.matmul(out[:, 0:TALL], lora[0:64, f], zs[0:64, 12, :],
                                 start=True, stop=True).then_inc(banks.full_sem(("decay", m)), 1)
                pe.wait_ge(*banks.take(("a", m)))
                out = banks.bank(("a", m))
                nc.tensor.matmul(out[:, 0:TALL], lora[64:128, f], zs[64:128, 12, :],
                                 start=True, stop=True).then_inc(banks.full_sem(("a", m)), 1)
            for i in range(NT):
                pe.wait_ge(*banks.take(("g", i)))
                out = banks.bank(("g", i))
                ins = nc.tensor.matmul(out[:, :], zs[:, 13, META + i * P:META + (i + 1) * P], lora[:, 512:1024],
                                       start=True, stop=True)
                ins.then_inc(banks.full_sem(("g", i)), 1)
            last_use(("g", NT - 1))
            pe.wait_ge(sem("kk_sq"), 1)
            for m in range(RM):
                pe.wait_ge(*banks.take(("kk_sum", m)))
                out = banks.bank(("kk_sum", m))
                ins = nc.tensor.matmul(out[:, 0:TALL], k("headsum"), E1[:, m, :], start=True, stop=True)
                ins.then_inc(banks.full_sem(("kk_sum", m)), 1)
            for j in range(4, GATES_AT["NV"]):
                gate_tile(pe, j)
            pe.wait_ge(sem("conv_out_in"), CT)
            branch_out(pe, "conv_out", ycv)
            pe.wait_ge(sem("rkr_ready"), 1)
            pe.wait_ge(sem("rksel_ready"), 1)
            for i in range(NT):
                pe.wait_ge(*banks.take(("bonus", i)))
                out = banks.bank(("bonus", i))
                for m in range(RM):
                    ins = nc.tensor.matmul(out[:, 0:8], tt[:, m, META + i * P:META + (i + 1) * P], rksel[:, m, :],
                                           start=m == 0, stop=m == RM - 1)
                ins.then_inc(banks.full_sem(("bonus", i)), 1)
            pe.wait_ge(sem("abkr_ready"), 1)
            fms = (alpha, beta, kappa, zs[:, 8:12, :])
            for i in range(NT):
                for q, src in enumerate(fms):
                    pe.wait_ge(*banks.take(("tm", i, q)))
                    out = banks.bank(("tm", i, q))
                    for m in range(RM):
                        ins = nc.tensor.transpose(out[:, m * P:(m + 1) * P],
                                                  src[:, m, META + i * P:META + (i + 1) * P], ident)
                    ins.then_inc(banks.full_sem(("tm", i, q)), 1)
            for q, src in enumerate(fms):
                pe.wait_ge(*banks.take(("tm", "meta", q)))
                out = banks.bank(("tm", "meta", q))
                for m in range(RM):
                    ins = nc.tensor.transpose(out[0:META, m * P:(m + 1) * P], src[:, m, 0:META], ident)
                ins.then_inc(banks.full_sem(("tm", "meta", q)), 1)
            for i, par in ALLG:
                n = META if i == "meta" else P
                at = 0 if i == "meta" else META + i * P
                r = slice(64 * par, 64 * par + 64)
                for name, lhs, rhs in (("MT", beta, alpha), ("NT", kappa, alpha), ("QK", kappa, rho), ("QB", beta, rho)):
                    if i == "meta" and name[0] == "Q":
                        continue
                    pe.wait_ge(*banks.take((name, i, par)))
                    out = banks.bank((name, i, par))
                    for m in range(RM):
                        ins = nc.tensor.matmul(out[0:n, m * n:(m + 1) * n], lhs[r, m, at:at + n], rhs[r, m, at:at + n],
                                               start=True, stop=True)
                    ins.then_inc(banks.full_sem((name, i, par)), 1)
            for n_g, g in enumerate(ALLG):
                n = META if g[0] == "meta" else P
                pe.wait_ge(sem("first_joined"), n_g + 1)
                pe.wait_ge(*banks.take(("X", 0, g)))
                out = banks.bank(("X", 0, g))
                for m in range(4):
                    ins = nc.tensor.transpose(out[0:n, m * n:(m + 1) * n], Wm[g][0:n, m, :], ident[0:n, 0:n])
                ins.then_inc(banks.full_sem(("X", 0, g)), 1)
            for lev in range(1, LEVELS):
                groups = [g for g in ALLG if lev < LEVELS_OF[g[0]]]
                for g in groups:
                    n = META if g[0] == "meta" else P
                    mtl, t, w, y = level_bufs(g)
                    pe.wait_ge(sem("joins_ready"), JOINS[lev, g])
                    pe.wait_ge(*banks.emptied(("X", lev - 1, g)))
                    if lev > 1:
                        pe.wait_ge(*banks.emptied(("XT", lev - 1, g)))
                    pe.wait_ge(*banks.take(("Y", lev, g)))
                    out = banks.bank(("Y", lev, g))
                    for m in range(4):
                        ins = nc.tensor.matmul(out[0:n, m * n:(m + 1) * n], mtl[:, m, :], t[:, m, :], start=True,
                                               stop=True)
                    ins.then_inc(banks.full_sem(("Y", lev, g)), 1)
                for g in groups:
                    n = META if g[0] == "meta" else P
                    mtl, t, w, y = level_bufs(g)
                    pe.wait_ge(*banks.emptied(("Y", lev, g)))
                    for name, lhs, rhs in (("X", w, y), ("XT", y, w)):
                        if name == "X" and lev == LEVELS_OF[g[0]] - 1:
                            continue
                        pe.wait_ge(*banks.take((name, lev, g)))
                        out = banks.bank((name, lev, g))
                        for m in range(4):
                            ins = nc.tensor.matmul(out[0:n, m * n:(m + 1) * n], lhs[:, m, :], rhs[:, m, :],
                                                   start=True, stop=True)
                        ins.then_inc(banks.full_sem((name, lev, g)), 1)
            for g in ALLG:
                pe.wait_ge(*banks.emptied(("XT", LEVELS_OF[g[0]] - 1, g)))
            for i in (0, 1, "meta"):
                for n_q in range(4):
                    pe.wait_ge(*banks.emptied(("tm", i, n_q)))
            for g in ALLG:
                pe.wait_ge(*banks.emptied(("NT", *g)))
                i, par = g
                n = META if i == "meta" else P
                pe.wait_ge(*banks.take(("NV", g)))
                out = banks.bank(("NV", g))
                for m in range(RM):
                    ins = nc.tensor.matmul(out[0:n, m * RH:(m + 1) * RH], NTm[g][:, m, :],
                                           tmv(i, 3)[:, (2 * m + par) * RH:(2 * m + par + 1) * RH], start=True, stop=True)
                ins.then_inc(banks.full_sem(("NV", g)), 1)
            gate_tile(pe, GATES_AT["NV"])
            for g in ALLG:
                i, par = g
                n = META if i == "meta" else P
                pe.wait_ge(*banks.emptied(("NV", g)))
                pe.wait_ge(*banks.take(("UA", g)))
                out = banks.bank(("UA", g))
                for m in range(RM):
                    hs = slice((2 * m + par) * RH, (2 * m + par + 1) * RH)
                    nc.tensor.matmul(out[0:n, m * P:m * P + RH], Wm[g][:, m, :], NV[g][0:n, m, :], start=True, stop=True)
                    ins = nc.tensor.matmul(out[0:n, m * P + RH:(m + 1) * P], Wm[g][:, m, :], tmv(i, 0)[:, hs],
                                           start=True, stop=True)
                ins.then_inc(banks.full_sem(("UA", g)), 1)
            gate_tile(pe, GATES_AT["UA"])
            for g in ALLG:
                pe.wait_ge(*banks.emptied(("UA", g)))
            for c in range(4):
                i = "meta" if c == 0 else (c - 1) // 2
                lo = 0 if c == 0 else 64 * ((c - 1) % 2)
                r = slice(0, META) if c == 0 else slice(lo, lo + 64)
                pe.wait_ge(*banks.take(("KB", c), 1 if c == 0 else 2))
                out = banks.bank(("KB", c))
                for par in range(2):
                    o = slice(64 * par, 64 * par + 64)
                    for m in range(RM):
                        hs = slice((2 * m + par) * RH, (2 * m + par + 1) * RH)
                        ua = UA[i, par]
                        nc.tensor.matmul(out[o, m * RH:(m + 1) * RH], tmv(i, 2)[r, hs], tmv(i, 3)[r, hs],
                                         start=True, stop=False)
                        ins = nc.tensor.matmul(out[o, m * RH:(m + 1) * RH], tmv(i, 1)[r, hs], ua[r, m, 0:RH],
                                               start=False, stop=True)
                        if c:
                            ins = nc.tensor.matmul(out[o, 256 + m * RH:256 + (m + 1) * RH], ua[r, m, RH:P],
                                                   tmv(i, 1)[r, hs], start=True, stop=True)
                ins.then_inc(banks.full_sem(("KB", c)), 1)
            for i in range(NT):
                for par in range(2):
                    pe.wait_ge(*banks.emptied(("QB", i, par)))
                    pe.wait_ge(*banks.emptied(("QK", i, par)))
                pe.wait_ge(*banks.take(("RQ", i)))
                out = banks.bank(("RQ", i))
                for par in range(2):
                    for m in range(RM):
                        ins = nc.tensor.matmul(out[64 * par:64 * par + 64, m * P:(m + 1) * P], UA[i, par][:, m, RH:P],
                                               QB[i, par][:, m, :], start=True, stop=True)
                ins.then_inc(banks.full_sem(("RQ", i)), 1)
            for c in range(1, 4):
                pe.wait_ge(*banks.emptied(("KB", c)))
                if c == 1:
                    pe.wait_ge(*banks.emptied(("KB", 0)))
                else:
                    if c == 2:
                        gate_tile(pe, GATES_AT["S"])
                    pe.wait_ge(sem("state_ready"), c - 1)
                for par in range(2):
                    r = slice(64 * par, 64 * par + 64)
                    pe.wait_ge(*banks.take(("S", c, par)))
                    out = banks.bank(("S", c, par))
                    for m in range(RM):
                        ins = nc.tensor.matmul(out[r, m * RH:(m + 1) * RH], GT[r, c - 1, m, :], S[r, c - 1, m, :],
                                               start=True, stop=True)
                    ins.then_inc(banks.full_sem(("S", c, par)), 1)
            for i in range(NT):
                pe.wait_ge(*banks.emptied(("RQ", i)))
            pe.wait_ge(sem("state_ready"), 3)
            for i, par in GROUPS:
                r = slice(64 * par, 64 * par + 64)
                pe.wait_ge(*banks.take(("O", i, par)))
                out = banks.bank(("O", i, par))
                for m in range(RM):
                    hs = slice((2 * m + par) * RH, (2 * m + par + 1) * RH)
                    cs = slice(m * RH, (m + 1) * RH)
                    nc.tensor.matmul(out[:, cs], QK[i, par][:, m, :], tmv(i, 3)[:, hs], start=True, stop=False)
                    nc.tensor.matmul(out[:, cs], QB[i, par][:, m, :], UA[i, par][:, m, 0:RH], start=False, stop=True)
                    for c in range(2):
                        ins = nc.tensor.matmul(out[64 * c:64 * c + 64, cs], RQT[r, m, i, 64 * c:64 * c + 64],
                                               S[r, 2 * i + c, m, :], start=False, stop=True, skip_group_check=True)
                ins.then_inc(banks.full_sem(("O", i, par)), 1)
            for j in range(GATES_AT["O"], 16):
                gate_tile(pe, j)
            pe.wait_ge(sem("rwkv_gated"), 1)
            for i in range(NT):
                pe.wait_ge(*banks.take(("oT", i)))
                out = banks.bank(("oT", i))
                for m in range(RM):
                    ins = nc.tensor.transpose(out[:, m * P:(m + 1) * P], otm[:, i * 8 + 2 * m:i * 8 + 2 * m + 2, :].rearrange("p a b -> p (a b)"), ident)
                ins.then_inc(banks.full_sem(("oT", i)), 1)
            for i in range(NT):
                pe.wait_ge(*banks.emptied(("oT", i)))
            branch_out(pe, "rwkv_out", oT)
            tm_out(pe, "w_o", [gates[:, f, :] for f in range(KC)],
                   ready={f: [(sem("mix_ready"), f + 1)] for f in range(KC)})

        def gate_tile(pe, j):
            fm_tile(pe, ("ab", j), ("ab", j), xT[:, :, META:TALL], TOK)

        def tmv(i, q):
            return tmm[0:META, q, :] if i == "meta" else tm[:, i * 4 + q, :]

        def level_bufs(g):
            n = META if g[0] == "meta" else P
            mtl = mm[g, "MTl"] if g[0] == "meta" else MTl4[ALLG.index(g)]
            return mtl[0:n], Tm[g][0:n], Wm[g][0:n], Ym[g][0:n]

        def branch_out(pe, name, x):
            for j in range(4):
                pe.wait_ge(*landed((name, j)))
                w = slot((name, j))
                for s in range(2):
                    pe.wait_ge(*banks.take((name, 2 * j + s)))
                    out = banks.bank((name, 2 * j + s))
                    for c in range(4):
                        at = (s * 4 + c) * P
                        ins = nc.tensor.matmul(out[:, 0:TOK], w[:, at:at + P], x[:, c, :], start=c == 0, stop=c == 3)
                    ins.then_inc(banks.full_sem((name, 2 * j + s)), 1)
                last_use((name, 2 * j + 1))

        def tm_out(pe, name, x, width=D, order=range(KC), ready={}):
            outs = {}
            for n_kc, kc in enumerate(order):
                pe.wait_ge(*landed((name, kc)))
                w = slot((name, kc))
                for wait in ready.get(kc, ()):
                    pe.wait_ge(*wait)
                for i in range(NT):
                    for half in range((width + 511) // 512):
                        if n_kc == 0:
                            pe.wait_ge(*banks.take((name, i, half)))
                            outs[i, half] = banks.bank((name, i, half))
                        hw = min(512, width - 512 * half)
                        ins = nc.tensor.matmul(outs[i, half][:, 0:hw], x[kc][:, i * P:(i + 1) * P],
                                               w[:, 512 * half:512 * half + hw], start=n_kc == 0, stop=n_kc == KC - 1)
                        if n_kc == KC - 1:
                            ins.then_inc(banks.full_sem((name, i, half)), 1)
                if n_kc < KC - 1:
                    ins.then_inc(sem("blocks_used"), 1)
                    last_use_here()
                else:
                    last_use((name, i, half))

        def one_scalar(act):
            act.wait_ge(sem("small_zero"), 1)
            for i in range(NT):
                act.wait_ge(sem(f"h_in_{i}"), 16)
                ins = nc.scalar.activation(hsq[:, :], h[:, i, :], ACT.Square, accum_out=small[:, i:i + 1])
                ins.then_inc(sem("act_step"), 1)
                act.wait_ge(sem("act_step"), i + 1)
            act.wait_ge(sem("meta_in"), 16)
            nc.scalar.activation(hsq[0:META, :], hmeta[0:META, :], ACT.Square,
                                 accum_out=small[0:META, 2:3]).then_inc(sem("in_squares"), 1)
            act.wait_ge(sem("in_rstd"), 1)
            nc.scalar.activation(small[:, 3:6], small[:, 3:6], ACT.Sqrt).then_inc(sem("in_rstd"), 1)
            act.wait_ge(sem("in_rstd"), 2)
            for i in range(NT):
                ins = nc.scalar.activation(hn[:, i, :], h[:, i, :], ACT.Copy, scale=small[:, 3 + i:4 + i])
                ins.then_inc(sem("hn_ready"), 1)
            ins = nc.scalar.activation(hmeta[0:META, :], hmeta[0:META, :], ACT.Copy, scale=small[0:META, 5:6])
            ins.then_inc(sem("hn_ready"), 1)
            act.wait_ge(sem("const_in"), 16)
            act.wait_ge(sem("cols_in"), 16)
            for kc in range(KC):
                act.wait_ge(*banks.full(("xT", kc)))
                out = banks.bank(("xT", kc))
                ins = nc.scalar.activation(xT[:, kc, :], out[:, 0:TALL], ACT.Copy, scale=col("g_mix", kc))
                ins.then_inc(banks.emptied_sem(("xT", kc)), 1)
            for c in range(CT):
                act.wait_ge(*banks.full(("gate", c)))
                out = banks.bank(("gate", c))
                ins = nc.scalar.activation(sgate[:, c, :], out[:, 0:TALL], ACT.Sigmoid)
                ins.then_inc(banks.emptied_sem(("gate", c)), 1)
            for j in range(14):
                act.wait_ge(*banks.full(("z", j)))
                out = banks.bank(("z", j))
                ins = nc.scalar.activation(z[:, j, 1:TALL + 1], out[:, 0:TALL], ACT.Copy)
                ins.then_inc(banks.emptied_sem(("z", j)), 1)
            for j in range(4):
                gate_in(act, j)
            act.wait_ge(*banks.emptied("conv_sum"))
            nc.scalar.activation(sq[:, :, :], ycv[:, :, :], ACT.Square).then_inc(sem("conv_sq"), 1)
            act.wait_ge(sem("shifted"), 14)
            nc.scalar.activation(zs[0:64, 12, :], zs[0:64, 12, :], ACT.Tanh).then_inc(sem("lora_in"), 1)
            nc.scalar.activation(zs[:, 13, META:TALL], zs[:, 13, META:TALL], ACT.Sigmoid).then_inc(sem("lora_in"), 1)
            for m in range(RM):
                act.wait_ge(*banks.full(("decay", m)))
                out = banks.bank(("decay", m))
                ins = nc.scalar.activation(sg[:, m, :], out[:, 0:TALL], ACT.Sigmoid, bias=col("w0", m))
                ins.then_inc(banks.emptied_sem(("decay", m)), 1)
                act.wait_ge(*banks.full(("a", m)))
                out = banks.bank(("a", m))
                ins = nc.scalar.activation(av[:, m, :], out[:, 0:TALL], ACT.Sigmoid, bias=col("a0", m))
                ins.then_inc(banks.emptied_sem(("a", m)), 1)
            for i in range(NT):
                act.wait_ge(*banks.full(("g", i)))
                out = banks.bank(("g", i))
                nc.scalar.activation(gtm[:, i, :], out[:, :], ACT.Copy).then_inc(banks.emptied_sem(("g", i)), 1)
            act.wait_ge(sem("conv_rstd"), 1)
            nc.scalar.activation(sq[:, 0, :], sq[:, 0, :], ACT.Sqrt).then_inc(sem("conv_rstd"), 1)
            act.wait_ge(sem("kk_norm"), 1)
            nc.scalar.activation(E2[:, :, :], E2[:, :, :], ACT.Sqrt).then_inc(sem("kk_norm"), 1)
            act.wait_ge(sem("conv_normal"), 1)
            for c in range(CT):
                nc.scalar.activation(ycv[:, c, :], ycv[:, c, :], ACT.Silu, scale=col("conv_ln_g", c),
                                     bias=col("conv_ln_b", c)).then_inc(sem("conv_out_in"), 1)
            act.wait_ge(sem("cum_ready"), 1)
            act.wait_ge(sem("kk_ready"), 1)
            nc.scalar.activation(E1[:, :, :], cum[:, :, :], ACT.Exp, scale=-DECAY).then_inc(sem("decays"), 1)
            nc.scalar.activation(E2[:, :, :], cum[:, :, :], ACT.Exp, scale=DECAY).then_inc(sem("decays"), 1)
            nc.scalar.activation(E3[:, :, :], sg[:, :, :], ACT.Exp, scale=-DECAY).then_inc(sem("decays"), 1)
            for j in range(4, GATES_AT["NV"]):
                gate_in(act, j)
            for i in (0, 1, "meta"):
                for q in range(4):
                    act.wait_ge(*banks.full(("tm", i, q)))
                    out = banks.bank(("tm", i, q))
                    n = META if i == "meta" else P
                    ins = nc.scalar.activation(tmv(i, q), out[0:n, :], ACT.Copy)
                    ins.then_inc(banks.emptied_sem(("tm", i, q)), 1)
            for g in ALLG:
                n = META if g[0] == "meta" else P
                act.wait_ge(*banks.full(("X", 0, g)))
                out = banks.bank(("X", 0, g))
                nc.scalar.activation(Tm[g][0:n], out[0:n, 0:4 * n].rearrange("p (a b) -> p a b", a=4),
                                     ACT.Copy).then_inc(banks.emptied_sem(("X", 0, g)), 1)
            for lev in range(1, LEVELS):
                for g in ALLG:
                    if lev >= LEVELS_OF[g[0]]:
                        continue
                    n = META if g[0] == "meta" else P
                    act.wait_ge(*banks.full(("Y", lev, g)))
                    out = banks.bank(("Y", lev, g))
                    nc.scalar.activation(Ym[g][0:n], out[0:n, 0:4 * n].rearrange("p (a b) -> p a b", a=4),
                                         ACT.Copy).then_inc(banks.emptied_sem(("Y", lev, g)), 1)
            for g in ALLG:
                n = META if g[0] == "meta" else P
                act.wait_ge(*banks.full(("NV", g)))
                out = banks.bank(("NV", g))
                nc.scalar.activation(NV[g][0:n], out[0:n, 0:256].rearrange("p (a b) -> p a b", a=4),
                                     ACT.Copy).then_inc(banks.emptied_sem(("NV", g)), 1)
            gate_in(act, GATES_AT["NV"])
            for g in ALLG:
                n = META if g[0] == "meta" else P
                act.wait_ge(*banks.full(("UA", g)))
                out = banks.bank(("UA", g))
                nc.scalar.activation(UA[g][0:n], out[0:n, :].rearrange("p (a b) -> p a b", a=4),
                                     ACT.Copy).then_inc(banks.emptied_sem(("UA", g)), 1)
            gate_in(act, GATES_AT["UA"])
            gate_in(act, GATES_AT["S"])
            for i, par in GROUPS:
                act.wait_ge(*banks.full(("O", i, par)))
                out = banks.bank(("O", i, par))
                to = otm[:, i * 8:(i + 1) * 8, :].rearrange("p (m two) v -> p m two v", two=2)[:, :, par, :]
                ins = nc.scalar.activation(to, out[:, 0:256].rearrange("p (a b) -> p a b", a=4), ACT.Copy)
                ins.then_inc(banks.emptied_sem(("O", i, par)), 1)
            for j in range(GATES_AT["O"], 16):
                gate_in(act, j)
            act.wait_ge(sem("gn_rstd"), 1)
            nc.scalar.activation(small[:, 16:32], small[:, 16:32], ACT.Sqrt).then_inc(sem("gn_rstd"), 1)
            for i in range(NT):
                act.wait_ge(*banks.full(("oT", i)))
                out = banks.bank(("oT", i))
                nc.scalar.activation(oT[:, :, i * P:(i + 1) * P], out[:, :].rearrange("p (a b) -> p a b", a=4),
                                     ACT.Copy).then_inc(banks.emptied_sem(("oT", i)), 1)

        def gate_in(act, j):
            act.wait_ge(*banks.full(("ab", j)))
            out = banks.bank(("ab", j))
            nc.scalar.activation(gates[:, j, :], out[:, 0:TOK], ACT.Sigmoid).then_inc(banks.emptied_sem(("ab", j)), 1)

        def one_vector(v):
            V = nc.vector
            for b in range(NB):
                V.memset(cum[:, 0, b:b + 1], 0.0).then_inc(sem(f"emptied_{b}"), 1)
            V.memset(small[:, :], 0.0).then_inc(sem("small_zero"), 1)
            v.wait_ge(sem("small_zero"), 1)
            V.memset(z[:, :, 0:1], 0.0).then_inc(sem("zeros"), 1)
            V.memset(u[:, :, 0:TAPS - 1], 0.0).then_inc(sem("zeros"), 1)
            v.wait_ge(sem("in_squares"), 1)
            ins = V.tensor_scalar(small[:, 3:6], small[:, 0:3], 1.0 / D, 1e-6, ALU.mult, ALU.add)
            ins.then_inc(sem("dve_step"), 1)
            v.wait_ge(sem("dve_step"), count("dve_step"))
            V.reciprocal(small[:, 3:6], small[:, 3:6]).then_inc(sem("in_rstd"), 1)
            v.wait_ge(sem("const_in"), 16)
            v.wait_ge(sem("cols_in"), 16)
            v.wait_ge(sem("l1const_in"), 16)
            for m in range(RM):
                ins = V.tensor_scalar(rksel[:, m, :], onehead[:, m, :], col("r_k", m), None, ALU.mult)
            ins.then_inc(sem("rksel_ready"), 1)
            v.wait_ge(sem("zeros"), 2)
            for c in range(CT):
                v.wait_ge(*banks.emptied(("gate", c)))
                v.wait_ge(*banks.full(("val", c)))
                out = banks.bank(("val", c))
                ins = V.tensor_tensor(u[:, c, TAPS - 1:], out[:, 0:TALL], sgate[:, c, :], ALU.mult)
                ins.then_inc(banks.emptied_sem(("val", c)), 1)
            w0 = COLS["conv_w"][0]
            for c in range(CT):
                v.wait_ge(*banks.emptied(("val", c)))
                V.tensor_scalar(ycv[:, c, :], u[:, c, META:META + TOK], cols[:, w0 + c:w0 + c + 1],
                                col("conv_b", c), ALU.mult, ALU.add).then_inc(sem("conv_tap"), 1)
            with v.Fori(1, TAPS) as tap:
                for c in range(CT):
                    v.wait_ge(sem("conv_tap"), tap * CT - (CT - 1 - c))
                    V.scalar_tensor_tensor(ycv[:, c, :], u[:, c, bass.ds(tap + META, TOK)],
                                           cols[:, bass.ds(tap * CT + (w0 + c), 1)], ycv[:, c, :],
                                           ALU.mult, ALU.add).then_inc(sem("conv_tap"), 1)
            v.wait_ge(sem("conv_tap"), CT * TAPS)
            v.wait_ge(*banks.full("conv_sum"))
            out = banks.bank("conv_sum")
            ins = V.scalar_tensor_tensor(ycv[:, :, :], bc(out[:, 0:TOK], (0, CT), (1, TOK)), -1.0 / CONV_C,
                                         ycv[:, :, :], ALU.mult, ALU.add)
            ins.then_inc(banks.emptied_sem("conv_sum"), 1)
            for j in range(14):
                v.wait_ge(*banks.emptied(("z", j)))
            ins = V.tensor_tensor(zs[:, :, :], z[:, :, 0:TALL], z[:, :, 1:TALL + 1], ALU.subtract)
            ins.then_inc(sem("dve_step"), 1)
            v.wait_ge(sem("dve_step"), count("dve_step"))
            for j in range(14):
                V.scalar_tensor_tensor(zs[:, j, :], zs[:, j, :], col("mu", j), z[:, j, 1:TALL + 1],
                                       ALU.mult, ALU.add).then_inc(sem("shifted"), 1)
            v.wait_ge(sem("shifted"), 14)
            for m in range(RM):
                ins = V.tensor_scalar(kk[:, m, :], zs[:, 4 + m, :], col("k_k", m), None, ALU.mult)
                ins.then_inc(sem("dve_step"), 1)
                v.wait_ge(sem("dve_step"), count("dve_step"))
            V.tensor_tensor(E1[:, :, :], kk[:, :, :], kk[:, :, :], ALU.mult).then_inc(sem("kk_sq"), 1)
            v.wait_ge(*banks.full("conv_var"))
            out = banks.bank("conv_var")
            ins = V.tensor_scalar(sq[:, 0, :], out[:, 0:TOK], 1.0 / CONV_C, 1e-5, ALU.mult, ALU.add)
            ins.then_inc(banks.emptied_sem("conv_var"), 1)
            v.wait_ge(*banks.emptied("conv_var"))
            V.reciprocal(sq[:, 0, :], sq[:, 0, :]).then_inc(sem("conv_rstd"), 1)
            for m in range(RM):
                v.wait_ge(*banks.full(("kk_sum", m)))
                out = banks.bank(("kk_sum", m))
                ins = V.tensor_scalar(E2[:, m, :], out[:, 0:TALL], 1e-24, None, ALU.max)
                ins.then_inc(banks.emptied_sem(("kk_sum", m)), 1)
            for m in range(RM):
                v.wait_ge(*banks.emptied(("kk_sum", m)))
            V.reciprocal(E2[:, :, :], E2[:, :, :]).then_inc(sem("kk_norm"), 1)
            for m in range(RM):
                v.wait_ge(*banks.emptied(("decay", m)))
                v.wait_ge(*banks.emptied(("a", m)))
                ins = V.tensor_tensor_scan(cum[:, m, :], k("scan_all"), sg[:, m, :], 0.0, ALU.mult, ALU.add)
                ins.then_inc(sem("dve_step"), 1)
                v.wait_ge(sem("dve_step"), count("dve_step"))
            V.tensor_tensor(sg[:, :, :], cum[:, :, :], sg[:, :, :], ALU.subtract).then_inc(sem("cum_ready"), 1)
            v.wait_ge(sem("conv_rstd"), 2)
            ins = V.tensor_tensor(ycv[:, :, :], ycv[:, :, :], bc(sq[:, 0, :], (0, CT), (1, TOK)), ALU.mult)
            ins.then_inc(sem("conv_normal"), 1)
            for m in range(RM):
                ins = V.tensor_scalar(kp[:, m, :], av[:, m, :], -1.0, col("k_a", m), ALU.add, ALU.mult)
                ins.then_inc(sem("dve_step"), 1)
                v.wait_ge(sem("dve_step"), count("dve_step"))
            ins = V.scalar_tensor_tensor(kp[:, :, :], kp[:, :, :], 1.0, zs[:, 4:8, :], ALU.add, ALU.mult)
            ins.then_inc(sem("dve_step"), 1)
            v.wait_ge(sem("dve_step"), count("dve_step"))
            V.tensor_tensor(tt[:, :, :], kp[:, :, :], zs[:, 0:4, :], ALU.mult).then_inc(sem("rkr_ready"), 1)
            v.wait_ge(sem("kk_norm"), 2)
            V.tensor_tensor(kk[:, :, :], kk[:, :, :], E2[:, :, :], ALU.mult).then_inc(sem("kk_ready"), 1)
            v.wait_ge(sem("kk_ready"), 1)
            V.tensor_tensor(av[:, :, :], av[:, :, :], kk[:, :, :], ALU.mult).then_inc(sem("dve_step"), 1)
            v.wait_ge(sem("dve_step"), count("dve_step"))
            v.wait_ge(sem("decays"), 3)
            V.tensor_tensor(alpha[:, :, :], kk[:, :, :], E3[:, :, :], ALU.mult)
            V.scalar_tensor_tensor(beta[:, :, :], av[:, :, :], -1.0, E2[:, :, :], ALU.mult, ALU.mult)
            V.tensor_tensor(kappa[:, :, :], kp[:, :, :], E2[:, :, :], ALU.mult)
            V.tensor_tensor(rho[:, :, :], zs[:, 0:4, :], E1[:, :, :], ALU.mult).then_inc(sem("dve_step"), 1)
            v.wait_ge(sem("dve_step"), count("dve_step"))
            for c in range(5):
                at = META - 1 + c * CH
                ins = V.tensor_copy(pend[:, c, :], E1[:, :, at])
            ins.then_inc(sem("abkr_ready"), 1)
            branch_in(v, "conv_out", 0)
            for i in range(NT):
                v.wait_ge(*banks.full(("bonus", i)))
                out = banks.bank(("bonus", i))
                ins = V.tensor_copy(small[:, 32 + 8 * i:40 + 8 * i], out[:, 0:8])
                ins.then_inc(banks.emptied_sem(("bonus", i)), 1)
            for n_g, g in enumerate(ALLG):
                n = META if g[0] == "meta" else P
                for name, to, mask in (("MT", MT, "strict"), ("NT", NTm, "strict"), ("QK", QK, "incl"), ("QB", QB, "incl")):
                    if g[0] == "meta" and name[0] == "Q":
                        continue
                    v.wait_ge(*banks.full((name, *g)))
                    out = banks.bank((name, *g))
                    ins = V.tensor_tensor(to[g][0:n], out[0:n, 0:4 * n].rearrange("p (a b) -> p a b", a=4),
                                          bc(k(mask)[0:n, 0:n], (0, 4), (1, n)), ALU.mult)
                    ins.then_inc(banks.emptied_sem((name, *g)), 1)
            for g in ALLG:
                n = META if g[0] == "meta" else P
                v.wait_ge(sem("joins_ready"), JOINS[0, g])
                V.tensor_tensor(Wm[g][0:n], level_bufs(g)[0], bc(ident[0:n, 0:n], (0, 4), (1, n)),
                                ALU.add).then_inc(sem("first_joined"), 1)
            v.wait_ge(sem("first_joined"), len(ALLG))
            for lev in range(1, LEVELS):
                for g in ALLG:
                    if lev >= LEVELS_OF[g[0]]:
                        continue
                    n = META if g[0] == "meta" else P
                    for name, t in (("X", Tm), ("XT", Wm)):
                        if name == "X" and lev == LEVELS_OF[g[0]] - 1:
                            continue
                        v.wait_ge(*banks.full((name, lev, g)))
                        out = banks.bank((name, lev, g))
                        if name == "X" or lev > 1:
                            v.wait_ge(*banks.emptied((name, lev - 1, g)))
                        ins = V.tensor_tensor(t[g][0:n], t[g][0:n],
                                              out[0:n, 0:4 * n].rearrange("p (a b) -> p a b", a=4), ALU.add)
                        ins.then_inc(banks.emptied_sem((name, lev, g)), 1)
            v.wait_ge(*banks.full(("KB", 0)))
            out = banks.bank(("KB", 0))
            ins = V.tensor_tensor(S[:, 0, :, :], out[:, 0:256].rearrange("p (a b) -> p a b", a=4),
                                  bc(pend[:, 0, :], (1, 4), (0, RH)), ALU.mult)
            ins.then_inc(banks.emptied_sem(("KB", 0)), 1)
            for c in range(1, 4):
                v.wait_ge(*banks.full(("KB", c)))
                out = banks.bank(("KB", c))
                ins = V.tensor_copy(KB[:, c, :, :], out[:, 0:256].rearrange("p (a b) -> p a b", a=4))
                ins.then_inc(banks.emptied_sem(("KB", c)), 1)
                ins = V.tensor_tensor(GT[:, c - 1, :, :], out[:, 256:512].rearrange("p (a b) -> p a b", a=4),
                                      bc(k("ident2"), (0, 4), (1, 64)), ALU.add)
                ins.then_inc(banks.emptied_sem(("KB", c)), 1)
            for i in range(NT):
                v.wait_ge(*banks.full(("RQ", i)))
                out = banks.bank(("RQ", i))
                ins = V.tensor_tensor(RQT[:, :, i, :], out[:, :].rearrange("p (a b) -> p a b", a=4),
                                      rho[:, :, META + i * P:META + (i + 1) * P], ALU.add)
                ins.then_inc(banks.emptied_sem(("RQ", i)), 1)
            for c in range(1, 4):
                v.wait_ge(*banks.emptied(("KB", c)))
                for par in range(2):
                    r = slice(64 * par, 64 * par + 64)
                    v.wait_ge(*banks.full(("S", c, par)))
                    out = banks.bank(("S", c, par))
                    ins = V.tensor_tensor(S[r, c, :, :], out[r, 0:256].rearrange("p (a b) -> p a b", a=4), KB[r, c, :, :],
                                          ALU.add)
                    ins.then_inc(banks.emptied_sem(("S", c, par)), 1)
                    v.wait_ge(*banks.emptied(("S", c, par)))
                ins = V.tensor_tensor(S[:, c, :, :], S[:, c, :, :], bc(pend[:, c, :], (1, 4), (0, RH)), ALU.mult)
                ins.then_inc(sem("state_ready"), 1)
            for i, par in GROUPS:
                v.wait_ge(*banks.emptied(("O", i, par)))
            V.tensor_reduce(small[:, 16:32], otm[:, :, :], AX.X, ALU.add).then_inc(sem("dve_step"), 1)
            v.wait_ge(sem("dve_step"), count("dve_step"))
            V.tensor_scalar(small[:, 16:32], small[:, 16:32], 1.0 / RH, None, ALU.mult).then_inc(sem("dve_step"), 1)
            v.wait_ge(sem("dve_step"), count("dve_step"))
            ins = V.tensor_tensor(otm[:, :, :], otm[:, :, :], bc(small[:, 16:32], (1, 16), (0, RH)), ALU.subtract)
            ins.then_inc(sem("dve_step"), 1)
            v.wait_ge(sem("dve_step"), count("dve_step"))
            V.tensor_tensor(otmp[:, :, :], otm[:, :, :], otm[:, :, :], ALU.mult).then_inc(sem("dve_step"), 1)
            v.wait_ge(sem("dve_step"), count("dve_step"))
            V.tensor_reduce(small[:, 16:32], otmp[:, :, :], AX.X, ALU.add).then_inc(sem("dve_step"), 1)
            v.wait_ge(sem("dve_step"), count("dve_step"))
            ins = V.tensor_scalar(small[:, 16:32], small[:, 16:32], 1.0 / RH, 64e-5, ALU.mult, ALU.add)
            ins.then_inc(sem("dve_step"), 1)
            v.wait_ge(sem("dve_step"), count("dve_step"))
            V.reciprocal(small[:, 16:32], small[:, 16:32]).then_inc(sem("gn_rstd"), 1)
            for i in range(NT):
                v.wait_ge(*banks.emptied(("bonus", i)))
            for i in range(NT):
                ins = V.tensor_tensor(otmp[:, i * 8:(i + 1) * 8, :], bc(tmv(i, 3), (64, 8), (1, 64)),
                                      bc(small[:, 32 + 8 * i:40 + 8 * i], (1, 8), (0, RH)), ALU.mult)
            ins.then_inc(sem("dve_step"), 1)
            v.wait_ge(sem("dve_step"), count("dve_step"))
            v.wait_ge(sem("gn_rstd"), 2)
            ins = V.tensor_tensor(otm[:, :, :], otm[:, :, :], bc(small[:, 16:32], (1, 16), (0, RH)), ALU.mult)
            ins.then_inc(sem("dve_step"), 1)
            v.wait_ge(sem("dve_step"), count("dve_step"))
            v.wait_ge(sem("rows_in_0"), 16)
            halves = otm.rearrange("p (i a) b -> p i (a b)", i=NT)
            ins = V.tensor_tensor(halves, halves, bc(rows[:, 0, 0:RW], (0, NT), (1, RW)), ALU.mult)
            ins.then_inc(sem("dve_step"), 1)
            v.wait_ge(sem("dve_step"), count("dve_step"))
            ins = V.tensor_tensor(halves, halves, bc(rows[:, 0, RW:2 * RW], (0, NT), (1, RW)), ALU.add)
            ins.then_inc(sem("dve_step"), 1)
            v.wait_ge(sem("dve_step"), count("dve_step"))
            V.tensor_tensor(otm[:, :, :], otm[:, :, :], otmp[:, :, :], ALU.add).then_inc(sem("dve_step"), 1)
            v.wait_ge(sem("dve_step"), count("dve_step"))
            V.tensor_tensor(halves, halves, gtm[:, :, :], ALU.mult).then_inc(sem("rwkv_gated"), 1)
            branch_in(v, "rwkv_out", 8)
            for f in range(KC):
                v.wait_ge(*banks.emptied(("rwkv_out", f)))
                ins = V.tensor_tensor(gates[:, f, :], gates[:, f, :], gates[:, 8 + f, :], ALU.add)
                ins.then_inc(sem("mix_ready"), 1)
            mixed_vector(v, "w_o", 0, 1.0)

        def branch_in(v, name, at):
            for f in range(KC):
                v.wait_ge(*banks.emptied(("ab", at + f)))
                v.wait_ge(*banks.full((name, f)))
                out = banks.bank((name, f))
                ins = nc.vector.tensor_tensor(gates[:, at + f, :], out[:, 0:TOK], gates[:, at + f, :], ALU.mult)
                ins.then_inc(banks.emptied_sem((name, f)), 1)

        def residual_in(v, name, i, alpha_):
            for half in range(2):
                v.wait_ge(*banks.full((name, i, half)))
                out = banks.bank((name, i, half))
                hs = h[:, i, half * 512:(half + 1) * 512]
                ins = nc.vector.scalar_tensor_tensor(hs, hs, alpha_, out[:, :], ALU.mult, ALU.add)
                ins.then_inc(banks.emptied_sem((name, i, half)), 1)

        def one_gpsimd(pool):
            pool.wait_ge(sem("l1const_in"), 16)
            for (lev, g), n_join in JOINS.items():
                n = META if g[0] == "meta" else P
                if lev == 0:
                    pool.wait_ge(*banks.emptied(("MT", *g)))
                elif lev == 1:
                    pool.wait_ge(sem("first_joined"), ALLG.index(g) + 1)
                else:
                    pool.wait_ge(*banks.full(("Y", lev - 1, g)))
                ins = nc.gpsimd.tensor_tensor(level_bufs(g)[0], MT[g][0:n], bc(levels[0:n, lev, 0:n], (0, 4), (1, n)),
                                              ALU.mult)
                ins.then_inc(sem("joins_ready"), 1)

        def one_sync(sp):
            x = io["x"].rearrange("(i p) d -> i p d", p=P)
            for i in range(NT):
                sp.dma_start(h[:, i, :], x[i]).then_inc(sem(f"h_in_{i}"), 16)
            sp.dma_start(hmeta[0:META, :], io["meta"]).then_inc(sem("meta_in"), 16)
            sp.dma_start(const[:, :], io["const"][:, 0:NCONST_KEEP]).then_inc(sem("const_in"), 16)
            sp.dma_start(cols[:, :], io["cols"]).then_inc(sem("cols_in"), 16)
            at = CONST["onehead"][0]
            l1 = arena_t[:, L1C:L1C + NCONST - at]
            sp.dma_start(l1, io["const"][:, at:NCONST]).then_inc(sem("l1const_in"), 16)
            sp.dma_start(rows[:, 0, :], io["gn_rows"].partition_broadcast(P)).then_inc(sem("rows_in_0"), 16)
            load_row(sp, 1, 0)

        def squares(act, n, i):
            if n > 1:
                act.wait_ge(sem("ln_mean"), NT * (n - 2) + i + 1)
            kw = {"bias": small[:, 4 + i:5 + i]} if n > 1 else {}
            ins = nc.scalar.activation(actjunk, h[:, i, :], ACT.Square, accum_out=small[:, i:i + 1], **kw)
            ins.then_inc(sem("squares"), 1)
            act.wait_ge(sem("squares"), n * NT + i + 1)

        def root(act, n, i):
            act.wait_ge(sem("norm_var"), 2 * (NT * n + i) + 1)
            nc.scalar.activation(small[:, 2 + i:3 + i], small[:, 2 + i:3 + i], ACT.Sqrt).then_inc(sem("norm_var"), 1)

        def mean(v, n, i):
            nc.vector.tensor_reduce(small[:, 4 + i:5 + i], h[:, i, :], AX.X, ALU.add).then_inc(sem("dve_step"), 1)
            v.wait_ge(sem("dve_step"), count("dve_step"))
            nc.vector.tensor_scalar(small[:, 4 + i:5 + i], small[:, 4 + i:5 + i], -1.0 / D, None,
                                    ALU.mult).then_inc(sem("ln_mean"), 1)
            v.wait_ge(sem("ln_mean"), NT * (n - 2) + i + 1)

        def variance(v, n, i):
            v.wait_ge(sem("squares"), NT * n + i + 1)
            ins = nc.vector.tensor_scalar(small[:, 2 + i:3 + i], small[:, i:i + 1], 1.0 / D, 1e-5 if n > 1 else 1e-6,
                                          ALU.mult, ALU.add)
            ins.then_inc(sem("dve_step"), 1)
            v.wait_ge(sem("dve_step"), count("dve_step"))
            if n or i:
                v.wait_ge(sem("norm_var"), 2 * (NT * n + i))
            nc.vector.reciprocal(small[:, 2 + i:3 + i], small[:, 2 + i:3 + i]).then_inc(sem("norm_var"), 1)

        def rms_apply(v, n, i, to, row):
            variance(v, n, i)
            v.wait_ge(sem("norm_var"), 2 * (NT * n + i) + 2)
            ins = nc.vector.scalar_tensor_tensor(to[:, i, :], h[:, i, :], small[:, 2 + i:3 + i], row, ALU.mult, ALU.mult)
            ins.then_inc(sem("normed"), 1)

        def ln_apply(v, n, i):
            variance(v, n, i)
            v.wait_ge(sem("rows_in_1"), 16 * n)
            ins = nc.vector.scalar_tensor_tensor(h[:, i, :], h[:, i, :], small[:, 4 + i:5 + i], rows[:, 1, :],
                                                 ALU.add, ALU.mult)
            ins.then_inc(sem("dve_step"), 1)
            v.wait_ge(sem("dve_step"), count("dve_step"))
            v.wait_ge(sem("norm_var"), 2 * (NT * n + i) + 2)
            v.wait_ge(sem("rows_in_0"), 16 * (n + 1))
            nc.vector.scalar_tensor_tensor(h[:, i, :], h[:, i, :], small[:, 2 + i:3 + i], rows[:, 0, :],
                                           ALU.mult, ALU.add).then_inc(sem("normed"), 1)

        def fm_tensor(pe, n, i, src):
            pe.wait_ge(sem("normed"), NT * n + i + 1)
            for half in range(2):
                pe.wait_ge(*banks.take(("xT", n, i, half)))
                out = banks.bank(("xT", n, i, half))
                for j in range(4):
                    kc = 4 * half + j
                    ins = nc.tensor.transpose(out[:, j * P:(j + 1) * P], src[:, i, kc * P:(kc + 1) * P], ident)
                ins.then_inc(banks.full_sem(("xT", n, i, half)), 1)

        def fm_wait(pe, n):
            for i in range(NT):
                for half in range(2):
                    pe.wait_ge(*banks.emptied(("xT", n, i, half)))

        def fm_scalar(act, n, i):
            for half in range(2):
                act.wait_ge(*banks.full(("xT", n, i, half)))
                out = banks.bank(("xT", n, i, half))
                ins = nc.scalar.activation(xT[:, 4 * half:4 * half + 4, i * P:(i + 1) * P],
                                           out[:, :].rearrange("p (a b) -> p a b", a=4), ACT.Copy)
                ins.then_inc(banks.emptied_sem(("xT", n, i, half)), 1)

        def mixed_vector(v, name, n, alpha_):
            for i in range(NT):
                residual_in(v, name, i, alpha_)
                for half in range(2):
                    v.wait_ge(*banks.emptied((name, i, half)))
                if n:
                    mean(v, n, i)
            for i in range(NT):
                if n == 0:
                    v.wait_ge(sem("rows_in_1"), 16)
                    rms_apply(v, n, i, xn, rows[:, 1, :])
                else:
                    ln_apply(v, n, i)

        def mixed_scalar(act, name, n):
            for i in range(NT):
                for half in range(2):
                    act.wait_ge(*banks.emptied((name, i, half)))
                squares(act, n, i)
            for i in range(NT):
                root(act, n, i)
            for i in range(NT):
                fm_scalar(act, n, i)

        def mixed_tensor(pe, n):
            for i in range(NT):
                fm_tensor(pe, n, i, h if n else xn)
            fm_wait(pe, n)

        def experts_vector(v, n, i):
            ins = nc.vector.scalar_tensor_tensor(h[:, i, :], h[:, i, :], 1.0 if n == 1 else ALPHA,
                                                 ysum[:, i * D:(i + 1) * D], ALU.mult, ALU.add)
            ins.then_inc(sem("peer_added"), 1)
            v.wait_ge(sem("peer_added"), count("peer_added"))
            if n == 1:
                v.wait_ge(sem("rows_in_0"), 32)
                rms_apply(v, n, i, h, rows[:, 0, :])
            else:
                mean(v, n, i)
                ln_apply(v, n, i)

        def experts_scalar(act, n, i):
            if n == 1:
                act.wait_ge(sem("peer_added"), i + 1)
            squares(act, n, i)
            root(act, n, i)

        UNITS = NT * PH
        G = Arena(arena_t, ARENA)
        ring_u, ring_v = G.take(RING, D), G.take(RING, D)
        scores = G.take((UNITS + 1) * 2 * NKEYS)
        qT = G.take(16, TOK)
        xn = G.take(NT, D)
        ysum = G.take(NT * D)
        actjunk = G.take(D)
        diag = G.take(PK, P)
        sc, sc2 = G.take(2, NKEYS), G.take(2, NKEYS)
        cand, cand2, eq = (G.take(PK, PK) for _ in range(3))
        top, topi, posf = (G.take(2, PK) for _ in range(3))
        best, expo, gate, dots, actv, coef, e1, e2 = (G.take(PK) for _ in range(8))
        tiny = G.take(4)

        def peer_scores_tensor(pe, n):
            for lo, hi in Q_GROUPS:
                for j in range(lo, hi):
                    fm_tile(pe, ("q", n, j), ("w_q", n, j), xT[:, :, 0:TOK], TOK)
                pe.wait_ge(*landed(("keys", n, lo)))
                w = slot(("keys", n, lo))
                for j in range(lo, hi):
                    pe.wait_ge(*banks.emptied(("q", n, j)))
                for i in range(NT):
                    pe.wait_ge(*banks.take(("score", n, lo, i)))
                    out = banks.bank(("score", n, lo, i))
                    for x in range(hi - lo):
                        ins = nc.tensor.matmul(out[:, x * P:(x + 1) * P], qT[:, lo + x, i * P:(i + 1) * P],
                                               w[:, x * P:(x + 1) * P], start=True, stop=True)
                    ins.then_inc(banks.full_sem(("score", n, lo, i)), 1)
                last_use(("score", n, lo, NT - 1))

        def peer_scores_scalar(act, n):
            for lo, hi in Q_GROUPS:
                for j in range(lo, hi):
                    act.wait_ge(*banks.full(("q", n, j)))
                    out = banks.bank(("q", n, j))
                    nc.scalar.activation(qT[:, j, :], out[:, 0:TOK], ACT.Copy).then_inc(
                        banks.emptied_sem(("q", n, j)), 1)
                for i in range(NT):
                    act.wait_ge(*banks.full(("score", n, lo, i)))
                    out = banks.bank(("score", n, lo, i))
                    at = i * PH * 2 * NKEYS + lo * NKEYS
                    nc.scalar.activation(scores[:, at:at + (hi - lo) * P], out[:, 0:(hi - lo) * P], ACT.Copy).then_inc(
                        banks.emptied_sem(("score", n, lo, i)), 1)
                if lo == 0:
                    act.wait_ge(*banks.emptied(("score", n, lo, 0)))
                    copy_scores(act, n, 0)
                if lo == 2:
                    act.wait_ge(*banks.emptied(("score", n, lo, 0)))
                    copy_scores(act, n, 1)
                    softmax_exp(act, n * UNITS)
            act.wait_ge(sem("pad_zero"), n + 1)
            for lo, hi in Q_GROUPS:
                for i in range(NT):
                    act.wait_ge(*banks.emptied(("score", n, lo, i)))

        def copy_scores(act, n, unit):
            if type(unit) is int and unit == 0:
                if n:
                    act.wait_ge(sem("sc_in"), n * (UNITS + 1))
            else:
                act.wait_ge(sem("sc_read"), unit + n * UNITS)
            nc.scalar.activation(sc[:, :, :], scores[:, bass.ds(unit * 2 * NKEYS, 2 * NKEYS)].rearrange(
                "p (a b) -> p a b", a=2), ACT.Copy).then_inc(sem("sc_in"), 1)

        class Steps:

            def __init__(self, base):
                self.base, self.n = base, 0

            def __call__(self):
                self.n += 1
                return self.base + self.n

        TOPK_STEPS = 25

        def topk_find(v, step, n, unit):
            V = nc.vector
            v.wait_ge(sem("sc_in"), unit + (n * (UNITS + 1) + 1))
            v.sem_inc(sem("waits_passed"), 1)
            for c in range(2):
                V.max(out=top[:, c, 0:8], in_=sc[:, c, :]).then_inc(sem("topk_step"), 1)
                v.wait_ge(sem("topk_step"), step())
                v.sem_inc(sem("waits_passed"), 1)
                ins = V.max_index(out=idx_best[:, c, 0:8], in_max=top[:, c, 0:8], in_values=sc[:, c, :])
                ins.then_inc(sem("topk_step"), 1)
                v.wait_ge(sem("topk_step"), step())
                v.sem_inc(sem("waits_passed"), 1)
                V.match_replace(out=sc2[:, c, :], in_to_replace=top[:, c, 0:8], in_values=sc[:, c, :],
                                imm_value=-3.0e38).then_inc(sem("topk_step"), 1)
                v.wait_ge(sem("topk_step"), step())
                v.sem_inc(sem("waits_passed"), 1)
                V.max(out=top[:, c, 8:16], in_=sc2[:, c, :]).then_inc(sem("topk_step"), 1)
                v.wait_ge(sem("topk_step"), step())
                v.sem_inc(sem("waits_passed"), 1)
                ins = V.max_index(out=idx_best[:, c, 8:16], in_max=top[:, c, 8:16], in_values=sc2[:, c, :])
                if c == 0:
                    ins.then_inc(sem("topk_step"), 1)
                    v.wait_ge(sem("topk_step"), step())
                    v.sem_inc(sem("waits_passed"), 1)
            ins.then_inc(sem("sc_read"), 1)
            v.wait_ge(sem("sc_read"), unit + (n * UNITS + 1))
            v.sem_inc(sem("waits_passed"), 1)
            V.tensor_copy(topi[:, :, :], idx_best[:, :, :])
            flat, flat2 = cand.rearrange("p a b -> p (a b)"), cand2.rearrange("p a b -> p (a b)")
            ins = V.tensor_tensor(cand[:, :, :], bc(top[:, 0, :], (1, PK), (0, PK)), bc(top[:, 1, :], (0, PK), (1, PK)), ALU.add)
            ins.then_inc(sem("topk_step"), 1)
            v.wait_ge(sem("topk_step"), step())
            v.sem_inc(sem("waits_passed"), 1)
            V.max(out=best[:, 0:8], in_=flat).then_inc(sem("topk_step"), 1)
            v.wait_ge(sem("topk_step"), step())
            v.sem_inc(sem("waits_passed"), 1)
            V.max_index(out=idx_pos[:, 0, 0:8], in_max=best[:, 0:8], in_values=flat).then_inc(sem("topk_step"), 1)
            v.wait_ge(sem("topk_step"), step())
            v.sem_inc(sem("waits_passed"), 1)
            ins = V.match_replace(out=flat2, in_to_replace=best[:, 0:8], in_values=flat, imm_value=-3.0e38)
            ins.then_inc(sem("topk_step"), 1)
            v.wait_ge(sem("topk_step"), step())
            v.sem_inc(sem("waits_passed"), 1)
            V.max(out=best[:, 8:16], in_=flat2).then_inc(sem("topk_step"), 1)
            v.wait_ge(sem("topk_step"), step())
            v.sem_inc(sem("waits_passed"), 1)
            V.max_index(out=idx_pos[:, 0, 8:16], in_max=best[:, 8:16], in_values=flat2).then_inc(sem("topk_step"), 1)
            v.wait_ge(sem("topk_step"), step())
            v.sem_inc(sem("waits_passed"), 1)
            V.tensor_scalar(tiny[:, 0:1], best[:, 0:1], -1.0, None, ALU.mult).then_inc(sem("best_found"), 1)

        def topk_numbers(v, step, n, unit):
            V = nc.vector
            V.tensor_scalar(idx_pos[:, 1, :], idx_pos[:, 0, :], 4, None, ALU.logical_shift_right)
            ins = V.tensor_scalar(idx_pos[:, 2, :], idx_pos[:, 0, :], 15, None, ALU.bitwise_and)
            ins.then_inc(sem("topk_step"), 1)
            v.wait_ge(sem("topk_step"), step())
            v.sem_inc(sem("waits_passed"), 1)
            V.tensor_copy(posf[:, :, :], idx_pos[:, 1:3, :]).then_inc(sem("topk_step"), 1)
            v.wait_ge(sem("topk_step"), step())
            v.sem_inc(sem("waits_passed"), 1)
            for c, e in ((0, e1), (1, e2)):
                V.tensor_tensor(eq[:, :, :], bc(posf[:, c, :], (1, PK), (0, PK)), bc(k("iota"), (0, PK), (1, PK)),
                                ALU.is_equal).then_inc(sem("topk_step"), 1)
                v.wait_ge(sem("topk_step"), step())
                v.sem_inc(sem("waits_passed"), 1)
                ins = V.tensor_tensor(eq[:, :, :], eq[:, :, :], bc(topi[:, c, :], (0, PK), (1, PK)), ALU.mult)
                ins.then_inc(sem("topk_step"), 1)
                v.wait_ge(sem("topk_step"), step())
                v.sem_inc(sem("waits_passed"), 1)
                V.tensor_reduce(e, eq[:, :, :], AX.X, ALU.add).then_inc(sem("topk_step"), 1)
                v.wait_ge(sem("topk_step"), step())
                v.sem_inc(sem("waits_passed"), 1)
            if type(unit) is not int or unit + n:
                v.wait_ge(sem("idx_taken"), unit + n * UNITS)
            V.scalar_tensor_tensor(idx_next[:, :], e1, float(NKEYS), e2, ALU.mult, ALU.add).then_inc(sem("topk_done"), 1)

        def topk_gate(v, step, n, unit):
            V = nc.vector
            v.wait_ge(sem("exp_done"), unit + (n * UNITS + 1))
            V.reciprocal(tiny[:, 2:3], tiny[:, 1:2]).then_inc(sem("topk_step"), 1)
            v.wait_ge(sem("topk_step"), step())
            v.sem_inc(sem("waits_passed"), 1)
            V.tensor_scalar(gate, expo, tiny[:, 2:3], None, ALU.mult).then_inc(sem("topk_step"), 1)
            v.wait_ge(sem("topk_step"), step())
            v.sem_inc(sem("waits_passed"), 1)

        def softmax_exp(act, topk_n):
            act.wait_ge(sem("best_found"), topk_n + 1)
            ins = nc.scalar.activation(expo, best, ACT.Exp, bias=tiny[:, 0:1], accum_out=tiny[:, 1:2])
            ins.then_inc(sem("exp_done"), 1)

        def peer_vector(v, n):
            V = nc.vector
            base = n * UNITS
            x = xn if n == 0 else h

            def dots_of(t, tile, lo, hi):
                for kx in range(lo, hi):
                    s = kx % RING
                    v.wait_ge(sem(f"u_landed_{s}"), (t + base) * 32 + 16 * (kx // RING + 1))
                    V.tensor_tensor_reduce(out=ring_u[:, s, :], in0=ring_u[:, s, :], in1=x[:, tile, :], scale=1.0,
                                           scalar=0.0, op0=ALU.mult, op1=ALU.add,
                                           accum_out=dots[:, kx:kx + 1]).then_inc(sem("u_free"), 1)

            def coefficients(t):
                v.wait_ge(sem("gelu_done"), t + (base + 1))
                if type(t) is not int or t + n:
                    v.wait_ge(sem("diag_ready"), (t + base) * PK)
                V.tensor_tensor(coef, actv, gate, ALU.mult).then_inc(sem("coef_ready"), 1)
                v.wait_ge(sem("coef_ready"), t + (base + 1))

            def add_sum(t, tile):
                v.wait_ge(sem("v_free"), (t + base) * PK + 2 * PK)
                for half, bank in enumerate((acc_lo, acc_hi)):
                    y = ysum[:, tile * D + half * 512:tile * D + half * 512 + 512]
                    if type(t) is not int or t + n:
                        v.wait_ge(sem("y_added"), (t + base) * 2 + (half + 1))
                    V.tensor_tensor(y, y, bank[:, :], ALU.add).then_inc(sem("y_added"), 1)

            def unit_step(t, x_tile, y_tile):
                step = Steps((t + (base + 1)) * TOPK_STEPS)
                topk_find(v, step, n, t + 1)
                first = type(t) is int and t == 0
                if not first:
                    dots_of(t, x_tile, 0, PK // 2)
                topk_numbers(v, step, n, t + 1)
                dots_of(t, x_tile, 0 if first else PK // 2, PK)
                coefficients(t)
                topk_gate(v, step, n, t + 1)
                if y_tile is not None:
                    add_sum(t - 1, y_tile)

            if n == 0:
                V.memset(tiny[:, 3:4], 0.0).then_inc(sem("u_free"), RING)
                V.memset(small[:, 6:7], 0.0).then_inc(sem("y_added"), 2)
            V.memset(scores[:, UNITS * 2 * NKEYS:], 0.0).then_inc(sem("pad_zero"), 1)
            V.memset(ysum[:, :], 0.0).then_inc(sem("y_zero"), 1)
            v.wait_ge(sem("y_zero"), n + 1)
            step = Steps(base * TOPK_STEPS)
            topk_find(v, step, n, 0)
            topk_numbers(v, step, n, 0)
            topk_gate(v, step, n, 0)
            assert step.n == TOPK_STEPS, step.n
            unit_step(0, 0, None)
            with v.Fori(1, PH) as t:
                unit_step(t, 0, 0)
            unit_step(PH, 1, 0)
            with v.Fori(PH + 1, UNITS - 1) as t:
                unit_step(t, 1, 1)
            v.wait_ge(sem("y_added"), 2 * (base + UNITS - 2) + 2)
            experts_vector(v, 2 * n + 1, 0)
            dots_of(UNITS - 1, 1, 0, PK)
            coefficients(UNITS - 1)
            add_sum(UNITS - 2, 1)
            add_sum(UNITS - 1, 1)
            v.wait_ge(sem("y_added"), 2 * UNITS * (n + 1) + 2)

        def peer_scalar(act, n):
            base = n * UNITS

            def coefficients(t):
                act.wait_ge(sem("u_free"), (t + base) * PK + (PK + RING))
                nc.scalar.activation(actv, dots, ACT.Gelu).then_inc(sem("gelu_done"), 1)
                act.wait_ge(sem("coef_ready"), t + (base + 1))
                for kx in range(PK):
                    act.wait_ge(sem("v_free"), (t + base) * PK + (kx + 1))
                    ins = nc.scalar.activation(diag[:, kx, :], ident, ACT.Copy, scale=coef[:, kx:kx + 1])
                    ins.then_inc(sem("diag_ready"), 1)

            for lo, hi in ((0, PH + 1), (PH + 1, UNITS - 1)):
                with act.Fori(lo, hi) as t:
                    softmax_exp(act, t + (base + 1))
                    copy_scores(act, n, t + 2)
                    coefficients(t)
                if lo == 0 and n < 2:
                    mem_kv_scalar(act, n)
            experts_scalar(act, 2 * n + 1, 0)
            coefficients(UNITS - 1)
            if n < 2:
                fm_scalar(act, 2 * n + 1, 0)

        def peer_tensor(pe, n):
            base = n * UNITS

            def weighted_sum(t):
                pe.wait_ge(sem("y_added"), (t + base) * 2 + 2)
                for kx in range(PK):
                    s = kx % RING
                    pe.wait_ge(sem("diag_ready"), (t + base) * PK + (kx + 1))
                    pe.wait_ge(sem(f"v_landed_{s}"), (t + base) * 32 + 16 * (kx // RING + 1))
                    nc.tensor.matmul(acc_lo[:, :], diag[:, kx, :], ring_v[:, s, 0:512], start=kx == 0,
                                     stop=kx == PK - 1)
                    nc.tensor.matmul(acc_hi[:, :], diag[:, kx, :], ring_v[:, s, 512:1024], start=kx == 0,
                                     stop=kx == PK - 1).then_inc(sem("v_free"), 1)

            with pe.Fori(0, PH) as t:
                weighted_sum(t)
            if n < 2:
                mem_kv_tensor(pe, n)
            with pe.Fori(PH, UNITS - 1) as t:
                weighted_sum(t)
            if n < 2:
                fm_tensor(pe, 2 * n + 1, 0, h)
            weighted_sum(UNITS - 1)

        def peer_gpsimd(pool, n):
            base = n * UNITS

            def take_numbers(t, at):
                pool.wait_ge(sem("topk_done"), t + (base + 1))
                pool.sem_inc(sem("waits_passed"), 1)
                nc.gpsimd.tensor_copy(idx[:, at, :], idx_next[:, :]).then_inc(sem("idx_taken"), 1)
                pool.wait_ge(sem("idx_taken"), t + (base + 1))
                pool.sem_inc(sem("waits_passed"), 1)

            def gather(name, t, at, kx):
                table, ring = (io[f"u{n}"], ring_u) if name == "u" else (io[f"v{n}"], ring_v)
                s = kx % RING
                pool.wait_ge(sem(f"{name}_free"), (t + base) * PK + (kx + 1 + (PK - RING if name == "v" else 0)))
                pool.sem_inc(sem("waits_passed"), 1)
                nc.gpsimd.indirect_dma_start(out=ring[:, s, :], out_offset=None, in_=table,
                                             in_offset=bass.IndirectOffsetOnAxis(ap=idx[:, at, kx:kx + 1], axis=0)
                                             ).then_inc(sem(f"{name}_landed_{s}"), 16)

            if n == 0:
                nc.gpsimd.memset(idx[:, 1, :], 0).then_inc(sem("v_free"), PK)
            take_numbers(0, 0)
            for kx in range(PK):
                gather("u", 0, 0, kx)
            with pool.Fori(0, (UNITS - 1) // 3) as three:
                for at in range(3):
                    t = three * 3 + at
                    take_numbers(t + 1, (at + 1) % 3)
                    for kx in range(PK):
                        gather("u", t + 1, (at + 1) % 3, kx)
                        gather("v", t, at, kx)
            for kx in range(PK):
                gather("v", UNITS - 1, (UNITS - 1) % 3, kx)

        def load_row(sp, slot, which):
            sp.dma_start(rows[:, slot, :], io["rows"][which].partition_broadcast(P)).then_inc(sem(f"rows_in_{slot}"), 16)

        MEM_AT = ARENA - KC * 256 - 2 * 2 * 256
        M = Arena(arena_t, ARENA)
        M.at = MEM_AT
        memT = M.take(KC, 256)
        kmT = M.take(2, 256)
        vm = M.take(2, 256)
        assert G.at <= MEM_AT, (G.at, MEM_AT)
        T2 = Arena(arena_t, 29952)
        cat = T2.take(KC, TOK)
        qf, kf = T2.take(6, TOK), T2.take(6, TOK)
        qm = T2.take(2, TOK)
        vt = T2.take(NT, 768)
        probs = T2.take(NT * MEM_H, 256)
        probsT = T2.take(NT * MEM_H * 2, P)
        two_at = T2.at
        rf = T2.take(6, TOK)
        glr = T2.take(TOK)
        gate2 = T2.take(384)
        lg, bsum, eb, enb, ke, tmp2 = (T2.take(12, CH) for _ in range(6))
        keT = T2.take(NT, 384)
        attn = T2.take(NT * 2, 3, P)
        states = T2.take(4, 3, P)
        rs = T2.take(6, TOK)
        T3 = Arena(arena_t, 29952)
        T3.at = two_at
        zb, lb, sp_ = (T3.take(4, 3 * P) for _ in range(3))
        att = T3.take(12, 3 * P)
        mask3 = T3.take(3 * P)

        def mem_kv_tensor(pe, n):
            pe.wait_ge(sem("memT_in"), 16)
            for j in range(2):
                fm_tile(pe, ("mk", n, j), ("mem_k", n, j), memT, 256)
            outs = []
            for i in range(2):
                pe.wait_ge(*banks.take(("mv", n, i)))
                outs.append(banks.bank(("mv", n, i)))
            for j in range(2):
                pe.wait_ge(*landed(("mem_v", n, j)))
                w = slot(("mem_v", n, j))
                for i in range(2):
                    for x in range(4):
                        kc = 4 * j + x
                        ins = nc.tensor.matmul(outs[i][:, 0:256], memT[:, kc, i * P:(i + 1) * P],
                                               w[:, x * 256:(x + 1) * 256], start=kc == 0, stop=kc == KC - 1)
                    if j == 1:
                        ins.then_inc(banks.full_sem(("mv", n, i)), 1)
                if j == 0:
                    ins.then_inc(sem("blocks_used"), 1)
                    last_use_here()
                else:
                    last_use(("mv", n, 1))

        def mem_kv_scalar(act, n):
            for name, to in (("mk", kmT), ("mv", vm)):
                for j in range(2):
                    act.wait_ge(*banks.full((name, n, j)))
                    out = banks.bank((name, n, j))
                    ins = nc.scalar.activation(to[:, j, :], out[:, 0:256], ACT.Copy)
                    ins.then_inc(banks.emptied_sem((name, n, j)), 1)

        def memory_tensor(pe, n):
            for j in range(2):
                pe.wait_ge(*banks.emptied(("mk", n, j)))
                pe.wait_ge(*banks.emptied(("qm", n, j)))
                pe.wait_ge(*banks.emptied(("mv", n, j)))
            for i in range(NT):
                for par in range(2):
                    r = slice(64 * par, 64 * par + 64)
                    pe.wait_ge(*banks.take(("ms", n, i, par)))
                    out = banks.bank(("ms", n, i, par))
                    for j in range(2):
                        ins = nc.tensor.matmul(out[:, j * 256:(j + 1) * 256], qm[r, j, i * P:(i + 1) * P], kmT[r, j, :],
                                               start=True, stop=True)
                    ins.then_inc(banks.full_sem(("ms", n, i, par)), 1)

        def memory_values_tensor(pe, n):
            pe.wait_ge(sem("probs_ready"), n + 1)
            for i in range(NT):
                for par in range(2):
                    pe.wait_ge(*banks.take(("pT", n, i, par)))
                    out = banks.bank(("pT", n, i, par))
                    for x in range(4):
                        p_at = probs[:, (i * 2 + par) * 2 + x // 2, (x % 2) * P:(x % 2 + 1) * P]
                        ins = nc.tensor.transpose(out[:, x * P:(x + 1) * P], p_at, ident)
                    ins.then_inc(banks.full_sem(("pT", n, i, par)), 1)
            for i in range(NT):
                for par in range(2):
                    pe.wait_ge(*banks.emptied(("pT", n, i, par)))
            for i in range(NT):
                pe.wait_ge(*banks.take(("mo", n, i)))
                out = banks.bank(("mo", n, i))
                for par in range(2):
                    for j in range(2):
                        m = 2 * j + par
                        for mt in range(2):
                            ins = nc.tensor.matmul(out[64 * par:64 * par + 64, j * P:(j + 1) * P],
                                                   vm[:, mt, m * 64:(m + 1) * 64],
                                                   probsT[:, ((i * 2 + par) * 2 + j) * 2 + mt, :],
                                                   start=mt == 0, stop=mt == 1)
                ins.then_inc(banks.full_sem(("mo", n, i)), 1)

        def memory_max_vector(v, n):
            for i in range(NT):
                for par in range(2):
                    v.wait_ge(*banks.full(("ms", n, i, par)))
                    out = banks.bank(("ms", n, i, par))
                    at = 16 + 2 * (2 * i + par)
                    nc.vector.tensor_reduce(small[:, at:at + 2], out[:, :].rearrange("p (a b) -> p a b", a=2),
                                            AX.X, ALU.max).then_inc(sem("dve_step"), 1)
                    v.wait_ge(sem("dve_step"), count("dve_step"))
                    ins = nc.vector.tensor_scalar(small[:, at:at + 2], small[:, at:at + 2], -0.125, None, ALU.mult)
                    ins.then_inc(sem("mem_max"), 1)

        def memory_norm_vector(v, n):
            v.wait_ge(sem("mem_exp"), 8 * (n + 1))
            nc.vector.reciprocal(small[:, 24:32], small[:, 24:32]).then_inc(sem("dve_step"), 1)
            v.wait_ge(sem("dve_step"), count("dve_step"))
            ins = nc.vector.tensor_tensor(probs[:, :, :], probs[:, :, :], bc(small[:, 24:32], (1, 8), (0, 256)), ALU.mult)
            ins.then_inc(sem("probs_ready"), 1)

        def memory_exp_scalar(act, n):
            for i in range(NT):
                for par in range(2):
                    act.wait_ge(sem("mem_max"), 4 * n + 2 * i + par + 1)
                    act.wait_ge(*banks.full(("ms", n, i, par)))
                    out = banks.bank(("ms", n, i, par))
                    for j in range(2):
                        at = 2 * (2 * i + par) + j
                        ins = nc.scalar.activation(probs[:, at, :], out[:, j * 256:(j + 1) * 256], ACT.Exp, scale=0.125,
                                                   bias=small[:, 16 + at:17 + at], accum_out=small[:, 24 + at:25 + at])
                        if j == 0:
                            ins.then_inc(sem("mem_exp"), 1)
                    ins.then_inc(banks.emptied_sem(("ms", n, i, par)), 1)
            for i in range(NT):
                for par in range(2):
                    act.wait_ge(*banks.emptied(("ms", n, i, par)))
            nc.scalar.activation(small[:, 6:8], small[:, 6:8], ACT.Copy).then_inc(sem("mem_exp"), 4)

        def memory_out_scalar(act, n):
            for i in range(NT):
                for par in range(2):
                    act.wait_ge(*banks.full(("pT", n, i, par)))
                    out = banks.bank(("pT", n, i, par))
                    at = (i * 2 + par) * 4
                    nc.scalar.activation(probsT[:, at:at + 4, :], out[:, :].rearrange(
         "p (a b) -> p a b", a=4), ACT.Copy).then_inc(banks.emptied_sem(("pT", n, i, par)), 1)
            for i in range(NT):
                act.wait_ge(*banks.full(("mo", n, i)))
                out = banks.bank(("mo", n, i))
                nc.scalar.activation(cat[:, 6:8, i * P:(i + 1) * P], out[:, 0:256].rearrange(
     "p (a b) -> p a b", a=2), ACT.Copy).then_inc(banks.emptied_sem(("mo", n, i)), 1)

        def two_tensor(pe):
            pe.wait_ge(*landed("glr"))
            w = slot("glr")
            pe.wait_ge(*banks.take("glr"))
            out = banks.bank("glr")
            for kc in range(KC):
                ins = nc.tensor.matmul(out[0:16, 0:TOK], w[:, kc * 16:(kc + 1) * 16], xT[:, kc, 0:TOK],
                                       start=kc == 0, stop=kc == KC - 1)
            ins.then_inc(banks.full_sem("glr"), 1)
            last_use("glr")
            x = xT[:, :, 0:TOK]
            fm_tile(pe, ("q2", 0), ("a_q", 0), x, TOK)
            pe.wait_ge(*banks.emptied("glr"))
            pe.wait_ge(sem("gate2_in"), 16)
            for j in range(3):
                pe.wait_ge(*banks.take(("lg", j)))
                out = banks.bank(("lg", j))
                nc.tensor.matmul(out[:, 0:TOK], gate2[0:16, j * P:(j + 1) * P], glr[0:16, :],
                                 start=True, stop=True).then_inc(banks.full_sem(("lg", j)), 1)
            fm_tile(pe, ("k2", 0), ("a_k", 0), x, TOK)
            for j in range(1, 3):
                fm_tile(pe, ("q2", j), ("a_q", j), x, TOK)
                fm_tile(pe, ("k2", j), ("a_k", j), x, TOK)
            tm_out(pe, "a_v", [xT[:, kc, 0:TOK] for kc in range(KC)], 768)
            for j in range(2):
                fm_tile(pe, ("qm", 0, j), ("a_qm", j), x, TOK)
            memory_tensor(pe, 0)
            for j in range(6):
                fm_tile(pe, ("r2", j), ("a_r", j), x, TOK)
            pe.wait_ge(sem("ke_ready"), 1)
            for i in range(NT):
                pe.wait_ge(*banks.take(("keT", i)))
                out = banks.bank(("keT", i))
                for j in range(3):
                    ins = nc.tensor.transpose(out[:, j * P:(j + 1) * P],
                                              ke[:, 4 * j + 2 * i:4 * j + 2 * i + 2, :].rearrange("p a b -> p (a b)"), ident)
                ins.then_inc(banks.full_sem(("keT", i)), 1)
            for i in range(NT):
                for par in range(2):
                    r = slice(64 * par, 64 * par + 64)
                    pe.wait_ge(*banks.take(("attn", i, par)))
                    out = banks.bank(("attn", i, par))
                    for j in range(3):
                        ins = nc.tensor.matmul(out[:, j * P:(j + 1) * P], kf[r, j, i * P:(i + 1) * P],
                                               qf[r, j, i * P:(i + 1) * P], start=True, stop=True)
                    ins.then_inc(banks.full_sem(("attn", i, par)), 1)
            for i in range(NT):
                pe.wait_ge(*banks.emptied(("keT", i)))
                for half in range(2):
                    pe.wait_ge(*banks.emptied(("a_v", i, half)))
            for c in range(3):
                r = slice(64 * (c % 2), 64 * (c % 2) + 64)
                pe.wait_ge(*banks.take(("du", c), 3))
                out = banks.bank(("du", c))
                for par in range(2):
                    for j in range(3):
                        hd = 2 * j + par
                        ins = nc.tensor.matmul(out[64 * par:64 * par + 64, j * P:(j + 1) * P],
                                               keT[r, c // 2, hd * 64:(hd + 1) * 64], vt[r, c // 2, hd * P:(hd + 1) * P],
                                               start=True, stop=True)
                ins.then_inc(banks.full_sem(("du", c)), 1)
            memory_values_tensor(pe, 0)
            for c in range(3):
                pe.wait_ge(*banks.emptied(("du", c)))
            for i in range(NT):
                for par in range(2):
                    r = slice(64 * par, 64 * par + 64)
                    pe.wait_ge(*banks.emptied(("attn", i, par)))
                    pe.wait_ge(*banks.take(("o2", i, par)))
                    out = banks.bank(("o2", i, par))
                    for j in range(3):
                        hd = 2 * j + par
                        ins = nc.tensor.matmul(out[:, j * P:(j + 1) * P], vt[:, i, hd * P:(hd + 1) * P],
                                               attn[:, 2 * i + par, j, :], start=True, stop=True)
                        for c in range(2):
                            if 2 * i + c:
                                at = i * P + c * CH
                                ins = nc.tensor.matmul(out[:, j * P + c * CH:j * P + (c + 1) * CH],
                                                       states[r, 2 * i + c, j, :], qf[r, j, at:at + CH],
                                                       start=False, stop=True, skip_group_check=True)
                    ins.then_inc(banks.full_sem(("o2", i, par)), 1)
            pe.wait_ge(sem("o_squares"), 1)
            for x_ in range(3):
                pe.wait_ge(*banks.take(("os", x_)))
                out = banks.bank(("os", x_))
                nc.tensor.matmul(out[:, :], ones, rs[:, 2 * x_:2 * x_ + 2, :].rearrange("p a b -> p (a b)"),
                                 start=True, stop=True).then_inc(banks.full_sem(("os", x_)), 1)
            ready = {6: [banks.emptied(("mo", 0, i)) for i in range(NT)]}
            ready.update({2 * x_: [(sem("o_gated"), x_ + 1)] for x_ in range(3)})
            tm_out(pe, "a_out", [cat[:, kc, :] for kc in range(KC)], order=OUT_ORDER, ready=ready)

        def two_scalar(act):
            act.wait_ge(*banks.full("glr"))
            out = banks.bank("glr")
            nc.scalar.activation(glr[0:16, :], out[0:16, 0:TOK], ACT.Copy).then_inc(banks.emptied_sem("glr"), 1)

            def plain(name, to, scale=1.0):
                act.wait_ge(*banks.full(name))
                out = banks.bank(name)
                nc.scalar.activation(to, out[:, 0:TOK], ACT.Copy, scale=scale).then_inc(banks.emptied_sem(name), 1)

            plain(("q2", 0), qf[:, 0, :], 0.125)
            plain(("k2", 0), kf[:, 0, :])
            for j in range(1, 3):
                plain(("q2", j), qf[:, j, :], 0.125)
                plain(("k2", j), kf[:, j, :])
            act.wait_ge(sem("gate_abs"), 1)
            nc.scalar.activation(eb[:, :, :], eb[:, :, :], ACT.Exp).then_inc(sem("gate_exp"), 1)
            act.wait_ge(sem("gate_exp"), 1)
            nc.scalar.activation(eb[:, :, :], eb[:, :, :], ACT.Ln, bias=ones[:, 0:1]).then_inc(sem("gate_ln"), 1)
            for i in range(NT):
                for half, w in ((0, 512), (1, 256)):
                    act.wait_ge(*banks.full(("a_v", i, half)))
                    out = banks.bank(("a_v", i, half))
                    ins = nc.scalar.activation(vt[:, i, half * 512:half * 512 + w], out[:, 0:w], ACT.Copy)
                    ins.then_inc(banks.emptied_sem(("a_v", i, half)), 1)
            act.wait_ge(sem("gate_sums"), 1)
            nc.scalar.activation(eb[:, :, :], bsum[:, :, :], ACT.Exp, scale=1.0 / 16).then_inc(sem("gla_decays"), 1)
            nc.scalar.activation(enb[:, :, :], bsum[:, :, :], ACT.Exp, scale=-1.0 / 16).then_inc(sem("gla_decays"), 1)
            act.wait_ge(sem("to_end"), 1)
            nc.scalar.activation(ke[:, :, :], ke[:, :, :], ACT.Exp, scale=1.0 / 16).then_inc(sem("gla_decays"), 1)
            ins = nc.scalar.activation(small[:, 32:44], bsum[:, :, CH - 1], ACT.Exp, scale=1.0 / 16)
            ins.then_inc(sem("gla_decays"), 1)
            for j in range(2):
                plain(("qm", 0, j), qm[:, j, :])
            memory_exp_scalar(act, 0)
            for j in range(6):
                act.wait_ge(*banks.full(("r2", j)))
                out = banks.bank(("r2", j))
                nc.scalar.activation(rf[:, j, :], out[:, 0:TOK], ACT.Silu).then_inc(banks.emptied_sem(("r2", j)), 1)
            for i in range(NT):
                act.wait_ge(*banks.full(("keT", i)))
                out = banks.bank(("keT", i))
                nc.scalar.activation(keT[:, i, :], out[:, 0:384], ACT.Copy).then_inc(banks.emptied_sem(("keT", i)), 1)
            memory_out_scalar(act, 0)
            for i in range(NT):
                for par in range(2):
                    act.wait_ge(*banks.full(("o2", i, par)))
                    out = banks.bank(("o2", i, par))
                    to = cat[:, 0:6, i * P:(i + 1) * P].rearrange("p (j two) t -> p j two t", two=2)[:, :, par, :]
                    ins = nc.scalar.activation(to, out[:, 0:384].rearrange("p (a b) -> p a b", a=3), ACT.Copy)
                    ins.then_inc(banks.emptied_sem(("o2", i, par)), 1)
            for i in range(NT):
                for par in range(2):
                    act.wait_ge(*banks.emptied(("o2", i, par)))
            nc.scalar.activation(rs[:, :, :], cat[:, 0:6, :], ACT.Square).then_inc(sem("o_squares"), 1)
            act.wait_ge(sem("o_rstd"), 1)
            nc.scalar.activation(rs[:, :, :], rs[:, :, :], ACT.Sqrt).then_inc(sem("o_rstd"), 1)

        def two_vector(v):
            V = nc.vector

            V.memset(attn.rearrange("p a b c -> p (a b c)"), 0.0).then_inc(sem("dve_step"), 1)
            v.wait_ge(sem("dve_step"), count("dve_step"))
            lgj, tj, ebj = (x.rearrange("p (j c) t -> p j (c t)", j=3) for x in (lg, tmp2, eb))
            bj = bsum.rearrange("p (j c) t -> p j (c t)", j=3)
            for j in range(3):
                v.wait_ge(*banks.full(("lg", j)))
                out = banks.bank(("lg", j))
                ins = V.tensor_scalar(lgj[:, j, :], out[:, 0:TOK], col("b_gate", j), None, ALU.add)
                ins.then_inc(banks.emptied_sem(("lg", j)), 1)
            for j in range(3):
                v.wait_ge(*banks.emptied(("lg", j)))
            V.tensor_scalar(tmp2[:, :, :], lg[:, :, :], 0.0, None, ALU.min).then_inc(sem("dve_step"), 1)
            v.wait_ge(sem("dve_step"), count("dve_step"))
            ins = V.scalar_tensor_tensor(eb[:, :, :], lg[:, :, :], -1.0, lg[:, :, :], ALU.mult, ALU.min)
            ins.then_inc(sem("gate_abs"), 1)
            v.wait_ge(sem("gate_ln"), 1)
            V.tensor_tensor(lg[:, :, :], tmp2[:, :, :], eb[:, :, :], ALU.subtract).then_inc(sem("dve_step"), 1)
            v.wait_ge(sem("dve_step"), count("dve_step"))
            for j in range(3):
                ins = V.tensor_tensor_scan(bj[:, j, :], k("scan"), lgj[:, j, :], 0.0, ALU.mult, ALU.add)
            ins.then_inc(sem("gate_sums"), 1)
            v.wait_ge(sem("gate_sums"), 1)
            ins = V.tensor_tensor(ke[:, :, :], bc(bsum[:, :, CH - 1:CH], (CH, 12), (0, CH)), bsum[:, :, :], ALU.subtract)
            ins.then_inc(sem("to_end"), 1)
            for j in range(3):
                v.wait_ge(*banks.emptied(("q2", j)))
                v.wait_ge(*banks.emptied(("k2", j)))
            v.wait_ge(sem("gla_decays"), 4)
            kv = kf[:, 0:3, :].rearrange("p j t -> p (j t)")
            qv = qf[:, 0:3, :].rearrange("p j t -> p (j t)")
            flat = lambda x: x.rearrange("p a b -> p (a b)")
            V.tensor_tensor(flat(ke), flat(ke), kv, ALU.mult).then_inc(sem("dve_step"), 1)
            v.wait_ge(sem("dve_step"), count("dve_step"))
            V.tensor_tensor(qv, qv, flat(eb), ALU.mult).then_inc(sem("dve_step"), 1)
            v.wait_ge(sem("dve_step"), count("dve_step"))
            V.tensor_tensor(kv, kv, flat(enb), ALU.mult).then_inc(sem("ke_ready"), 1)
            memory_max_vector(v, 0)
            memory_norm_vector(v, 0)
            for i in range(NT):
                for par in range(2):
                    v.wait_ge(*banks.full(("attn", i, par)))
                    out = banks.bank(("attn", i, par))
                    ins = V.copy_predicated(attn[:, 2 * i + par, :, :], bc(k("incl"), (0, 3), (1, P)).bitcast(U32),
                                            out[:, 0:384].rearrange("p (a b) -> p a b", a=3))
                    ins.then_inc(banks.emptied_sem(("attn", i, par)), 1)
            for c in range(3):
                v.wait_ge(*banks.full(("du", c)))
                out = banks.bank(("du", c))
                if c:
                    v.wait_ge(*banks.emptied(("du", c - 1)))
                for j in range(3):
                    f = slice(j * P, (j + 1) * P)
                    if c == 0:
                        ins = V.tensor_copy(states[:, 1, j, :], out[:, f])
                    else:
                        ins = V.scalar_tensor_tensor(states[:, c + 1, j, :], states[:, c, j, :],
                                                     small[:, 32 + 4 * j + c:33 + 4 * j + c], out[:, f], ALU.mult, ALU.add)
                    ins.then_inc(banks.emptied_sem(("du", c)), 1)
            v.wait_ge(sem("o_squares"), 1)
            for hd in range(6):
                v.wait_ge(*banks.emptied(("r2", hd)))
                ins = V.scalar_tensor_tensor(rf[:, hd, :], cat[:, hd, :], col("head_g", hd), rf[:, hd, :], ALU.mult,
                                             ALU.mult)
            ins.then_inc(sem("dve_step"), 1)
            v.wait_ge(sem("dve_step"), count("dve_step"))
            for x_ in range(3):
                v.wait_ge(*banks.full(("os", x_)))
                out = banks.bank(("os", x_))
                V.tensor_scalar(rs[:, 2 * x_:2 * x_ + 2, :], out[:, :].rearrange("p (a b) -> p a b", a=2),
                                1.0 / GLA_DV, 1e-5, ALU.mult, ALU.add).then_inc(banks.emptied_sem(("os", x_)), 1)
            for x_ in range(3):
                v.wait_ge(*banks.emptied(("os", x_)))
            V.reciprocal(rs[:, :, :], rs[:, :, :]).then_inc(sem("o_rstd"), 1)
            v.wait_ge(sem("o_rstd"), 2)
            for hd in range(0, 6, 2):
                V.tensor_tensor(cat[:, hd:hd + 2, :], rf[:, hd:hd + 2, :], rs[:, hd:hd + 2, :],
                                ALU.mult).then_inc(sem("o_gated"), 1)
            mixed_vector(v, "a_out", 2, ALPHA)

        def three_tensor(pe):
            x = xT[:, :, 0:TOK]
            for q in range(3):
                for j in (2 * q, 2 * q + 1):
                    fm_tile(pe, ("q3", j), ("b_q", j), x, TOK)
                    fm_tile(pe, ("k3", j), ("b_k", j), x, TOK)
                if q:
                    sb_above_tensor(pe, q - 1)
                sb_scores_tensor(pe, q)
            for j in range(2):
                fm_tile(pe, ("qm", 1, j), ("b_qm", j), x, TOK)
            sb_above_tensor(pe, 2)
            memory_tensor(pe, 1)
            tm_out(pe, "b_v", [xT[:, kc, 0:TOK] for kc in range(KC)], 768)
            memory_values_tensor(pe, 1)
            for i in range(NT):
                for half in range(2):
                    pe.wait_ge(*banks.emptied(("b_v", i, half)))
            for q in range(3):
                pe.wait_ge(sem("att_ready"), q + 1)
                pe.wait_ge(*banks.take(("o3", q)))
                out = banks.bank(("o3", q))
                for x_ in range(4):
                    hd = 4 * q + x_
                    o = slice(64 * (hd % 2), 64 * (hd % 2) + 64)
                    at = (x_ // 2) * TOK
                    hs = slice(hd * 64, (hd + 1) * 64)
                    nc.tensor.matmul(out[o, at:at + TOK], vt[:, 0, hs], att[:, hd, 0:TOK], start=True, stop=True)
                    ins = nc.tensor.matmul(out[o, at + P:at + TOK], vt[:, 1, hs], att[:, hd, TOK:3 * P],
                                           start=False, stop=True, skip_group_check=True)
                ins.then_inc(banks.full_sem(("o3", q)), 1)
            ready = {6: [banks.emptied(("mo", 1, i)) for i in range(NT)]}
            ready.update({2 * q: [banks.emptied(("o3", q))] for q in range(3)})
            tm_out(pe, "b_out", [cat[:, kc, :] for kc in range(KC)], order=OUT_ORDER, ready=ready)

        def sb_scores_tensor(pe, q):
            for j in (2 * q, 2 * q + 1):
                pe.wait_ge(*banks.emptied(("q3", j)))
                pe.wait_ge(*banks.emptied(("k3", j)))
            for x_ in range(4):
                hd = 4 * q + x_
                j, r = hd // 2, slice(64 * (hd % 2), 64 * (hd % 2) + 64)
                pe.wait_ge(*banks.take(("sb", hd)))
                out = banks.bank(("sb", hd))
                nc.tensor.matmul(out[:, 0:TOK], kf[r, j, 0:P], qf[r, j, :], start=True, stop=True)
                ins = nc.tensor.matmul(out[:, TOK:3 * P], kf[r, j, P:TOK], qf[r, j, P:TOK], start=True, stop=True)
                ins.then_inc(banks.full_sem(("sb", hd)), 1)

        def sb_above_tensor(pe, q):
            pe.wait_ge(sem("softplus_ready"), q + 1)
            for x_ in range(4):
                hd = 4 * q + x_
                pe.wait_ge(*banks.take(("above", hd)))
                out = banks.bank(("above", hd))
                nc.tensor.matmul(out[:, 0:TOK], k("below"), lb[:, x_, 0:TOK], start=True, stop=True)
                nc.tensor.matmul(out[:, P:TOK], ones, lb[:, x_, TOK:3 * P], start=False, stop=True, skip_group_check=True)
                ins = nc.tensor.matmul(out[:, TOK:3 * P], k("below"), lb[:, x_, TOK:3 * P], start=True, stop=True)
                ins.then_inc(banks.full_sem(("above", hd)), 1)

        def three_scalar(act):

            def plain(name, to, scale=1.0):
                act.wait_ge(*banks.full(name))
                out = banks.bank(name)
                nc.scalar.activation(to, out[:, 0:TOK], ACT.Copy, scale=scale).then_inc(banks.emptied_sem(name), 1)


            def att_exp(q):
                act.wait_ge(sem("log_a"), q + 1)
                nc.scalar.activation(att[:, 4 * q:4 * q + 4, :], sp_[:, :, :], ACT.Exp).then_inc(sem("att_exp"), 1)

            for q in range(3):
                for j in (2 * q, 2 * q + 1):
                    plain(("q3", j), qf[:, j, :], 0.125)
                    plain(("k3", j), kf[:, j, :])
                if q:
                    att_exp(q - 1)
                    act.wait_ge(sem("att_before"), q)
                for x_ in range(4):
                    act.wait_ge(*banks.full(("sb", 4 * q + x_)))
                    out = banks.bank(("sb", 4 * q + x_))
                    ins = nc.scalar.activation(zb[:, x_, :], out[:, 0:3 * P], ACT.Copy)
                    ins.then_inc(banks.emptied_sem(("sb", 4 * q + x_)), 1)
                act.wait_ge(sem("z_abs"), q + 1)
                nc.scalar.activation(lb[:, :, :], lb[:, :, :], ACT.Exp).then_inc(sem("sb_exp"), 1)
                act.wait_ge(sem("sb_exp"), q + 1)
                nc.scalar.activation(lb[:, :, :], lb[:, :, :], ACT.Ln, bias=ones[:, 0:1]).then_inc(sem("sb_ln"), 1)
            for j in range(2):
                plain(("qm", 1, j), qm[:, j, :])
            att_exp(2)
            memory_exp_scalar(act, 1)
            for i in range(NT):
                for half, w in ((0, 512), (1, 256)):
                    act.wait_ge(*banks.full(("b_v", i, half)))
                    out = banks.bank(("b_v", i, half))
                    ins = nc.scalar.activation(vt[:, i, half * 512:half * 512 + w], out[:, 0:w], ACT.Copy)
                    ins.then_inc(banks.emptied_sem(("b_v", i, half)), 1)
            memory_out_scalar(act, 1)
            for q in range(3):
                act.wait_ge(*banks.full(("o3", q)))
                out = banks.bank(("o3", q))
                nc.scalar.activation(cat[:, 2 * q:2 * q + 2, :], out[:, :].rearrange(
     "p (a b) -> p a b", a=2), ACT.Copy).then_inc(banks.emptied_sem(("o3", q)), 1)

        def three_vector(v):
            V = nc.vector

            V.tensor_copy(mask3[:, 0:P], k("sbmask"))
            V.memset(mask3[:, P:TOK], 1.0)
            V.tensor_copy(mask3[:, TOK:3 * P], k("sbmask")).then_inc(sem("dve_step"), 1)
            v.wait_ge(sem("dve_step"), count("dve_step"))
            m4 = bc(mask3, (0, 4), (1, 3 * P))
            for q in range(3):
                for x_ in range(4):
                    v.wait_ge(*banks.emptied(("sb", 4 * q + x_)))
                ins = V.scalar_tensor_tensor(lb[:, :, :], zb[:, :, :], -1.0, zb[:, :, :], ALU.mult, ALU.min)
                ins.then_inc(sem("z_abs"), 1)
                v.wait_ge(sem("sb_ln"), q + 1)
                ins = V.scalar_tensor_tensor(sp_[:, :, :], zb[:, :, :], 0.0, lb[:, :, :], ALU.max, ALU.add)
                ins.then_inc(sem("dve_step"), 1)
                v.wait_ge(sem("dve_step"), count("dve_step"))
                V.tensor_tensor(lb[:, :, :], sp_[:, :, :], m4, ALU.mult).then_inc(sem("softplus_ready"), 1)
                V.tensor_tensor(sp_[:, :, :], zb[:, :, :], sp_[:, :, :], ALU.subtract).then_inc(sem("dve_step"), 1)
                v.wait_ge(sem("dve_step"), count("dve_step"))
                for x_ in range(4):
                    v.wait_ge(*banks.full(("above", 4 * q + x_)))
                    out = banks.bank(("above", 4 * q + x_))
                    ins = V.tensor_tensor(sp_[:, x_, :], sp_[:, x_, :], out[:, 0:3 * P], ALU.subtract)
                    ins.then_inc(banks.emptied_sem(("above", 4 * q + x_)), 1)
                for x_ in range(4):
                    v.wait_ge(*banks.emptied(("above", 4 * q + x_)))
                V.tensor_scalar(sp_[:, :, :], sp_[:, :, :], 0.0, None, ALU.min).then_inc(sem("log_a"), 1)
                v.wait_ge(sem("att_exp"), q + 1)
                a = att[:, 4 * q:4 * q + 4, :]
                V.tensor_tensor(a, a, m4, ALU.mult).then_inc(sem("att_ready"), 1)
                if q < 2:
                    V.memset(small[:, 44:45], 0.0).then_inc(sem("att_before"), 1)
            memory_max_vector(v, 1)
            memory_norm_vector(v, 1)
            mixed_vector(v, "b_out", 4, ALPHA)

        blk = ctx.enter_context(nc.Block())

        @blk.tensor
        def _(pe):
            one_tensor(pe)
            for n, mixer in enumerate((two_tensor, three_tensor, None)):
                mixed_tensor(pe, 2 * n)
                peer_scores_tensor(pe, n)
                peer_tensor(pe, n)
                if mixer:
                    fm_tensor(pe, 2 * n + 1, 1, h)
                    fm_wait(pe, 2 * n + 1)
                    mixer(pe)

        @blk.vector
        def _(v):
            one_vector(v)
            for n, mixer in enumerate((two_vector, three_vector, None)):
                peer_vector(v, n)
                experts_vector(v, 2 * n + 1, 1)
                if mixer:
                    mixer(v)

        @blk.scalar
        def _(act):
            one_scalar(act)
            for n, mixer in enumerate((two_scalar, three_scalar, None)):
                mixed_scalar(act, ("w_o", "a_out", "b_out")[n], 2 * n)
                peer_scores_scalar(act, n)
                peer_scalar(act, n)
                experts_scalar(act, 2 * n + 1, 1)
                if mixer:
                    fm_scalar(act, 2 * n + 1, 1)
                    mixer(act)

        @blk.gpsimd
        def _(pool):
            one_gpsimd(pool)
            for n in range(3):
                peer_gpsimd(pool, n)

        @blk.sync
        def _(sp):
            first = {b[0]: n for n, b in reversed(list(enumerate(plan)))}
            one_sync(sp)
            at = first["w_q", 0, 0]
            load_blocks(sp, 0, at)
            sp.wait_ge(*banks.full(("rwkv_out", 0)))
            load_row(sp, 0, 1)
            banks_of_o = [banks.full(("oT", i)) for i in range(NT)]
            for wait in banks_of_o:
                sp.wait_ge(*wait)
            sp.dma_start(memT.rearrange("p a b -> p (a b)"), io["memT"]).then_inc(sem("memT_in"), 16)
            for norm, layer in ((2, 0), (4, 1)):
                load_blocks(sp, at, first[LAYER_START[layer]] + SLOTS)
                at = first[LAYER_START[layer]] + SLOTS
                sp.wait_ge(sem("normed"), NT * norm)
                if layer == 0:
                    sp.dma_start(gate2[0:16, :], io["a_gate2"]).then_inc(sem("gate2_in"), 16)
                load_row(sp, 1, 2 * norm - 2)
                load_row(sp, 0, 2 * norm - 1)
                load_blocks(sp, at, first["w_q", layer + 1, 0] + SLOTS)
                at = first["w_q", layer + 1, 0] + SLOTS
                sp.wait_ge(sem("normed"), NT * (norm + 1))
                load_row(sp, 1, 2 * norm)
                load_row(sp, 0, 2 * norm + 1)
            load_blocks(sp, at, len(plan))
            out = io["out"].rearrange("(i p) d -> i p d", p=P)
            for i in range(NT):
                sp.wait_ge(sem("normed"), NT * 5 + i + 1)
                sp.dma_start(out[i], h[:, i, :]).then_inc(sem("out_written"), 16)
            sp.wait_ge(sem("out_written"), 16 * NT)


def fm_blocks(w):
    n = w.shape[1] // P
    return np.ascontiguousarray(w.reshape(KC, P, n, P).transpose(2, 1, 0, 3).reshape(n, P, KC * P))


def half_fm_blocks(w):
    return np.ascontiguousarray(w.reshape(4, P, 4, 2, P).transpose(2, 1, 3, 0, 4).reshape(4, P, D))


def column(a):
    return a.reshape(-1, P).T


def lay_out(i):
    a = {}
    a["const"] = constants()
    a["x"] = i["x"][0]
    a["meta"] = i["meta_tokens"]
    a["w_in"] = fm_blocks(i["w_in"][0])
    a["lora"] = np.concatenate([np.concatenate([i["w_up"][0], i["a_up"][0]], 0), i["g_up"][0]], 1)
    a["cols"] = np.concatenate([column(i["g_mix"][0]), column(i["mu_shift"][0]), column(i["w0"][0]),
                                column(i["a0"][0]), column(i["k_k"][0]), column(i["k_a"][0]),
                                column(i["r_k"][0].reshape(-1)), column(i["conv_b"][0]), column(i["conv_ln_g"][0]),
                                column(i["conv_ln_b"][0]),
                                i["conv_w"][0].reshape(TAPS, CT, P).transpose(2, 0, 1).reshape(P, -1),
                                column(i["a_b_gate_2"][0]), column(i["a_head_g_2"][0].reshape(-1))], 1)
    a["w_conv_out"] = half_fm_blocks(i["w_conv_out"][0])
    a["w_rwkv_out"] = half_fm_blocks(i["w_rwkv_out"][0])
    a["w_o"] = i["w_o"][0].reshape(KC, P, D)
    a["gn_rows"] = np.concatenate([i["gn_g"][0], i["gn_b"][0]])
    w_q = np.concatenate([i["w_q"], i["peer_w_q_2"]])
    a["w_q"] = np.stack([fm_blocks(w) for w in w_q])
    keys = np.concatenate([i["sub_keys"], i["peer_subkeys_2"]])
    a["keys"] = keys.reshape(3, 2 * PH, P, P).transpose(0, 3, 1, 2).reshape(3, P, 2 * PH * P)
    kv = np.concatenate([i["a_w_mem_kv_2"], i["b_w_mem_kv_2"]])
    a["mem_k"] = np.stack([fm_blocks(w[:, :256]) for w in kv])
    a["mem_v"] = kv[:, :, 256:].reshape(2, 2, 4, P, 256).transpose(0, 1, 3, 2, 4).reshape(2, 2, P, D)
    a["memT"] = i["mem_2"][0].T.reshape(KC, P, 256).transpose(1, 0, 2).reshape(P, KC * 256)
    w = i["a_w_in_2"][0]
    a["a_fm"] = fm_blocks(np.concatenate([w[:, :768], w[:, 1536:2304], w[:, 2320:]], 1))
    a["a_glr"] = w[:, 2304:2320].reshape(KC, P, 16).transpose(1, 0, 2).reshape(P, P)
    a["a_v"] = w[:, 768:1536].reshape(KC, P, 768)
    a["a_gate2"] = i["a_w_gate2_2"][0]
    a["a_out"] = i["a_w_out_2"][0].reshape(KC, P, D)
    a["b_fm"] = fm_blocks(i["b_w_in_2"][0])
    a["sb_k"] = fm_blocks(i["sb_w_kv_2"][:, :768])
    a["sb_v"] = i["sb_w_kv_2"][:, 768:].reshape(KC, P, 768)
    a["b_out"] = i["b_w_out_2"][0].reshape(KC, P, D)
    a["rows"] = np.stack([i["g_ffn"][0], i["g_final"], i["ln_g_2"][0, 0], i["ln_b_2"][0, 0], i["ln_g_2"][0, 1],
                          i["ln_b_2"][0, 1], i["ln_g_2"][1, 0], i["ln_b_2"][1, 0], i["ln_g_2"][1, 1], i["ln_b_2"][1, 1]])
    a["u0"], a["v0"] = i["expert_u"][0], i["expert_v"][0]
    for n in range(2):
        a[f"u{n + 1}"], a[f"v{n + 1}"] = i["peer_u_2"][n], i["peer_v_2"][n]
    return {name: np.ascontiguousarray(v) for name, v in a.items()}


def kernel(**inputs):
    import concourse.bacc as bacc
    from concourse.bass_utils import run_bass_kernel_spmd

    arrays = lay_out({name: np.asarray(v) for name, v in inputs.items()})
    nc = bacc.Bacc("TRN2", target_bir_lowering=False, num_devices=1)
    io = {name: nc.dram_tensor(f"in_{name}", v.shape, F32, kind="ExternalInput").ap() for name, v in arrays.items()}
    io["out"] = nc.dram_tensor("out", (TOK, D), F32, kind="ExternalOutput").ap()
    build(nc, io)
    r = run_bass_kernel_spmd(nc, [{f"in_{name}": v for name, v in arrays.items()}], core_ids=[0])
    return r.results[0]["out"].reshape(1, TOK, D)
```
